# Optimizing a Trainium2 kernel written in Bass

```python
import jax, jax.numpy as jnp
from jax import lax
import numpy as np

D_MODEL = 1024
BATCH = 1
SEQ = 256
DEPTH = 1

HG_HEADS = 8
HG_KEY_DIM = 128
HG_VAL_DIM = D_MODEL // HG_HEADS
HG_KEY = HG_HEADS * HG_KEY_DIM
HG_VAL = HG_HEADS * HG_VAL_DIM
HG_CHUNK = 64
SG_GROUPS = 8
SG_GROUP_DIM = 64
SG_WIDTH = SG_GROUPS * SG_GROUP_DIM
SG_CHUNK = 128
FFN_HIDDEN = ((8 * D_MODEL // 3 + 255) // 256) * 256
PLE_DIM = 256
EPS = 1e-6
IN_SPLITS = (HG_KEY, HG_KEY, HG_KEY, HG_VAL, HG_VAL, SG_WIDTH, SG_WIDTH, D_MODEL, D_MODEL)
N_IN = HG_KEY * 3 + HG_VAL * 2 + SG_WIDTH * 2 + D_MODEL * 2


def rms_norm(x, g):
    xf = x.astype(jnp.float32)
    y = xf * lax.rsqrt(jnp.mean(xf * xf, axis=-1, keepdims=True) + EPS)
    return (y * g.astype(jnp.float32)).astype(x.dtype)

def layer_norm(x, g, b):
    xf = x.astype(jnp.float32)
    mu = jnp.mean(xf, axis=-1, keepdims=True)
    xc = xf - mu
    y = xc * lax.rsqrt(jnp.mean(xc * xc, axis=-1, keepdims=True) + EPS)
    return (y * g.astype(jnp.float32) + b.astype(jnp.float32)).astype(x.dtype)

def layer_lower_bounds(gamma):
    sm = jax.nn.softmax(gamma.astype(jnp.float32), axis=0)
    return jnp.cumsum(sm, axis=0) - sm[0:1]

def _to_chunks(t):
    b, s, h, d = t.shape
    return t.reshape(b, s // HG_CHUNK, HG_CHUNK, h, d).transpose(1, 0, 3, 2, 4)

def hgrn2_direction(q, k, v, logf):
    bsz, s, h, dk = q.shape
    dv = v.shape[-1]
    mask = jnp.tril(jnp.ones((HG_CHUNK, HG_CHUNK), dtype=jnp.float32))

    def step(state, inp):
        qc, kc, vc, gc = inp
        b = jnp.cumsum(gc, axis=2)
        o_inter = jnp.einsum('bhtk,bhkv->bhtv', qc * jnp.exp(b), state)
        diff = b[:, :, :, None, :] - b[:, :, None, :, :]
        decay = jnp.exp(jnp.minimum(diff, 0.0)) * mask[:, :, None]
        scores = jnp.einsum('bhtk,bhsk,bhtsk->bhts', qc, kc, decay)
        o_intra = jnp.einsum('bhts,bhsv->bhtv', scores, vc)
        b_last = b[:, :, -1:, :]
        new_state = (jnp.exp(b_last[:, :, 0, :])[..., None] * state
                     + jnp.einsum('bhsk,bhsv->bhkv', kc * jnp.exp(b_last - b), vc))
        return new_state, o_inter + o_intra

    init = jnp.zeros((bsz, h, dk, dv), jnp.float32)
    _, o = lax.scan(step, init, (_to_chunks(q), _to_chunks(k), _to_chunks(v), _to_chunks(logf)))
    return o.transpose(1, 0, 3, 2, 4).reshape(bsz, s, h, dv)

def hgrn2_mixer(zq, zf_fwd, zf_bwd, zi, zg, lb_f, lb_b, norm_g):
    bsz, s, _ = zq.shape
    f32 = jnp.float32
    tiny = jnp.finfo(f32).tiny
    q = jax.nn.silu(zq.astype(f32)).reshape(bsz, s, HG_HEADS, HG_KEY_DIM)
    v = zi.astype(f32).reshape(bsz, s, HG_HEADS, HG_VAL_DIM)

    def gates(zf, lb):
        zf = zf.astype(f32)
        f = lb + (1.0 - lb) * jax.nn.sigmoid(zf)
        logf = jnp.log(jnp.maximum(f, tiny))
        k = (1.0 - lb) * jax.nn.sigmoid(-zf)
        return (k.reshape(bsz, s, HG_HEADS, HG_KEY_DIM), logf.reshape(bsz, s, HG_HEADS, HG_KEY_DIM))

    k_f, logf_f = gates(zf_fwd, lb_f)
    k_b, logf_b = gates(zf_bwd, lb_b)
    o_fwd = hgrn2_direction(q, k_f, v, logf_f)
    o_bwd = hgrn2_direction(q[:, ::-1], k_b[:, ::-1], v[:, ::-1], logf_b[:, ::-1])[:, ::-1]
    o = o_fwd + o_bwd
    o = rms_norm(o, norm_g.reshape(HG_HEADS, HG_VAL_DIM)).reshape(bsz, s, HG_VAL)
    return (o * jax.nn.silu(zg.astype(f32))).astype(zq.dtype)

def spatial_gating(zu, zv, w_s, b_s, ln_g, ln_b):
    bsz, s, _ = zu.shape
    u = jax.nn.gelu(zu, approximate=False)
    v = layer_norm(jax.nn.gelu(zv, approximate=False), ln_g, ln_b)
    vr = v.reshape(bsz, s // SG_CHUNK, SG_CHUNK, SG_GROUPS, SG_GROUP_DIM)
    sg = jnp.einsum('gts,bcsge->bctge', w_s, vr) + b_s.T[None, None, :, :, None]
    return u * sg.reshape(bsz, s, SG_WIDTH)

def first_inputs(seed: int = 0) -> dict:
    key = jax.random.key(seed)
    ks = jax.random.split(key, 24)
    f32 = jnp.float32

    def nrm(k, shape, scale):
        return jax.random.normal(k, shape, f32) * scale

    def gain(k, shape):
        return 1.0 + 0.05 * jax.random.normal(k, shape, f32)

    return {
        "x": nrm(ks[0], (BATCH, SEQ, D_MODEL), 1.0),
        "p": nrm(ks[1], (DEPTH, BATCH, SEQ, PLE_DIM), 1.0),
        "norm_mix_pre": gain(ks[2], (DEPTH, D_MODEL)),
        "w_in": nrm(ks[3], (DEPTH, D_MODEL, N_IN), D_MODEL ** -0.5),
        "lb_gamma_fwd": nrm(ks[4], (DEPTH, HG_KEY), 0.1),
        "lb_gamma_bwd": nrm(ks[5], (DEPTH, HG_KEY), 0.1),
        "hg_norm": gain(ks[6], (DEPTH, HG_VAL)),
        "sg_w": nrm(ks[7], (DEPTH, SG_GROUPS, SG_CHUNK, SG_CHUNK), SG_CHUNK ** -0.5),
        "sg_b": gain(ks[8], (DEPTH, SG_GROUPS, SG_CHUNK)),
        "sg_ln_g": gain(ks[9], (DEPTH, SG_WIDTH)),
        "sg_ln_b": nrm(ks[10], (DEPTH, SG_WIDTH), 0.02),
        "w_a": nrm(ks[11], (DEPTH, HG_VAL, D_MODEL), HG_VAL ** -0.5),
        "w_b": nrm(ks[12], (DEPTH, SG_WIDTH, D_MODEL), SG_WIDTH ** -0.5),
        "w_out": nrm(ks[13], (DEPTH, D_MODEL, D_MODEL), D_MODEL ** -0.5),
        "norm_mix_post": gain(ks[14], (DEPTH, D_MODEL)),
        "norm_ffn_pre": gain(ks[15], (DEPTH, D_MODEL)),
        "w_gate": nrm(ks[16], (DEPTH, D_MODEL, FFN_HIDDEN), D_MODEL ** -0.5),
        "w_up": nrm(ks[17], (DEPTH, D_MODEL, FFN_HIDDEN), D_MODEL ** -0.5),
        "w_down": nrm(ks[18], (DEPTH, FFN_HIDDEN, D_MODEL), FFN_HIDDEN ** -0.5),
        "norm_ffn_post": gain(ks[19], (DEPTH, D_MODEL)),
        "w_ple": nrm(ks[20], (DEPTH, PLE_DIM, D_MODEL), PLE_DIM ** -0.5),
        "w_ple_gate": nrm(ks[21], (DEPTH, D_MODEL, D_MODEL), D_MODEL ** -0.5),
    }

def first_block(x, p, norm_mix_pre, w_in, lb_gamma_fwd, lb_gamma_bwd, hg_norm, sg_w, sg_b,
              sg_ln_g, sg_ln_b, w_a, w_b, w_out, norm_mix_post, norm_ffn_pre, w_gate, w_up,
              w_down, norm_ffn_post, w_ple, w_ple_gate):
    lb_fwd_all = layer_lower_bounds(lb_gamma_fwd)
    lb_bwd_all = layer_lower_bounds(lb_gamma_bwd)
    offsets = [int(o) for o in np.cumsum(IN_SPLITS)[:-1]]
    for l in range(DEPTH):
        h = rms_norm(x, norm_mix_pre[l])
        z = jnp.einsum('bsd,dn->bsn', h, w_in[l])
        zq, zf_f, zf_b, zi, zg, zu, zv, ga, gb = jnp.split(z, offsets, axis=-1)
        a_out = hgrn2_mixer(zq, zf_f, zf_b, zi, zg, lb_fwd_all[l], lb_bwd_all[l], hg_norm[l])
        b_out = spatial_gating(zu, zv, sg_w[l], sg_b[l], sg_ln_g[l], sg_ln_b[l])
        merged = (jax.nn.sigmoid(ga) * jnp.einsum('bsv,vd->bsd', a_out, w_a[l])
                  + jax.nn.sigmoid(gb) * jnp.einsum('bsw,wd->bsd', b_out, w_b[l]))
        mix = jnp.einsum('bsd,de->bse', merged, w_out[l])
        x = x + rms_norm(mix, norm_mix_post[l])
        h2 = rms_norm(x, norm_ffn_pre[l])
        ff = jnp.einsum('bsf,fd->bsd',
                        jax.nn.silu(jnp.einsum('bsd,df->bsf', h2, w_gate[l]))
                        * jnp.einsum('bsd,df->bsf', h2, w_up[l]), w_down[l])
        x = x + rms_norm(ff, norm_ffn_post[l])
        x = x + (jnp.einsum('bse,ed->bsd', p[l], w_ple[l])
                 * jax.nn.sigmoid(jnp.einsum('bsd,de->bse', x, w_ple_gate[l])))
    return x


DEPTH_2 = 2

N_MIXERS = 2
FOURIER_GROUPS = 4
FOURIER_GROUP_DIM = D_MODEL // FOURIER_GROUPS
RET_HEADS = 4
RET_QK_DIM = D_MODEL // RET_HEADS
RET_V_DIM = 2 * RET_QK_DIM
RET_CHUNK = 128
ROPE_BASE = 10000.0
D_FF = -(-8 * D_MODEL // (3 * 256)) * 256


def rmsnorm(x, g):
    xf = x.astype(jnp.float32)
    y = xf * lax.rsqrt(jnp.mean(xf * xf, axis=-1, keepdims=True) + EPS)
    return (y * g.astype(jnp.float32)).astype(x.dtype)

def modulate(h, shift, scale):
    return h * (1.0 + scale[:, None, :]) + shift[:, None, :]

def fourier_mixer(h, w_o):
    B, S, D = h.shape
    hg = h.astype(jnp.float32).reshape(B, S, FOURIER_GROUPS, FOURIER_GROUP_DIM)
    f = jnp.fft.fftn(hg, axes=(1, 3), norm="ortho").real.astype(h.dtype)
    return f.reshape(B, S, D) @ w_o

def rotary(x, pos):
    half = x.shape[-1] // 2
    inv_freq = ROPE_BASE ** (-jnp.arange(half, dtype=jnp.float32) / half)
    ang = pos[:, None] * inv_freq[None, :]
    cos, sin = jnp.cos(ang), jnp.sin(ang)
    x1, x2 = x[..., :half], x[..., half:]
    return jnp.concatenate([x1 * cos - x2 * sin, x1 * sin + x2 * cos], axis=-1)

def chunk_retention(q, k, v, log_gamma, inclusive):
    B, H, S, dk = q.shape
    dv = v.shape[-1]
    C = RET_CHUNK
    N = S // C
    to_chunks = lambda a: jnp.moveaxis(a.reshape(B, H, N, C, a.shape[-1]), 2, 0)
    qc, kc, vc = to_chunks(q), to_chunks(k), to_chunks(v)

    t = jnp.arange(C)
    diff = t[:, None] - t[None, :]
    mask = (diff >= 0) if inclusive else (diff > 0)
    lg = log_gamma.astype(jnp.float32)[:, None, None]
    dmask = jnp.where(mask, jnp.exp(jnp.where(mask, diff, 0).astype(jnp.float32) * lg), 0.0)
    tf = t.astype(jnp.float32)[None, :, None]
    q_decay = jnp.exp((tf + 1.0) * lg)
    k_decay = jnp.exp((C - 1.0 - tf) * lg)
    chunk_decay = jnp.exp(C * lg)

    def step(R, xs):
        qb, kb, vb = xs
        scores = jnp.einsum('bhtd,bhsd->bhts', qb, kb) * dmask
        inner = jnp.einsum('bhts,bhsv->bhtv', scores, vb)
        cross = jnp.einsum('bhtd,bhdv->bhtv', qb, R) * q_decay
        R = R * chunk_decay + jnp.einsum('bhsd,bhsv->bhdv', kb * k_decay, vb)
        return R, inner + cross

    R0 = jnp.zeros((B, H, dk, dv), jnp.float32)
    _, out = lax.scan(step, R0, (qc, kc, vc))
    return jnp.moveaxis(out, 0, 2).reshape(B, H, S, dv)

def retention_mixer(h, w_in, w_out, log_g_fwd, log_g_bwd):
    B, S, _ = h.shape
    H, dk, dv = RET_HEADS, RET_QK_DIM, RET_V_DIM
    proj = h @ w_in
    q, k, v, g = jnp.split(proj, [H * dk, 2 * H * dk, 2 * H * dk + H * dv], axis=-1)
    heads = lambda a, d: a.astype(jnp.float32).reshape(B, S, H, d).transpose(0, 2, 1, 3)
    pos = jnp.arange(S, dtype=jnp.float32)
    q = rotary(heads(q, dk), pos)
    k = rotary(heads(k, dk), pos) * (dk ** -0.5)
    v = heads(v, dv)
    y_fwd = chunk_retention(q, k, v, log_g_fwd, True)
    flip = lambda a: jnp.flip(a, axis=2)
    y_bwd = flip(chunk_retention(flip(q), flip(k), flip(v), log_g_bwd, False))
    y = y_fwd + y_bwd
    mu = jnp.mean(y, axis=-1, keepdims=True)
    var = jnp.mean(jnp.square(y - mu), axis=-1, keepdims=True)
    y = (y - mu) * lax.rsqrt(var + EPS)
    y = y.transpose(0, 2, 1, 3).reshape(B, S, H * dv).astype(h.dtype)
    return (jax.nn.silu(g) * y) @ w_out

def swiglu(h, w_in, w_out):
    gate, up = jnp.split(h @ w_in, 2, axis=-1)
    return (jax.nn.silu(gate) * up) @ w_out

def second_inputs(seed: int = 0) -> dict:
    key = jax.random.key(seed)
    ks = jax.random.split(key, 14)
    D, F = D_MODEL, D_FF
    n_four = len(range(0, DEPTH_2, N_MIXERS))
    n_ret = len(range(1, DEPTH_2, N_MIXERS))
    ret_in_w = 2 * RET_HEADS * RET_QK_DIM + 2 * RET_HEADS * RET_V_DIM
    ret_v_w = RET_HEADS * RET_V_DIM
    nrm = lambda k, shape, s: jax.random.normal(k, shape, jnp.float32) * s
    return {
        "x": nrm(ks[0], (BATCH, SEQ, D), 1.0),
        "c": nrm(ks[1], (BATCH, D), 1.0),
        "w_ada": nrm(ks[2], (DEPTH_2, D, 6 * D), 0.5 * D ** -0.5),
        "b_ada": nrm(ks[3], (DEPTH_2, 6 * D), 0.01),
        "norm_mix_g": 1.0 + nrm(ks[4], (DEPTH_2, D), 0.02),
        "norm_ffn_g": 1.0 + nrm(ks[5], (DEPTH_2, D), 0.02),
        "w_fourier_out": nrm(ks[6], (n_four, D, D), D ** -0.5),
        "w_ret_in": nrm(ks[7], (n_ret, D, ret_in_w), D ** -0.5),
        "w_ret_out": nrm(ks[8], (n_ret, ret_v_w, D), ret_v_w ** -0.5),
        "w_ffn_in": nrm(ks[9], (DEPTH_2, D, 2 * F), D ** -0.5),
        "w_ffn_out": nrm(ks[10], (DEPTH_2, F, D), F ** -0.5),
        "final_norm_g": 1.0 + nrm(ks[11], (D,), 0.02),
        "w_ada_final": nrm(ks[12], (D, 2 * D), 0.5 * D ** -0.5),
        "b_ada_final": nrm(ks[13], (2 * D,), 0.01),
    }

def second_block(x, c, w_ada, b_ada, norm_mix_g, norm_ffn_g, w_fourier_out, w_ret_in, w_ret_out,
              w_ffn_in, w_ffn_out, final_norm_g, w_ada_final, b_ada_final):
    hidx = jnp.arange(RET_HEADS, dtype=jnp.float32)
    log_g_fwd = jnp.log1p(-jnp.exp2(-5.0 - hidx))
    log_g_bwd = jnp.flip(log_g_fwd)
    c_act = jax.nn.silu(c)
    for i in range(DEPTH_2):
        mod = c_act @ w_ada[i] + b_ada[i]
        sh1, sc1, g1, sh2, sc2, g2 = jnp.split(mod, 6, axis=-1)
        h = modulate(rmsnorm(x, norm_mix_g[i]), sh1, sc1)
        j = i // N_MIXERS
        if i % N_MIXERS == 0:
            m = fourier_mixer(h, w_fourier_out[j])
        else:
            m = retention_mixer(h, w_ret_in[j], w_ret_out[j], log_g_fwd, log_g_bwd)
        x = x + g1[:, None, :] * m
        h = modulate(rmsnorm(x, norm_ffn_g[i]), sh2, sc2)
        x = x + g2[:, None, :] * swiglu(h, w_ffn_in[i], w_ffn_out[i])
    shf, scf = jnp.split(c_act @ w_ada_final + b_ada_final, 2, axis=-1)
    return modulate(rmsnorm(x, final_norm_g), shf, scf)


def setup_inputs(seed=0):
    out = dict(first_inputs(seed))
    for name, value in second_inputs(seed + 1).items():
        if name != "x":
            out[name + "_2"] = value
    return out


def reference(
    x, p, norm_mix_pre, w_in, lb_gamma_fwd, lb_gamma_bwd, hg_norm, sg_w, sg_b, sg_ln_g, sg_ln_b,
    w_a, w_b, w_out, norm_mix_post, norm_ffn_pre, w_gate, w_up, w_down, norm_ffn_post, w_ple,
    w_ple_gate, c_2, w_ada_2, b_ada_2, norm_mix_g_2, norm_ffn_g_2, w_fourier_out_2, w_ret_in_2,
    w_ret_out_2, w_ffn_in_2, w_ffn_out_2, final_norm_g_2, w_ada_final_2, b_ada_final_2,
):
    x = first_block(
        x, p, norm_mix_pre, w_in, lb_gamma_fwd, lb_gamma_bwd, hg_norm, sg_w, sg_b, sg_ln_g,
        sg_ln_b, w_a, w_b, w_out, norm_mix_post, norm_ffn_pre, w_gate, w_up, w_down,
        norm_ffn_post, w_ple, w_ple_gate,
    )
    return second_block(
        x, c_2, w_ada_2, b_ada_2, norm_mix_g_2, norm_ffn_g_2, w_fourier_out_2, w_ret_in_2,
        w_ret_out_2, w_ffn_in_2, w_ffn_out_2, final_norm_g_2, w_ada_final_2, b_ada_final_2,
    )


_drawn_inputs = setup_inputs


def setup_inputs(seed=0):
    import zlib

    import numpy as np

    out = dict(_drawn_inputs(seed))
    spreads = {}
    factors = {'sg_b': 2.684,
     'sg_ln_b': 5.742,
     'b_ada_2': 6.359,
     'norm_mix_g_2': 8.0,
     'norm_ffn_g_2': 8.0,
     'final_norm_g_2': 2.824,
     'b_ada_final_2': 4.281}
    for name, (base, spread) in spreads.items():
        noise = np.random.default_rng([zlib.crc32(name.encode()), seed]).standard_normal(out[name].shape)
        drawn = base * np.exp(spread * noise) if base else spread * noise
        out[name] = __import__('jax').numpy.asarray(drawn.astype(out[name].dtype))
    for name, factor in factors.items():
        out[name] = (out[name] * factor).astype(out[name].dtype)
    return out
```

```python
from contextlib import ExitStack

import concourse.bass as bass
from concourse import mybir

F32 = mybir.dt.float32
F32R = mybir.dt.float32r
U8 = mybir.dt.uint8
ALU = mybir.AluOpType
ACT = mybir.ActivationFunctionType
AX = mybir.AxisListType

P = 128
S = 256
TT = S // P
D = 1024
KT = D // P
FF = 2816
FT = FF // P
HEADS = 8
HH = HEADS // 2
RH = 4
RV = 512
EPS = 1e-6
TINY = 1.1754943508222875e-38

RAW = 3
WS = 4
GROUPS = FT // 2

STAGES = [("zu", 2), ("zv", 2), ("qa", 2), ("fa", 2), ("ba", 2), ("zi", 4), ("zg", 4),
          ("qb", 2), ("fb", 2), ("bb", 2), ("ga", 4), ("gb", 4), ("wa", 4), ("wb", 2),
          ("wout", 4), ("ffn0", 2 * GROUPS), ("down0", GROUPS), ("ple", 1), ("pleg", 4),
          ("fo", 4), ("ffn1", 2 * GROUPS), ("down1", GROUPS), ("rq", 4), ("rk", 4), ("rv", 8),
          ("rg", 8), ("ro", 8), ("ffn2", 2 * GROUPS), ("down2", GROUPS)]
W0 = {}
NW = 0
for _name, _n in STAGES:
    W0[_name] = NW
    NW += _n

NADA = 56
ADA_TICKS = list(range(5, 10)) + list(range(18, 24)) + list(range(32, 37))
ADA_TICKS += [W0["ffn0"] + 2 * j for j in range(GROUPS)]
ADA_TICKS += [W0["ffn1"] + 2 * j for j in range(GROUPS)]
ADA_TICKS += [W0["down1"] + j for j in range(7)]
ADA_TICKS += [W0["ffn2"] + 2 * j for j in range(GROUPS)]
assert len(ADA_TICKS) == NADA
ADA_AT = {w: a for a, w in enumerate(ADA_TICKS)}
ADA_STATIC = {w: a for w, a in ADA_AT.items() if not any(W0[f] <= w < W0[f] + 2 * GROUPS for f in ("ffn0", "ffn1", "ffn2"))}


def stream_order():
    order = [("w", w) for w in range(WS)]
    for w in range(NW):
        if w + WS < NW:
            order.append(("w", w + WS))
        if w in ADA_AT:
            order.append(("a", ADA_AT[w]))
    return order


ORDER = stream_order()
AT_RAW = {c: n for n, c in enumerate(ORDER)}
NRAW = len(ORDER)

COLS = {}
NCOL = 0
for _name, _n in [("mix_pre", 8), ("ffn_pre", 8), ("mix_g", 16), ("ffn_g", 16), ("fin_g", 8),
                  ("c", 8), ("gamma", 16), ("sg_b", 8), ("b_ada", 112)]:
    COLS[_name] = NCOL
    NCOL += _n


def plan_psum():
    use, u = {}, 0
    for name, n in [("zu", 1), ("zv", 1), ("qa", 1), ("fa", 1), ("ba", 1), ("zi", 2), ("zg", 2),
                    ("qb", 1), ("fb", 1), ("bb", 1), ("ga", 2), ("gb", 2), ("wa", 2), ("wb", 2),
                    ("wout", 2), ("ffn0", GROUPS), ("down0", 2), ("ple", 2), ("pleg", 2),
                    ("fo", 2), ("ffn1", GROUPS), ("down1", 2), ("rq", 2), ("rk", 2), ("rv", 4),
                    ("rg", 4), ("ro", 2), ("ffn2", GROUPS), ("down2", 2)]:
        use[name] = u
        u += n
    jobs, release, split, counts, splits, k = {}, [], {}, {}, 0, 0
    table = [("norm0", 4, "norm"), ("sgu", 2, "sgu_read"), ("pa", 16, "p_copied"),
             ("offa", 2, "off_copied"), ("pva", 2, "pv_read"), ("pb", 16, "p_copied"),
             ("offb", 2, "off_copied"), ("pvb", 2, "pv_read"), ("ta", 4, "split"),
             ("tb", 2, "split"), ("tm", 4, "split"), ("norm1", 4, "norm"),
             ("h0", GROUPS, "split"), ("rows0", 2, "row_copied"), ("tx", 4, "split"),
             ("norm2", 4, "norm"), ("dft1", 8, "split"), ("dft2", 4, "split"),
             ("rows1", 2, "row_copied"), ("norm3", 4, "norm"), ("h1", GROUPS, "split"),
             ("rows2", 2, "row_copied"), ("norm4", 4, "norm"), ("sc", 4, "sc_read"),
             ("av", 8, "av_read"), ("ty", 8, "split"), ("norm5", 4, "norm"),
             ("h2", GROUPS, "split"), ("rows3", 2, "row_copied"), ("norm6", 4, "fin_read")]
    for name, n, kind in table:
        jobs[name] = k
        for _ in range(n):
            if kind in ("norm", "split"):
                split[k] = splits
                splits += 1
            sem = {"norm": "norm_read", "split": "lo_done"}.get(kind, kind)
            if kind == "split":
                release.append((sem, splits))
            else:
                counts[sem] = counts.get(sem, 0) + 1
                release.append((sem, counts[sem]))
            k += 1
    return use, jobs, release, split


USE, JOB, RELEASE, SPLIT = plan_psum()

RQ = {}
NRQ = 0
for _name, _n in [("norm0", 2), ("ln", 2), ("pva", 2), ("pvb", 2), ("mix", 4), ("ffn", 2),
                  ("norm2", 2), ("norm3", 2), ("norm4", 2), ("av", 8), ("norm5", 2), ("norm6", 2)]:
    RQ[_name] = NRQ
    NRQ += _n
SS = {q: n + 1 for n, q in enumerate(RQ[name] + t for name, k in [
    ("norm0", 2), ("mix", 4), ("ffn", 2), ("norm2", 2), ("norm3", 2), ("norm4", 2), ("norm5", 2), ("norm6", 2)]
    for t in range(k))}


def program(nc, stream, x, pT, cols, rows, sg_wT, masks, ident, dft, rot, decay, outT):
    with ExitStack() as ctx:
        base = (nc.sbuf_base + 255) // 256 * 256

        def sb(name, kb, shape, dt=F32):
            return nc.alloc_sbuf_tensor_at(name, shape, dt, offset=int(base + kb * 1024))

        raw = sb("raw", 0, [P, RAW, 2048])
        w_hi = sb("w_hi", 24, [P, WS, 2048], F32R)
        w_lo = sb("w_lo", 56, [P, WS, 2048], F32R)
        ht = [sb("ht_hi", 96, [P, KT, S], F32R), sb("ht_lo", 104, [P, KT, S], F32R)]
        gt = [sb("gt_hi", 112, [P, FT, S], F32R), sb("gt_lo", 134, [P, FT, S], F32R)]
        xres = sb("xres", 156, [P, TT, D])
        xn = sb("xn", 164, [P, TT, D])
        idn = sb("idn", 172, [P, P])
        ones = sb("ones", 172.5, [P, P])
        col = sb("col", 173, [P, NCOL])
        mod = sb("mod", 173.875, [P, 112])
        moda = sb("moda", 174.375, [P, 5, 8])
        ca = sb("ca", 174.625, [P, 8])
        lbt = sb("lbt", 174.75, [P, 5, 16])
        expo = sb("expo", 175.125, [P, 4])
        st = sb("st", 175.25, [P, NRQ, 3, 4])
        bn = sb("bn", 177, [P, 2, 6])
        mv = sb("mv", 177.125, [P, 2, 2])
        acc = sb("acc", 177.25, [P, 2, 2, 256])
        hb = sb("hb", 181.25, [P, 2, 512])
        ga = sb("ga", 156, [P, TT, D])
        gb = sb("gb", 193.25, [P, TT, D])
        vv = sb("vv", 164, [P, TT, D])
        zg = sb("zg", 185.25, [P, TT, D])
        hgrow = sb("hgrow", 201.25, [P, 2, 512])
        msk = sb("msk", 205.25, [P, 8, P], U8)
        sgw = sb("sgw", 185.25, [P, HEADS, P])
        vg = sb("vg", 189.25, [P, TT, 512])
        lnrow = sb("lnrow", 193.25, [P, 2, 512])
        qf = sb("qf", 112, [P, HH, S])
        qb = sb("qb", 116, [P, HH, S])
        kf = sb("kf", 120, [P, HH, S])
        kb = sb("kb", 124, [P, HH, S])
        tf = sb("tf", 128, [P, HH, S])
        tb = sb("tb", 132, [P, HH, S])
        sq = sb("sq", 136, [P, HH, S])
        sk = sb("sk", 140, [P, HH, S])
        at = sb("at", 144, [P, 2, HH, S])
        u = sb("u", 152, [P, TT, 512])
        mskf = sb("mskf", 88, [P, 8, P])
        osq = sb("osq", 88, [P, TT, 512])
        on = sb("on", 92, [P, TT, 512])
        prow = sb("prow", 185.25, [P, 2, D])
        praw = sb("praw", 193.25, [P, 2, S])
        pt = [sb("pt_hi", 195.25, [P, 2, S], F32R), sb("pt_lo", 197.25, [P, 2, S], F32R)]
        dg = sb("dg", 88, [P, KT, P])
        prod = sb("prod", 92, [P, 2, TT, 256])
        csr = sb("csr", 112, [P, 2, 768])
        cs = [sb("cs_hi", 185.25, [P, 2, 768], F32R), sb("cs_lo", 191.25, [P, 2, 768], F32R)]
        grow = [sb("grow0", 201.25, [P, D]), sb("grow1", 197.25, [P, D])]
        tt = [sb("tt_hi", 112, [P, TT, 4, 512], F32R), sb("tt_lo", 134, [P, TT, 4, 512], F32R)]
        qr = sb("qr", 112, [P, RH, 2, S])
        kr = sb("kr", 120, [P, RH, 2, S])
        vr = sb("vr", 128, [P, TT, RH * RV])
        ar = sb("ar", 144, [P, RH, 2, S])
        yr = sb("yr", 112, [P, TT, RH * RV])
        gg = sb("gg", 185.25, [P, TT, RH * RV])
        dt = sb("dt", 88, [P, RH, 2, S])
        rt = sb("rt", 205.25, [P, 2, S])
        rab = sb("rab", 164, [P, 2, 4, S])
        gsig = sb("gsig", 118, [P, TT, D])
        outb = sb("outb", 185.25, [P, 4, 512])

        pair = [ctx.enter_context(nc.psum_tensor(f"pair{i}", [P, 2, 512], F32)) for i in range(2)]
        tp = [ctx.enter_context(nc.psum_tensor(f"tp{i}", [P, 512], F32)) for i in range(2)]
        adap = ctx.enter_context(nc.psum_tensor("adap", [P, 512], F32))

        sems = {}

        def sem(name):
            if name not in sems:
                sems[name] = ctx.enter_context(nc.semaphore(name))
            return sems[name]

        landed = [sem(f"landed{i}") for i in range(RAW)]
        raw_done = sem("raw_done")
        hi_done = sem("hi_done")
        w_used = sem("w_used")
        half_ready = sem("half_ready")
        evac = [sem("evac0"), sem("evac1")]
        tp_done = sem("tp_done")
        t_hi = sem("t_hi")
        lo_done = sem("lo_done")
        norm_read = sem("norm_read")
        ada_step = sem("ada_step")
        ada_used = sem("ada_used")
        ss_done = sem("ss_done")
        ms_done = sem("ms_done")
        rstd_done = sem("rstd_done")
        xn_done = sem("xn_done")
        x_ready = sem("x_ready")
        x_in = sem("x_in")
        small_in = sem("small_in")
        sgu_in = sem("sgu_in")
        hg_in = sem("hg_in")
        x_again = sem("x_again")
        prow_in = sem("prow_in")
        p_in = sem("p_in")
        dft_in = sem("dft_in")
        rot_in = sem("rot_in")
        decay_in = sem("decay_in")
        out_done = sem("out_done")
        consts = sem("consts")
        step = sem("step")
        a_step = sem("a_step")
        lb_e = sem("lb_e")
        ca_done = sem("ca_done")
        ln_done = sem("ln_done")
        hg_sk0 = sem("hg_sk0")
        hg_staged = sem("hg_staged")
        hg_qupd = sem("hg_qupd")
        hg_kupd = sem("hg_kupd")
        hg_tot = sem("hg_tot")
        pv_sq = sem("pv_sq")
        a_out = sem("a_out")
        b_out = sem("b_out")
        merged = sem("merged")
        silu_done = sem("silu_done")
        pt_hi = sem("pt_hi")
        pt_done = sem("pt_done")
        sig_done = sem("sig_done")
        cs_hi = sem("cs_hi")
        cs_done = sem("cs_done")
        dg_done = sem("dg_done")
        rot_done = sem("rot_done")
        y_done = sem("y_done")

        def colv(name, i, n=1):
            return col[:, COLS[name] + i:COLS[name] + i + n]

        def at_least(eng, s, value, per=0, i=None):
            if i is None or per == 0:
                if value > 0:
                    eng.wait_ge(s, value)
            else:
                assert value > 0
                eng.wait_ge(s, i * per + value)

        def wait_evac(eng, use, passes=None):
            at_least(eng, evac[use % 2], use // 2 + 1, 1, passes)

        block = ctx.enter_context(nc.Block())

        @block.sync
        def _(sp):
            for n in range(RAW):
                sp.dma_start(raw[:, n, :], stream[n]).then_inc(landed[n], 16)
            turns = NRAW // RAW
            with sp.Fori(1, turns) as i:
                for n in range(RAW):
                    sp.wait_ge(raw_done, i * RAW + (n + 1 - RAW))
                    sp.dma_start(raw[:, n, :], stream[i * RAW + n]).then_inc(landed[n], 16)
            for n in range(turns * RAW, NRAW):
                sp.wait_ge(raw_done, n + 1 - RAW)
                sp.dma_start(raw[:, n % RAW, :], stream[n]).then_inc(landed[n % RAW], 16)
            for j in range(4):
                t, half = j // 2, j % 2
                sp.wait_ge(sem("fin_read"), j + 1)
                dst = outT[4 * half:4 * half + 4, :, t * P:(t + 1) * P].rearrange("k p s -> p k s")
                sp.dma_start(dst, outb[:, j, :].rearrange("p (k s) -> p k s", k=4)).then_inc(out_done, 16)
            sp.wait_ge(out_done, 64)

        @block.gpsimd
        def _(pool):
            g = nc.gpsimd
            pool.dma_start(xres[:], x).then_inc(x_in, 16)
            pool.dma_start(idn[:], ident).then_inc(small_in, 16)
            pool.dma_start(col[:], cols).then_inc(small_in, 16)
            g.memset(ones[:], 1.0)
            g.memset(expo[:], -0.5).then_inc(consts, 1)
            pool.dma_start(sgw[:], sg_wT).then_inc(sgu_in, 16)
            pool.dma_start(lnrow[:, 0, :], rows[0:1, 0:512].to_broadcast([P, 512])).then_inc(sgu_in, 16)
            pool.dma_start(lnrow[:, 1, :], rows[0:1, 512:1024].to_broadcast([P, 512])).then_inc(sgu_in, 16)
            pool.dma_start(hgrow[:].rearrange("p a b -> p (a b)"), rows[1:2, :].to_broadcast([P, D])).then_inc(hg_in, 16)
            pool.dma_start(mskf[:], masks).then_inc(hg_in, 16)
            pool.wait_ge(consts, 1)

            def rsqrt(q, n=1, w=1):
                for r in range(q, q + n):
                    pool.wait_ge(ms_done, r + 1)
                    g.tensor_tensor(st[:, r, 2, 0:w], st[:, r, 1, 0:w], expo[:, 0:w], ALU.pow).then_inc(rstd_done, 1)

            def key_updates(half):
                for lv in range(1, 8):
                    h = 1 << (lv - 1)
                    v = [a[:].rearrange("p a (b two h) -> p (a b) two h", two=2, h=h) for a in (kf, kb, tf, tb)]
                    nb = HH * S // (2 * h)
                    pool.wait_ge(hg_staged, 8 * half + lv + 1)
                    if lv == 1:
                        pool.wait_ge(hg_qupd, 8 * half + 1)
                    else:
                        pool.wait_ge(hg_tot, 6 * half + lv - 1)
                    g.tensor_tensor(v[0][:, :, 0, :], v[0][:, :, 0, :], v[2][:, :, 1, 0:1].to_broadcast([P, nb, h]), ALU.mult)
                    g.tensor_tensor(v[1][:, :, 1, :], v[1][:, :, 1, :], v[3][:, :, 0, 0:1].to_broadcast([P, nb, h]), ALU.mult).then_inc(hg_kupd, 1)

            rsqrt(RQ["norm0"], 2)
            rsqrt(RQ["ln"], 2)
            key_updates(0)
            rsqrt(RQ["pva"], 2, 4)
            key_updates(1)
            rsqrt(RQ["pvb"], 2, 4)
            pool.wait_ge(tp_done, JOB["tm"] + 4)
            pool.dma_start(xres[:], x).then_inc(x_again, 16)
            pool.dma_start(prow[:].rearrange("p a b -> p (a b)"),
                           rows[2:4, :].rearrange("(o a) b -> o (a b)", o=1).to_broadcast([P, 2 * D])).then_inc(prow_in, 16)
            pool.dma_start(praw[:], pT).then_inc(p_in, 16)
            rsqrt(RQ["mix"], 4)
            rsqrt(RQ["ffn"], 2)
            pool.wait_ge(w_used, W0["down0"] + GROUPS)
            pool.dma_start(csr[:], dft).then_inc(dft_in, 16)
            rsqrt(RQ["norm2"], 2)
            rsqrt(RQ["norm3"], 2)
            pool.wait_ge(tp_done, JOB["rows2"] + 2)
            pool.dma_start(dt[:], decay).then_inc(decay_in, 16)
            pool.dma_start(rt[:], rot).then_inc(rot_in, 16)
            rsqrt(RQ["norm4"], 2)
            rsqrt(RQ["av"], 8)
            rsqrt(RQ["norm5"], 2)
            rsqrt(RQ["norm6"], 2)

        @block.tensor
        def _(pe):
            def passes(a, b):
                return [(a[1], b[0]), (a[0], b[0]), (a[0], b[1])]

            wsp = (w_hi, w_lo)

            def wait_chunk(w, i=None):
                at_least(pe, raw_done, AT_RAW["w", w] + 1, 6, i)

            def claim_pair(use, i=None):
                if use >= 2:
                    wait_evac(pe, use - 2, i)

            def claim(k):
                if k >= 2:
                    name, value = RELEASE[k - 2]
                    pe.wait_ge(sem(name), value)

            def wide_chunk(w, use, c, i=None):
                wait_chunk(w, i)
                if c == 0:
                    claim_pair(use, i)
                for t in range(TT):
                    for k in range(4):
                        for n, (a, b) in enumerate(passes(ht, wsp)):
                            mm = pe.matmul(pair[use % 2][:, t, :], a[:, 4 * c + k, t * P:(t + 1) * P],
                                           b[:, w % WS, k * 512:(k + 1) * 512],
                                           start=(c == 0 and k == 0 and n == 0), stop=(c == 1 and k == 3 and n == 2))
                mm.then_inc(w_used, 1)

            def wide(w, use, i=None):
                for c in range(2):
                    wide_chunk(w + c, use, c, i)

            def feat(w, use, c):
                wait_chunk(w)
                if c == 0:
                    claim_pair(use)
                wv = [a[:, w % WS, :].rearrange("p (k n) -> p k n", k=KT) for a in wsp]
                for m in range(2):
                    for k in range(KT):
                        for n, (a, b) in enumerate(passes(wv, ht)):
                            mm = pe.matmul(pair[use % 2][:, c, m * S:(m + 1) * S], a[:, k, m * P:(m + 1) * P],
                                           b[:, k, :], start=(k == 0 and n == 0), stop=(k == KT - 1 and n == 2))
                mm.then_inc(w_used, 1)

            def outer(w, n, use, src, k0=0, during=None):
                for c in range(n):
                    wait_chunk(w + c)
                    for t in range(TT):
                        if c == 0:
                            claim_pair(use + t)
                        for half in range(2):
                            for k in range(2):
                                for m, (a, b) in enumerate(passes(src, wsp)):
                                    mm = pe.matmul(pair[(use + t) % 2][:, half, :],
                                                   a[:, k0 + 2 * c + k, t * P:(t + 1) * P],
                                                   b[:, (w + c) % WS, k * D + half * 512:k * D + half * 512 + 512],
                                                   start=(c == 0 and k == 0 and m == 0),
                                                   stop=(c == n - 1 and k == 1 and m == 2))
                        if c == n - 1 and t == 0:
                            mm.then_inc(half_ready, 1)
                    mm.then_inc(w_used, 1)
                    ada_after(w + c)

            def turn(k, srcs, bank_free=True):
                if bank_free:
                    claim(k)
                for n, a in enumerate(srcs):
                    mm = pe.transpose(tp[k % 2][:, n * P:(n + 1) * P], a, idn[:])
                mm.then_inc(tp_done, 1)

            def ada(a, i=None):
                at_least(pe, raw_done, AT_RAW["a", a] + 1, 6, i)
                for half in range(2):
                    n = 2 * a + half
                    dst = adap[:, n:n + 1] if i is None else adap[:, bass.ds(i * 4 + n, 1)]
                    for b in range(2):
                        mm = pe.matmul(dst, acc[:, a % 2, b, half * P:(half + 1) * P], ones[:, 0:1],
                                       start=(b == 0), stop=(b == 1))
                mm.then_inc(ada_used, 1)

            def ada_after(w):
                if w - 2 in ADA_STATIC:
                    ada(ADA_STATIC[w - 2])

            def tokens_to_features(name, n_done):
                for t in range(TT):
                    pe.wait_ge(xn_done, n_done + t)
                    for half in range(2):
                        turn(JOB[name] + 2 * t + half,
                             [xn[:, t, (4 * half + k) * P:(4 * half + k + 1) * P] for k in range(4)])

            def wait_split(name, n):
                pe.wait_ge(lo_done, SPLIT[JOB[name]] + n)

            def gate_rows(name, n_done):
                pe.wait_ge(dg_done, n_done)
                for half in range(2):
                    k = JOB[name] + half
                    claim(k)
                    pe.matmul(tp[k % 2][:], ones[:], dg[:, 4 * half:4 * half + 4, :].rearrange("p a b -> p (a b)"),
                              start=True, stop=True).then_inc(tp_done, 1)

            def ffn(name, jobs):
                w, use, k, a = W0[name], USE[name], JOB[jobs], ADA_AT[W0[name]]

                def hidden(j, k, i=None):
                    wait_evac(pe, use + j, i)
                    at_least(pe, lo_done, SPLIT[k] - 1, 2, i)
                    turn(k, [prod[:, j % 2, t, m * P:(m + 1) * P] for m in range(2) for t in range(TT)], False)

                wide(w, use)
                with pe.Fori(0, (GROUPS - 1) // 2) as i:
                    for v in range(2):
                        wide(w + 2 + 2 * v, use + 1 + v, i)
                        hidden(v, k + v, i)
                        ada(a + v, i)
                hidden(GROUPS - 1, k + GROUPS - 1)
                ada(a + GROUPS - 1)

            def levels(half, name):
                job = JOB["pa" if half == 0 else "pb"]
                for lv in range(8):
                    wide_chunk(W0[name] + lv, USE[name] + lv // 2, lv % 2)
                    ada_after(W0[name] + lv)
                    pe.wait_ge(hg_staged, 8 * half + lv + 1)
                    if lv == 0:
                        pe.wait_ge(hg_sk0, half + 1)
                    for s in range(2):
                        k = job + 2 * lv + s
                        claim(k)
                        for hd in range(HH):
                            mm = pe.matmul(tp[k % 2][:, hd * P:(hd + 1) * P], sk[:, hd, s * P:(s + 1) * P],
                                           sq[:, hd, s * P:(s + 1) * P], start=True, stop=True)
                        mm.then_inc(tp_done, 1)

            def across(half):
                pe.wait_ge(hg_qupd, 8 * half + 8)
                pe.wait_ge(hg_kupd, 7 * half + 7)
                job = JOB["offa" if half == 0 else "offb"]
                for s in range(2):
                    k = job + s
                    claim(k)
                    ks, qs = (kf, qf) if s == 0 else (kb, qb)
                    for hd in range(HH):
                        mm = pe.matmul(tp[k % 2][:, hd * P:(hd + 1) * P], ks[:, hd, s * P:(s + 1) * P],
                                       qs[:, hd, (1 - s) * P:(2 - s) * P], start=True, stop=True)
                    mm.then_inc(tp_done, 1)

            def values(half):
                pe.wait_ge(sem("p_copied"), 16 * half + 16)
                pe.wait_ge(sem("off_copied"), 2 * half + 2)
                for t in range(TT):
                    k = JOB["pva" if half == 0 else "pvb"] + t
                    claim(k)
                    for hd in range(HH):
                        for s in range(2):
                            mm = pe.matmul(tp[k % 2][:, hd * P:(hd + 1) * P], at[:, s, hd, t * P:(t + 1) * P],
                                           vv[:, s, (HH * half + hd) * P:(HH * half + hd + 1) * P],
                                           start=(s == 0), stop=(s == 1))
                    mm.then_inc(tp_done, 1)

            pe.wait_ge(small_in, 32)
            pe.wait_ge(consts, 1)
            tokens_to_features("norm0", 1)
            wait_split("norm0", 4)
            wide(W0["zu"], USE["zu"])
            wide(W0["zv"], USE["zv"])
            for name in ("qa", "fa", "ba"):
                for c in range(2):
                    feat(W0[name] + c, USE[name], c)
                    ada_after(W0[name] + c)
                if name == "fa":
                    pe.wait_ge(ln_done, 2)
                    pe.wait_ge(sgu_in, 48)
                    for t in range(TT):
                        k = JOB["sgu"] + t
                        claim(k)
                        for gr in range(8):
                            mm = pe.matmul(tp[k % 2][:, gr * 64:(gr + 1) * 64], sgw[:, gr, :],
                                           vg[:, t, gr * 64:(gr + 1) * 64], start=True, stop=True)
                        mm.then_inc(tp_done, 1)
            levels(0, "zi")
            for n, name in enumerate(("qb", "fb", "bb")):
                for c in range(2):
                    feat(W0[name] + c, USE[name], c)
                    ada_after(W0[name] + c)
                    if n == 0 and c == 0:
                        across(0)
                if n == 0:
                    wait_evac(pe, USE["zi"] + 1)
                    values(0)
            levels(1, "ga")
            across(1)
            values(1)
            pe.wait_ge(b_out, 2)
            for t in range(TT):
                pe.wait_ge(a_out, 3 + t)
                for half in range(2):
                    turn(JOB["ta"] + 2 * t + half, [zg[:, t, (4 * half + k) * P:(4 * half + k + 1) * P] for k in range(4)])
            for t in range(TT):
                turn(JOB["tb"] + t, [u[:, t, k * P:(k + 1) * P] for k in range(4)])
            wait_split("ta", 4)
            outer(W0["wa"], 4, USE["wa"], gt, 0)
            wait_split("tb", 2)
            outer(W0["wb"], 2, USE["wb"], gt, 8)
            for t in range(TT):
                pe.wait_ge(merged, t + 1)
                for half in range(2):
                    turn(JOB["tm"] + 2 * t + half, [ga[:, t, (4 * half + k) * P:(4 * half + k + 1) * P] for k in range(4)])
            wait_split("tm", 4)
            outer(W0["wout"], 4, USE["wout"], ht)
            tokens_to_features("norm1", 3)
            wait_split("norm1", 4)
            ffn("ffn0", "h0")
            wait_split("h0", GROUPS)
            outer(W0["down0"], GROUPS, USE["down0"], gt)
            gate_rows("rows0", 1)
            pe.wait_ge(pt_done, 1)
            outer(W0["ple"], 1, USE["ple"], pt)
            for t in range(TT):
                pe.wait_ge(x_ready, 3 + t)
                for half in range(2):
                    turn(JOB["tx"] + 2 * t + half, [xres[:, t, (4 * half + k) * P:(4 * half + k + 1) * P] for k in range(4)])
            wait_split("tx", 4)
            outer(W0["pleg"], 4, USE["pleg"], ht)
            tokens_to_features("norm2", 5)
            wait_split("norm2", 4)
            pe.wait_ge(cs_done, 1)
            for gr in range(4):
                for t in range(TT):
                    k = JOB["dft1"] + 2 * gr + t
                    claim(k)
                    for d in range(2):
                        for n, (a, b) in enumerate(passes(ht, cs)):
                            mm = pe.matmul(tp[k % 2][:], a[:, 2 * gr + d, t * P:(t + 1) * P], b[:, d, 0:512],
                                           start=(d == 0 and n == 0), stop=(d == 1 and n == 2))
                    mm.then_inc(tp_done, 1)
            for gr in range(4):
                wait_split("dft1", 2 * gr + 2)
                k = JOB["dft2"] + gr
                claim(k)
                for m in range(2):
                    for n, (t, part) in enumerate([(0, 0), (0, 1), (1, 0), (1, 1)]):
                        for o, (a, b) in enumerate(passes(tt, cs)):
                            mm = pe.matmul(tp[k % 2][:, m * S:(m + 1) * S],
                                           a[:, t, gr, part * S + m * P:part * S + (m + 1) * P],
                                           b[:, t, 2 * part * S:(2 * part + 1) * S],
                                           start=(n == 0 and o == 0), stop=(n == 3 and o == 2))
                mm.then_inc(tp_done, 1)
            wait_split("dft2", 4)
            outer(W0["fo"], 4, USE["fo"], ht)
            gate_rows("rows1", 2)
            tokens_to_features("norm3", 7)
            wait_split("norm3", 4)
            ffn("ffn1", "h1")
            wait_split("h1", GROUPS)
            outer(W0["down1"], GROUPS, USE["down1"], gt)
            gate_rows("rows2", 3)
            tokens_to_features("norm4", 9)
            wait_split("norm4", 4)
            for name in ("rq", "rk"):
                for c in range(4):
                    feat(W0[name] + c, USE[name] + c // 2, c % 2)
            for gr in range(4):
                wide(W0["rv"] + 2 * gr, USE["rv"] + gr)
                if gr == 1:
                    pe.wait_ge(rot_done, 4)
                    for hd in range(RH):
                        k = JOB["sc"] + hd
                        claim(k)
                        for s in range(2):
                            for d in range(2):
                                mm = pe.matmul(tp[k % 2][:, s * S:(s + 1) * S], kr[:, hd, d, s * P:(s + 1) * P],
                                               qr[:, hd, d, :], start=(d == 0), stop=(d == 1))
                        mm.then_inc(tp_done, 1)
            for gr in range(4):
                wide(W0["rg"] + 2 * gr, USE["rg"] + gr)
                if gr == 0:
                    wait_evac(pe, USE["rv"] + 3)
                    wait_evac(pe, USE["rv"] + 2)
                    pe.wait_ge(sem("sc_read"), RH)
                for t in range(TT):
                    k = JOB["av"] + 2 * gr + t
                    claim(k)
                    for s in range(2):
                        mm = pe.matmul(tp[k % 2][:], ar[:, gr, s, t * P:(t + 1) * P], vr[:, s, gr * RV:(gr + 1) * RV],
                                       start=(s == 0), stop=(s == 1))
                    mm.then_inc(tp_done, 1)
            pe.wait_ge(y_done, 4)
            for t in range(TT):
                for q in range(4):
                    turn(JOB["ty"] + 4 * t + q, [gg[:, t, (4 * q + k) * P:(4 * q + k + 1) * P] for k in range(4)])
            wait_split("ty", 8)
            outer(W0["ro"], 8, USE["ro"], gt)
            tokens_to_features("norm5", 11)
            wait_split("norm5", 4)
            ffn("ffn2", "h2")
            gate_rows("rows3", 4)
            wait_split("h2", GROUPS)
            outer(W0["down2"], GROUPS, USE["down2"], gt)
            tokens_to_features("norm6", 13)

        @block.scalar
        def _(act):
            sc = nc.scalar

            def split_hi(w, i=None):
                if w >= NW:
                    return
                n = AT_RAW["w", w]
                at_least(act, landed[n % RAW], 16 * (n // RAW + 1), 32, i)
                if w >= WS:
                    at_least(act, w_used, w - WS + 1, 4, i)
                sc.activation(w_hi[:, w % WS, :], raw[:, n % RAW, :], ACT.Copy).then_inc(hi_done, 1)

            def tick(w, i=None):
                split_hi(w + WS, i)

            def pair_ready(w, i=None):
                at_least(act, w_used, w + 1, 4, i)

            def evacuate(dst, use, func, scale=1.0, last=True):
                ins = sc.activation(dst, pair[use % 2][:], func, scale=scale)
                if last:
                    ins.then_inc(evac[use % 2], 1)

            def hi(k, dst, src=None, i=None):
                if src is None:
                    at_least(act, tp_done, k + 1, 2, i)
                    src = tp[k % 2][:]
                sc.activation(dst, src, ACT.Copy).then_inc(t_hi, 1)

            def norm_squares(q, t, n_x):
                act.wait_ge(x_ready, n_x) if n_x else act.wait_ge(x_in, 16)
                sc.activation(xn[:, t, :], xres[:, t, :], ACT.Square, accum_out=st[:, q, 0, 0:1]).then_inc(ss_done, 1)

            def norm_his(name, t):
                for half in range(2):
                    k = JOB[name] + 2 * t + half
                    n = RELEASE[k][1]
                    act.wait_ge(norm_read, n)
                    hi(k, ht[0][:, 4 * half:4 * half + 4, t * P:(t + 1) * P],
                       hb[:, k % 2, :].rearrange("p (k s) -> p k s", k=4))

            def post_squares(q, t, w, use, halves):
                if t == 0:
                    act.wait_ge(half_ready, halves)
                else:
                    pair_ready(w)
                sc.activation(xn[:, t, :].rearrange("p (a b) -> p a b", a=2), pair[(use + t) % 2][:], ACT.Square,
                              accum_out=st[:, q, 0, 0:1]).then_inc(ss_done, 1)

            def turned(name, dst, n, k0=0):
                for t in range(TT):
                    for q in range(n):
                        hi(JOB[name] + n * t + q, dst[0][:, k0 + 4 * q:k0 + 4 * q + 4, t * P:(t + 1) * P],
                           _four(tp[(JOB[name] + n * t + q) % 2][:], JOB[name] + n * t + q))

            def _four(a, k):
                act.wait_ge(tp_done, k + 1)
                return a.rearrange("p (k s) -> p k s", k=4)

            def stage_level(half, lv):
                if lv == 0:
                    if half:
                        act.wait_ge(tp_done, JOB["pa"] + 16)
                    act.wait_ge(evac[USE["qa" if half == 0 else "qb"] % 2], USE["qa" if half == 0 else "qb"] // 2 + 1)
                    sc.activation(sq[:], qf[:], ACT.Copy).then_inc(hg_staged, 1)
                    return
                h = 1 << (lv - 1)
                v = [a[:].rearrange("p a (b two h) -> p (a b) two h", two=2, h=h) for a in (qf, qb, kf, kb, sq, sk)]
                act.wait_ge(hg_qupd, 8 * half + lv)
                at_least(act, hg_kupd, 7 * half + lv - 1)
                act.wait_ge(tp_done, JOB["pa" if half == 0 else "pb"] + 2 * lv)
                sc.activation(v[4][:, :, 1, :], v[0][:, :, 1, :], ACT.Copy)
                sc.activation(v[4][:, :, 0, :], v[1][:, :, 0, :], ACT.Copy)
                sc.activation(v[5][:, :, 0, :], v[2][:, :, 0, :], ACT.Copy)
                sc.activation(v[5][:, :, 1, :], v[3][:, :, 1, :], ACT.Copy).then_inc(hg_staged, 1)

            def across(half):
                for s in range(2):
                    k = JOB["offa" if half == 0 else "offb"] + s
                    act.wait_ge(tp_done, k + 1)
                    if half:
                        act.wait_ge(tp_done, JOB["pva"] + 2)
                    sc.activation(at[:, s, :, (1 - s) * P:(2 - s) * P], tp[k % 2][:].rearrange("p (a b) -> p a b", a=HH),
                                  ACT.Copy).then_inc(sem("off_copied"), 1)

            def value_squares(half):
                for t in range(TT):
                    k = JOB["pva" if half == 0 else "pvb"] + t
                    act.wait_ge(tp_done, k + 1)
                    if half:
                        act.wait_ge(a_out, 2)
                    sc.activation(osq[:, t, :], tp[k % 2][:], ACT.Square).then_inc(pv_sq, 1)

            def ffn(name, jobs):
                w, use, k = W0[name], USE[name], JOB[jobs]

                def group(j, w, use, i=None):
                    at_least(act, w_used, w + 2, 4, i)
                    if i is not None:
                        at_least(act, tp_done, k + j - 1, 2, i)
                    for t in range(TT):
                        sc.activation(prod[:, j % 2, t, :], pair[use % 2][:, t, 0:256], ACT.Silu).then_inc(silu_done, 1)

                def hidden_hi(j, k, i=None):
                    at_least(act, tp_done, k + 1, 2, i)
                    dst = gt[0][:, 2 * j:2 * j + 2, :] if i is None else gt[0][:, bass.ds(i * 4 + 2 * j, 2), :]
                    sc.activation(dst, tp[k % 2][:].rearrange("p (a b) -> p a b", a=2), ACT.Copy).then_inc(t_hi, 1)

                group(0, w, use)
                tick(w)
                tick(w + 1)
                with act.Fori(0, (GROUPS - 1) // 2) as i:
                    for v in range(2):
                        group(v + 1, w + 2 + 2 * v, use + 1 + v, i)
                        hidden_hi(v, k + v, i)
                        tick(w + 2 + 2 * v, i)
                        tick(w + 3 + 2 * v, i)
                hidden_hi(GROUPS - 1, k + GROUPS - 1)

            def gate_rows(name, row):
                for half in range(2):
                    k = JOB[name] + half
                    act.wait_ge(tp_done, k + 1)
                    sc.activation(row[:, half * 512:(half + 1) * 512], tp[k % 2][:], ACT.Copy).then_inc(sem("row_copied"), 1)

            act.wait_ge(small_in, 32)
            act.wait_ge(lb_e, 1)
            sc.activation(lbt[:, 1, :], lbt[:, 0, :], ACT.Exp).then_inc(lb_e, 1)
            for t in range(TT):
                norm_squares(RQ["norm0"] + t, t, 0)
            sc.activation(ca[:], colv("c", 0, 8), ACT.Silu).then_inc(ca_done, 1)
            for t in range(TT):
                norm_his("norm0", t)
            for w in range(WS):
                split_hi(w)
            tick(0)
            pair_ready(1)
            evacuate(u[:], USE["zu"], ACT.Gelu)
            tick(1)
            tick(2)
            pair_ready(3)
            evacuate(vg[:], USE["zv"], ACT.Gelu)
            tick(3)

            def head_gates(half):
                q, f, b = ("qa", "fa", "ba") if half == 0 else ("qb", "fb", "bb")
                tick(W0[q])
                if half:
                    act.wait_ge(tp_done, JOB["offa"] + 2)
                    across(0)
                pair_ready(W0[q] + 1)
                as4 = "p a (b s) -> p (a b) s"
                sc.activation(qf[:], pair[USE[q] % 2][:].rearrange(as4, b=2), ACT.Silu).then_inc(evac[USE[q] % 2], 1)
                tick(W0[q] + 1)
                if half:
                    value_squares(0)
                stage_level(half, 0)
                tick(W0[f])
                pair_ready(W0[f] + 1)
                sc.activation(tf[:], pair[USE[f] % 2][:].rearrange(as4, b=2), ACT.Sigmoid)
                sc.activation(kf[:], pair[USE[f] % 2][:].rearrange(as4, b=2), ACT.Sigmoid, scale=-1.0).then_inc(evac[USE[f] % 2], 1)
                tick(W0[f] + 1)
                tick(W0[b])
                pair_ready(W0[b] + 1)
                sc.activation(tb[:], pair[USE[b] % 2][:].rearrange(as4, b=2), ACT.Sigmoid)
                sc.activation(kb[:], pair[USE[b] % 2][:].rearrange(as4, b=2), ACT.Sigmoid, scale=-1.0).then_inc(evac[USE[b] % 2], 1)
                tick(W0[b] + 1)

            def gated_chunks(half, name0, plan):
                for lv in range(8):
                    w = W0[name0] + lv
                    if lv % 2 == 1:
                        pair_ready(w)
                        dst, func = plan[lv // 2]
                        use = USE[name0] + lv // 2
                        evacuate(dst, use, func)
                    tick(w)
                    if lv < 7:
                        stage_level(half, lv + 1)

            head_gates(0)
            gated_chunks(0, "zi", [(vv[:, :, 0:512], ACT.Copy), (vv[:, :, 512:1024], ACT.Copy),
                                   (zg[:, :, 0:512], ACT.Silu), (zg[:, :, 512:1024], ACT.Silu)])
            head_gates(1)
            gated_chunks(1, "ga", [(ga[:, :, 0:512], ACT.Sigmoid), (ga[:, :, 512:1024], ACT.Sigmoid),
                                   (gb[:, :, 0:512], ACT.Sigmoid), (gb[:, :, 512:1024], ACT.Sigmoid)])
            across(1)
            value_squares(1)
            turned("ta", gt, 2)
            turned("tb", gt, 1, 8)
            for w in range(W0["wa"], W0["wout"]):
                tick(w)
            turned("tm", ht, 2)
            for w in range(W0["wout"], W0["wout"] + 3):
                tick(w)
            for t in range(TT):
                post_squares(RQ["mix"] + 2 * t, t, W0["wout"] + 3, USE["wout"], 3)
                norm_squares(RQ["mix"] + 2 * t + 1, t, 1 + t)
                norm_his("norm1", t)
            tick(W0["wout"] + 3)
            ffn("ffn0", "h0")
            for w in range(W0["down0"], W0["down0"] + GROUPS - 1):
                tick(w)
            act.wait_ge(p_in, 16)
            sc.activation(pt[0][:], praw[:], ACT.Copy).then_inc(pt_hi, 1)
            for t in range(TT):
                post_squares(RQ["ffn"] + t, t, W0["down0"] + GROUPS - 1, USE["down0"], 4)
            tick(W0["down0"] + GROUPS - 1)
            gate_rows("rows0", grow[0])
            for t in range(TT):
                if t == 0:
                    act.wait_ge(half_ready, 5)
                else:
                    pair_ready(W0["ple"])
                act.wait_ge(x_ready, 3 + t)
                sc.activation(xn[:, t, :].rearrange("p (a b) -> p a b", a=2), pair[(USE["ple"] + t) % 2][:],
                              ACT.Copy).then_inc(evac[(USE["ple"] + t) % 2], 1)
            turned("tx", ht, 2)
            tick(W0["ple"])
            act.wait_ge(dft_in, 16)
            act.wait_ge(w_used, W0["ple"] + 1)
            act.wait_ge(x_ready, 4)
            sc.activation(cs[0][:], csr[:], ACT.Copy).then_inc(cs_hi, 1)
            for w in range(W0["pleg"], W0["pleg"] + 3):
                tick(w)
            for t in range(TT):
                if t == 0:
                    act.wait_ge(half_ready, 6)
                else:
                    pair_ready(W0["pleg"] + 3)
                sc.activation(gsig[:, t, :].rearrange("p (a b) -> p a b", a=2), pair[(USE["pleg"] + t) % 2][:],
                              ACT.Sigmoid).then_inc(evac[(USE["pleg"] + t) % 2], 1)
            for t in range(TT):
                norm_squares(RQ["norm2"] + t, t, 5 + t)
                norm_his("norm2", t)
            tick(W0["pleg"] + 3)
            for gr in range(4):
                for t in range(TT):
                    hi(JOB["dft1"] + 2 * gr + t, tt[0][:, t, gr, :])
            for gr in range(4):
                k = JOB["dft2"] + gr
                act.wait_ge(tp_done, k + 1)
                hi(k, ht[0][:, 2 * gr:2 * gr + 2, :], tp[k % 2][:].rearrange("p (a b) -> p a b", a=2))
            for w in range(W0["fo"], W0["fo"] + 3):
                tick(w)
            gate_rows("rows1", grow[1])
            for t in range(TT):
                norm_squares(RQ["norm3"] + t, t, 7 + t)
                norm_his("norm3", t)
            tick(W0["fo"] + 3)
            ffn("ffn1", "h1")
            for w in range(W0["down1"], W0["down1"] + GROUPS - 1):
                tick(w)
            gate_rows("rows2", grow[0])
            for t in range(TT):
                norm_squares(RQ["norm4"] + t, t, 9 + t)
                norm_his("norm4", t)
            tick(W0["down1"] + GROUPS - 1)
            for w in range(W0["rq"], W0["rv"]):
                tick(w)
            for gr in range(4):
                tick(W0["rv"] + 2 * gr)
                pair_ready(W0["rv"] + 2 * gr + 1)
                evacuate(vr[:, :, gr * RV:(gr + 1) * RV], USE["rv"] + gr, ACT.Copy)
                tick(W0["rv"] + 2 * gr + 1)
            for gr in range(4):
                tick(W0["rg"] + 2 * gr)
                pair_ready(W0["rg"] + 2 * gr + 1)
                evacuate(gg[:, :, gr * RV:(gr + 1) * RV], USE["rg"] + gr, ACT.Silu)
                tick(W0["rg"] + 2 * gr + 1)
            turned("ty", gt, 4)
            for w in range(W0["ro"], W0["ro"] + 7):
                tick(w)
            for t in range(TT):
                norm_squares(RQ["norm5"] + t, t, 11 + t)
                norm_his("norm5", t)
            tick(W0["ro"] + 7)
            ffn("ffn2", "h2")
            gate_rows("rows3", grow[1])
            for w in range(W0["down2"], W0["down2"] + GROUPS - 1):
                tick(w)
            for t in range(TT):
                norm_squares(RQ["norm6"] + t, t, 13 + t)

        @block.vector
        def _(dve):
            v = nc.vector
            steps = [0]

            def link(ins):
                steps[0] += 1
                ins.then_inc(step, 1)
                dve.wait_ge(step, steps[0])

            def as_f32(a):
                return a.bitcast(F32)

            whi32 = as_f32(w_hi[:])
            ht32, gt32, tt32 = as_f32(ht[0][:]), as_f32(gt[0][:]), as_f32(tt[0][:])

            def split_lo(w, i=None):
                if w >= NW:
                    return
                n = AT_RAW["w", w]
                at_least(dve, hi_done, w + 1, 4, i)
                v.tensor_tensor(w_lo[:, w % WS, :], raw[:, n % RAW, :], whi32[:, w % WS, :],
                                ALU.subtract).then_inc(raw_done, 1)

            def ada(a, i=None):
                n = AT_RAW["a", a]
                at_least(dve, landed[n % RAW], 16 * (n // RAW + 1), 32, i)
                if a >= 2:
                    at_least(dve, ada_used, a - 1, 2, i)
                for k in range(KT):
                    src, dst = raw[:, n % RAW, k * 256:(k + 1) * 256], acc[:, a % 2, k % 2, :]
                    if k < 2:
                        ins = v.tensor_scalar(dst, src, ca[:, k:k + 1], None, ALU.mult)
                    else:
                        at_least(dve, ada_step, 7 * a + k - 1, 14, i)
                        ins = v.scalar_tensor_tensor(out=dst, in0=src, scalar=ca[:, k:k + 1], in1=dst,
                                                     op0=ALU.mult, op1=ALU.add)
                    ins.then_inc(raw_done if k == KT - 1 else ada_step, 1)

            def tick(w, i=None):
                split_lo(w + WS, i)
                if w in ADA_AT:
                    ada(ADA_AT[w], i)

            def ready(use, t, w, halves):
                if t == 0:
                    dve.wait_ge(half_ready, halves)
                else:
                    dve.wait_ge(w_used, w + 1)

            def mean_square(q):
                dve.wait_ge(ss_done, SS[q])
                v.tensor_scalar(st[:, q, 1, 0:1], st[:, q, 0, 0:1], 1.0 / D, EPS, ALU.mult, ALU.add).then_inc(ms_done, 1)
                dve.wait_ge(rstd_done, q + 1)

            def two(a):
                return a.rearrange("p (a b) -> p a b", a=2)

            def norm(q, t):
                mean_square(q)
                v.tensor_scalar(xn[:, t, :], xres[:, t, :], st[:, q, 2, 0:1], None, ALU.mult).then_inc(xn_done, 1)

            def scaled(name, t, scale, shift, dst):
                for half in range(2):
                    k = JOB[name] + 2 * t + half
                    dve.wait_ge(tp_done, k + 1)
                    if k in SPLIT:
                        at_least(dve, lo_done, SPLIT[k] - 1)
                    for m in range(4):
                        f = 4 * half + m
                        ins = v.tensor_scalar(dst(k, half)[:, m * P:(m + 1) * P], tp[k % 2][:, m * P:(m + 1) * P],
                                              scale[:, f:f + 1], None if shift is None else shift[:, f:f + 1],
                                              ALU.mult, *(() if shift is None else (ALU.add,)))
                    ins.then_inc(sem(RELEASE[k][0]), 1)

            def norm_jobs(name, t, scale, shift=None):
                scaled(name, t, scale, shift, lambda k, half: hb[:, k % 2, :])
                for half in range(2):
                    k = JOB[name] + 2 * t + half
                    dve.wait_ge(norm_read, RELEASE[k][1])
                    dve.wait_ge(t_hi, SPLIT[k] + 1)
                    where = (slice(None), slice(4 * half, 4 * half + 4), slice(t * P, (t + 1) * P))
                    v.tensor_tensor(ht[1][where], hb[:, k % 2, :].rearrange("p (k s) -> p k s", k=4), ht32[where],
                                    ALU.subtract).then_inc(lo_done, 1)

            def lo(k, dst, hi32, src, i=None):
                at_least(dve, t_hi, SPLIT[k] + 1, 2, i)
                v.tensor_tensor(dst, src, hi32, ALU.subtract).then_inc(lo_done, 1)

            def turned(name, dst, hi32, n, k0=0):
                for t in range(TT):
                    for q in range(n):
                        k = JOB[name] + n * t + q
                        where = (slice(None), slice(k0 + 4 * q, k0 + 4 * q + 4), slice(t * P, (t + 1) * P))
                        lo(k, dst[1][where], hi32[where], tp[k % 2][:].rearrange("p (k s) -> p k s", k=4))

            def post(q, t, use, row):
                mean_square(q)
                p = (use + t) % 2
                v.scalar_tensor_tensor(out=two(xn[:, t, :]), in0=pair[p][:], scalar=st[:, q, 2, 0:1], in1=two(row),
                                       op0=ALU.mult, op1=ALU.mult).then_inc(evac[p], 1)
                wait_evac(dve, use + t)
                v.tensor_tensor(xres[:, t, :], xres[:, t, :], xn[:, t, :], ALU.add).then_inc(x_ready, 1)

            def gated_post(t, use, w, halves, row, rows):
                ready(use, t, w, halves)
                dve.wait_ge(sem("row_copied"), rows)
                p = (use + t) % 2
                v.tensor_tensor(two(xn[:, t, :]), pair[p][:], two(row), ALU.mult).then_inc(evac[p], 1)
                wait_evac(dve, use + t)
                v.tensor_tensor(xres[:, t, :], xres[:, t, :], xn[:, t, :], ALU.add).then_inc(x_ready, 1)

            def mod_columns(a, b, used):
                dve.wait_ge(ada_used, used)
                link(v.tensor_tensor(mod[:, a:b], adap[:, a:b], colv("b_ada", a, b - a), ALU.add))

            def mod_scale(n, at_col, gain):
                link(v.scalar_tensor_tensor(out=moda[:, n, :], in0=mod[:, at_col:at_col + 8], scalar=1.0, in1=gain,
                                            op0=ALU.add, op1=ALU.mult))

            def gate_diagonals(at_col, read=None):
                if read is not None:
                    dve.wait_ge(tp_done, read)
                for m in range(KT):
                    ins = v.tensor_scalar(dg[:, m, :], idn[:], mod[:, at_col + m:at_col + m + 1], None, ALU.mult)
                ins.then_inc(dg_done, 1)

            def ffn(name, jobs):
                w, use, k, n0 = W0[name], USE[name], JOB[jobs], GROUPS * int(name[-1])

                def group(j, use, i=None):
                    for t in range(TT):
                        at_least(dve, silu_done, 2 * (n0 + j) + t + 1, 4, i)
                        ins = v.tensor_tensor(prod[:, j % 2, t, :], prod[:, j % 2, t, :], pair[use % 2][:, t, 256:512], ALU.mult)
                    ins.then_inc(evac[use % 2], 1)

                def hidden_lo(j, k, i=None):
                    where = slice(2 * j, 2 * j + 2) if i is None else bass.ds(i * 4 + 2 * j, 2)
                    lo(k, gt[1][:, where, :], gt32[:, where, :], tp[k % 2][:].rearrange("p (a b) -> p a b", a=2), i)

                group(0, use)
                tick(w)
                tick(w + 1)
                with dve.Fori(0, (GROUPS - 1) // 2) as i:
                    for n in range(2):
                        group(n + 1, use + 1 + n, i)
                        hidden_lo(n, k + n, i)
                        tick(w + 2 + 2 * n, i)
                        tick(w + 3 + 2 * n, i)
                hidden_lo(GROUPS - 1, k + GROUPS - 1)

            def head_gates(half):
                q, f, b = ("qa", "fa", "ba") if half == 0 else ("qb", "fb", "bb")
                for name, d, fx, kx in ((f, 0, tf, kf), (b, 1, tb, kb)):
                    tick(W0[name]) if name == f else None
                    wait_evac(dve, USE[name])
                    for hd in range(HH):
                        n = 8 * d + HH * half + hd
                        v.tensor_scalar(kx[:, hd, :], kx[:, hd, :], lbt[:, 0, n:n + 1], None, ALU.mult)
                        ins = v.tensor_scalar(fx[:, hd, :], fx[:, hd, :], lbt[:, 0, n:n + 1], lbt[:, 4, n:n + 1],
                                              ALU.mult, ALU.add)
                    link(ins)
                    link(v.tensor_scalar(fx[:], fx[:], TINY, None, ALU.max))
                    if name == f:
                        tick(W0[f] + 1)
                        tick(W0[b])
                if half:
                    dve.wait_ge(tp_done, JOB["pa"] + 16)
                v.tensor_tensor(sk[:], kf[:], kb[:], ALU.add).then_inc(hg_sk0, 1)
                dve.wait_ge(hg_staged, 8 * half + 1)
                link(v.tensor_tensor(qb[:], qf[:], tb[:], ALU.mult))
                v.tensor_tensor(qf[:], qf[:], tf[:], ALU.mult).then_inc(hg_qupd, 1)
                tick(W0[b] + 1)

            def query_updates(half, lv):
                h = 1 << (lv - 1)
                nb = HH * S // (2 * h)
                qa, qc, fa, fc = [a[:].rearrange("p a (b two h) -> p (a b) two h", two=2, h=h) for a in (qf, qb, tf, tb)]
                dve.wait_ge(hg_qupd, 8 * half + lv)
                dve.wait_ge(hg_staged, 8 * half + lv + 1)
                if lv > 1:
                    dve.wait_ge(hg_tot, 6 * half + lv - 1)
                v.tensor_tensor(qa[:, :, 1, :], qa[:, :, 1, :], fa[:, :, 0, 0:1].to_broadcast([P, nb, h]), ALU.mult)
                v.tensor_tensor(qc[:, :, 0, :], qc[:, :, 0, :], fc[:, :, 1, 0:1].to_broadcast([P, nb, h]),
                                ALU.mult).then_inc(hg_qupd, 1)
                if lv < 7:
                    dve.wait_ge(hg_kupd, 7 * half + lv)
                    dve.wait_ge(hg_qupd, 8 * half + lv + 1)
                    v.tensor_tensor(fa[:, :, 0, 0:1], fa[:, :, 0, 0:1], fa[:, :, 1, 0:1], ALU.mult)
                    v.tensor_tensor(fc[:, :, 0, 0:1], fc[:, :, 0, 0:1], fc[:, :, 1, 0:1], ALU.mult).then_inc(hg_tot, 1)

            def take_scores(half, lv):
                for s in range(2):
                    k = JOB["pa" if half == 0 else "pb"] + 2 * lv + s
                    dve.wait_ge(tp_done, k + 1)
                    n = RELEASE[k][1]
                    if n > 2:
                        dve.wait_ge(sem("p_copied"), n - 2)
                    v.copy_predicated(at[:, s, :, s * P:(s + 1) * P], msk[:, lv:lv + 1, :].to_broadcast([P, HH, P]),
                                      tp[k % 2][:].rearrange("p (a b) -> p a b", a=HH)).then_inc(sem("p_copied"), 1)

            def head_outputs(half):
                for t in range(TT):
                    k, q = JOB["pva" if half == 0 else "pvb"] + t, RQ["pva" if half == 0 else "pvb"] + t
                    dve.wait_ge(pv_sq, 2 * half + t + 1)
                    link(v.tensor_reduce(st[:, q, 0, :], osq[:, t, :].rearrange("p (a b) -> p a b", a=HH), AX.X, ALU.add))
                    v.tensor_scalar(st[:, q, 1, :], st[:, q, 0, :], 1.0 / P, EPS, ALU.mult, ALU.add).then_inc(ms_done, 1)
                    dve.wait_ge(rstd_done, q + 1)
                    at_least(dve, a_out, 2 * half + t)
                    v.tensor_tensor(on[:, t, :].rearrange("p (a b) -> p a b", a=HH),
                                    tp[k % 2][:].rearrange("p (a b) -> p a b", a=HH),
                                    st[:, q, 2, :].unsqueeze(2).to_broadcast([P, HH, P]), ALU.mult).then_inc(sem("pv_read"), 1)
                    dve.wait_ge(sem("pv_read"), 2 * half + t + 1)
                    link(v.tensor_tensor(on[:, t, :], on[:, t, :], hgrow[:, half, :], ALU.mult))
                    z = zg[:, t, half * 512:(half + 1) * 512]
                    v.tensor_tensor(z, z, on[:, t, :], ALU.mult).then_inc(a_out, 1)

            dve.wait_ge(small_in, 32)
            gamma = colv("gamma", 0, 16)
            v.tensor_tensor(lbt[:, 0, :], gamma, gamma, ALU.subtract).then_inc(lb_e, 1)
            dve.wait_ge(lb_e, 2)
            link(v.reciprocal(lbt[:, 2, :], lbt[:, 1, :]))
            link(v.tensor_tensor(lbt[:, 3, :], lbt[:, 1, :], lbt[:, 2, :], ALU.mult))
            link(v.tensor_tensor(lbt[:, 4, :], lbt[:, 3, :], lbt[:, 3, :], ALU.subtract))
            link(v.tensor_scalar(lbt[:, 0, :], lbt[:, 4, :], -1.0, 1.0, ALU.mult, ALU.add))
            for t in range(TT):
                norm(RQ["norm0"] + t, t)
            for t in range(TT):
                norm_jobs("norm0", t, colv("mix_pre", 0, 8))
            dve.wait_ge(ca_done, 1)
            for w in range(WS):
                split_lo(w)
            for w in range(3):
                tick(w)
            wait_evac(dve, USE["zv"])
            dve.wait_ge(sgu_in, 48)
            for t in range(TT):
                link(v.bn_stats(bn[:, t, :], vg[:, t, :]))
                link(v.bn_aggr(mv[:, t, :], bn[:, t, :]))
                q = RQ["ln"] + t
                v.tensor_scalar(st[:, q, 1, 0:1], mv[:, t, 1:2], EPS, None, ALU.add).then_inc(ms_done, 1)
                dve.wait_ge(rstd_done, q + 1)
                link(v.tensor_scalar(vg[:, t, :], vg[:, t, :], mv[:, t, 0:1], st[:, q, 2, 0:1], ALU.subtract, ALU.mult))
                link(v.tensor_tensor(vg[:, t, :], vg[:, t, :], lnrow[:, 0, :], ALU.mult))
                v.tensor_tensor(vg[:, t, :], vg[:, t, :], lnrow[:, 1, :], ALU.add).then_inc(ln_done, 1)
            for w in range(3, 6):
                tick(w)

            def gate_positions():
                for t in range(TT):
                    k = JOB["sgu"] + t
                    dve.wait_ge(tp_done, k + 1)
                    v.tensor_tensor(vg[:, t, :].rearrange("p (a b) -> p a b", a=8), tp[k % 2][:].rearrange("p (a b) -> p a b", a=8),
                                    colv("sg_b", 0, 8).unsqueeze(2).to_broadcast([P, 8, 64]), ALU.add).then_inc(sem("sgu_read"), 1)
                    dve.wait_ge(sem("sgu_read"), t + 1)
                    v.tensor_tensor(u[:, t, :], u[:, t, :], vg[:, t, :], ALU.mult).then_inc(b_out, 1)

            head_gates(0)
            gate_positions()
            dve.wait_ge(hg_in, 32)
            link(v.tensor_copy(msk[:], mskf[:]))
            for lv in range(8):
                tick(W0["zi"] + lv)
                take_scores(0, lv)
                if lv < 7:
                    query_updates(0, lv + 1)
            tick(W0["qb"])
            tick(W0["qb"] + 1)
            head_outputs(0)
            head_gates(1)
            for lv in range(8):
                if lv < 7:
                    tick(W0["ga"] + lv)
                take_scores(1, lv)
                if lv < 7:
                    query_updates(1, lv + 1)
            head_outputs(1)
            turned("ta", gt, gt32, 2)
            turned("tb", gt, gt32, 1, 8)
            tick(W0["ga"] + 7)
            for w in range(W0["wa"], W0["wa"] + 3):
                tick(w)
            for t in range(TT):
                ready(USE["wa"], t, W0["wa"] + 3, 1)
                v.tensor_tensor(two(ga[:, t, :]), two(ga[:, t, :]), pair[(USE["wa"] + t) % 2][:],
                                ALU.mult).then_inc(evac[(USE["wa"] + t) % 2], 1)
            tick(W0["wa"] + 3)
            tick(W0["wb"])
            for t in range(TT):
                ready(USE["wb"], t, W0["wb"] + 1, 2)
                v.tensor_tensor(two(gb[:, t, :]), two(gb[:, t, :]), pair[(USE["wb"] + t) % 2][:],
                                ALU.mult).then_inc(evac[(USE["wb"] + t) % 2], 1)
                wait_evac(dve, USE["wb"] + t)
                v.tensor_tensor(ga[:, t, :], ga[:, t, :], gb[:, t, :], ALU.add).then_inc(merged, 1)
            turned("tm", ht, ht32, 2)
            tick(W0["wb"] + 1)
            for w in range(W0["wout"], W0["wout"] + 3):
                tick(w)
            dve.wait_ge(x_again, 16)
            dve.wait_ge(prow_in, 16)
            for t in range(TT):
                post(RQ["mix"] + 2 * t, t, USE["wout"], prow[:, 0, :])
                norm(RQ["mix"] + 2 * t + 1, t)
                norm_jobs("norm1", t, colv("ffn_pre", 0, 8))
            tick(W0["wout"] + 3)
            ffn("ffn0", "h0")
            for w in range(W0["down0"], W0["down0"] + GROUPS - 1):
                tick(w)
            dve.wait_ge(pt_hi, 1)
            v.tensor_tensor(pt[1][:], praw[:], as_f32(pt[0][:]), ALU.subtract).then_inc(pt_done, 1)
            mod_columns(0, 48, 27)
            mod_scale(0, 8, colv("mix_g", 0, 8))
            mod_scale(1, 32, colv("ffn_g", 0, 8))
            gate_diagonals(16)
            for t in range(TT):
                post(RQ["ffn"] + t, t, USE["down0"], prow[:, 1, :])
            tick(W0["down0"] + GROUPS - 1)
            turned("tx", ht, ht32, 2)
            tick(W0["ple"])
            dve.wait_ge(cs_hi, 1)
            v.tensor_tensor(cs[1][:], csr[:], as_f32(cs[0][:]), ALU.subtract).then_inc(cs_done, 1)
            for w in range(W0["pleg"], W0["pleg"] + 3):
                tick(w)
            for t in range(TT):
                wait_evac(dve, USE["pleg"] + t)
                link(v.tensor_tensor(xn[:, t, :], xn[:, t, :], gsig[:, t, :], ALU.mult))
                v.tensor_tensor(xres[:, t, :], xres[:, t, :], xn[:, t, :], ALU.add).then_inc(x_ready, 1)
                norm(RQ["norm2"] + t, t)
                norm_jobs("norm2", t, moda[:, 0, :], mod[:, 0:8])
            tick(W0["pleg"] + 3)
            for gr in range(4):
                for t in range(TT):
                    k = JOB["dft1"] + 2 * gr + t
                    lo(k, tt[1][:, t, gr, :], tt32[:, t, gr, :], tp[k % 2][:])
            for gr in range(4):
                k = JOB["dft2"] + gr
                lo(k, ht[1][:, 2 * gr:2 * gr + 2, :], ht32[:, 2 * gr:2 * gr + 2, :], tp[k % 2][:].rearrange("p (a b) -> p a b", a=2))
            for w in range(W0["fo"], W0["fo"] + 3):
                tick(w)
            gate_diagonals(40, JOB["rows0"] + 2)
            for t in range(TT):
                gated_post(t, USE["fo"], W0["fo"] + 3, 7, grow[0][:], 2)
                norm(RQ["norm3"] + t, t)
                norm_jobs("norm3", t, moda[:, 1, :], mod[:, 24:32])
            tick(W0["fo"] + 3)
            ffn("ffn1", "h1")
            for w in range(W0["down1"], W0["down1"] + GROUPS - 1):
                tick(w)
            mod_columns(48, 88, 45)
            mod_scale(2, 56, colv("mix_g", 8, 8))
            mod_scale(3, 80, colv("ffn_g", 8, 8))
            gate_diagonals(64, JOB["rows1"] + 2)
            for t in range(TT):
                gated_post(t, USE["down1"], W0["down1"] + GROUPS - 1, 8, grow[1][:], 4)
                norm(RQ["norm4"] + t, t)
                norm_jobs("norm4", t, moda[:, 2, :], mod[:, 48:56])
            tick(W0["down1"] + GROUPS - 1)
            dve.wait_ge(rot_in, 16)
            for n, name in enumerate(("rq", "rk")):
                dst = qr if n == 0 else kr
                for m in range(2):
                    tick(W0[name] + 2 * m)
                    use = USE[name] + m
                    dve.wait_ge(w_used, W0[name] + 2 * m + 2)
                    src = pair[use % 2][:].rearrange("p a (x s) -> p (a x) s", x=2)
                    if n or m:
                        dve.wait_ge(rot_done, 2 * n + m)
                    v.tensor_tensor(rab[:, 0, :, :], src, rt[:, 0:1, :].to_broadcast([P, 4, S]), ALU.mult)
                    v.tensor_tensor(rab[:, 1, :, :], src, rt[:, 1:2, :].to_broadcast([P, 4, S]), ALU.mult).then_inc(evac[use % 2], 1)
                    wait_evac(dve, use)
                    c, d = [rab[:, y, :, :].rearrange("p (a x) s -> p a x s", x=2) for y in range(2)]
                    v.tensor_tensor(dst[:, 2 * m:2 * m + 2, 0, :], c[:, :, 0, :], d[:, :, 1, :], ALU.subtract)
                    v.tensor_tensor(dst[:, 2 * m:2 * m + 2, 1, :], d[:, :, 0, :], c[:, :, 1, :], ALU.add).then_inc(rot_done, 1)
                    tick(W0[name] + 2 * m + 1)
            for gr in range(4):
                tick(W0["rv"] + 2 * gr)
                tick(W0["rv"] + 2 * gr + 1)
                if gr == 1:
                    dve.wait_ge(decay_in, 16)
                    for hd in range(RH):
                        k = JOB["sc"] + hd
                        dve.wait_ge(tp_done, k + 1)
                        v.tensor_tensor(ar[:, hd, :, :], tp[k % 2][:].rearrange("p (a b) -> p a b", a=2), dt[:, hd, :, :],
                                        ALU.mult).then_inc(sem("sc_read"), 1)
            for gr in range(4):
                tick(W0["rg"] + 2 * gr)
                tick(W0["rg"] + 2 * gr + 1)
                for t in range(TT):
                    k, q = JOB["av"] + 2 * gr + t, RQ["av"] + 2 * gr + t
                    dve.wait_ge(tp_done, k + 1)
                    link(v.bn_stats(bn[:, t, :], tp[k % 2][:]))
                    link(v.bn_aggr(mv[:, t, :], bn[:, t, :]))
                    v.tensor_scalar(st[:, q, 1, 0:1], mv[:, t, 1:2], EPS, None, ALU.add).then_inc(ms_done, 1)
                    dve.wait_ge(rstd_done, q + 1)
                    v.tensor_scalar(yr[:, t, gr * RV:(gr + 1) * RV], tp[k % 2][:], mv[:, t, 0:1], st[:, q, 2, 0:1],
                                    ALU.subtract, ALU.mult).then_inc(sem("av_read"), 1)
                dve.wait_ge(sem("av_read"), 2 * gr + 2)
                wait_evac(dve, USE["rg"] + gr)
                z = gg[:, :, gr * RV:(gr + 1) * RV]
                v.tensor_tensor(z, z, yr[:, :, gr * RV:(gr + 1) * RV], ALU.mult).then_inc(y_done, 1)
            turned("ty", gt, gt32, 4)
            for w in range(W0["ro"], W0["ro"] + 7):
                tick(w)
            for t in range(TT):
                gated_post(t, USE["ro"], W0["ro"] + 7, 9, grow[0][:], 6)
                norm(RQ["norm5"] + t, t)
                norm_jobs("norm5", t, moda[:, 3, :], mod[:, 72:80])
            tick(W0["ro"] + 7)
            ffn("ffn2", "h2")
            mod_columns(88, 112, NADA)
            mod_scale(4, 104, colv("fin_g", 0, 8))
            gate_diagonals(88)
            for w in range(W0["down2"], W0["down2"] + GROUPS - 1):
                tick(w)
            for t in range(TT):
                gated_post(t, USE["down2"], W0["down2"] + GROUPS - 1, 10, grow[1][:], 8)
                norm(RQ["norm6"] + t, t)
                scaled("norm6", t, moda[:, 4, :], mod[:, 96:104], lambda k, half: outb[:, k - JOB["norm6"], :])


def kernel(**inputs):
    import numpy as np
    import concourse.bacc as bacc
    from concourse.bass_utils import run_bass_kernel_spmd

    def get(name):
        return np.ascontiguousarray(inputs[name])

    def deep(w, n):
        k, cols = w.shape
        kt = 2048 // n
        a = w.reshape(k // (kt * P), kt, P, cols // n, n)
        return a.transpose(3, 0, 2, 1, 4).reshape(-1, P, 2048)

    def gate_up(wg, wu):
        a = np.stack([wg.reshape(D, GROUPS, 256), wu.reshape(D, GROUPS, 256)], axis=2)
        return deep(a.reshape(D, GROUPS * 512), 512)

    def outer(w):
        return w.reshape(-1, 2, P, D).transpose(0, 2, 1, 3).reshape(-1, P, 2048)

    w_in = get("w_in")[0]
    z = {}
    off = 0
    for name, n in (("q", 1024), ("f", 1024), ("b", 1024), ("zi", 1024), ("zg", 1024), ("zu", 512), ("zv", 512),
                    ("ga", 1024), ("gb", 1024)):
        z[name] = w_in[:, off:off + n]
        off += n
    ri, fi, fo = get("w_ret_in_2")[0], get("w_ffn_in_2"), get("w_ffn_out_2")
    parts = {
        "zu": deep(z["zu"], 512), "zv": deep(z["zv"], 512),
        "zi": deep(z["zi"], 512), "zg": deep(z["zg"], 512), "ga": deep(z["ga"], 512), "gb": deep(z["gb"], 512),
        "wa": outer(get("w_a")[0]), "wb": outer(get("w_b")[0]), "wout": outer(get("w_out")[0]),
        "ffn0": gate_up(get("w_gate")[0], get("w_up")[0]), "down0": outer(get("w_down")[0]),
        "ple": outer(get("w_ple")[0]), "pleg": outer(get("w_ple_gate")[0]), "fo": outer(get("w_fourier_out_2")[0]),
        "ffn1": gate_up(fi[0][:, :FF], fi[0][:, FF:]), "down1": outer(fo[0]),
        "rq": deep(ri[:, 0:1024], 256), "rk": deep(ri[:, 1024:2048], 256),
        "rv": deep(ri[:, 2048:4096], 512), "rg": deep(ri[:, 4096:6144], 512), "ro": outer(get("w_ret_out_2")[0]),
        "ffn2": gate_up(fi[1][:, :FF], fi[1][:, FF:]), "down2": outer(fo[1]),
    }
    for half, h in enumerate("ab"):
        for name in "qfb":
            parts[name + h] = deep(z[name][:, 512 * half:512 * half + 512], 256)
    weights = [c for name, n in STAGES for c in parts[name]]
    wada = get("w_ada_2")
    adas = [c for w in (wada[0], wada[1], get("w_ada_final_2")) for c in deep(w, 256)]
    stream = np.stack([(weights if kind == "w" else adas)[n] for kind, n in ORDER])

    def columns(a):
        return a.reshape(-1, P).T

    table = np.concatenate([columns(get(n).reshape(-1)) for n in (
        "norm_mix_pre", "norm_ffn_pre", "norm_mix_g_2", "norm_ffn_g_2", "final_norm_g_2", "c_2", "lb_gamma_fwd",
        "lb_gamma_bwd", "sg_b", "b_ada_2", "b_ada_final_2")], axis=1)
    rows = np.stack([np.concatenate([get("sg_ln_g")[0], get("sg_ln_b")[0]]), get("hg_norm")[0],
                     get("norm_mix_post")[0], get("norm_ffn_post")[0]])

    f32 = np.float32
    n = np.arange(P)
    masks = [n[:, None] == n[None, :]]
    for lv in range(7):
        h = 1 << lv
        masks.append((n[:, None] // (2 * h) == n[None, :] // (2 * h)) & (n[:, None] // h != n[None, :] // h))
    masks = np.stack(masks, axis=1).astype(np.float32)
    m = np.arange(S)
    ang = 2.0 * np.pi * ((m[:, None] * m[None, :]) % S) / S
    dft = np.concatenate([np.cos(ang), np.sin(ang), -np.sin(ang)], axis=1) / 16.0
    dft = dft.astype(f32).reshape(2, P, 768).transpose(1, 0, 2)
    freq = (f32(10000.0) ** (-np.arange(P, dtype=f32) / f32(P))).astype(f32)
    rang = (freq[:, None] * m[None, :].astype(f32)).astype(f32).astype(np.float64)
    rot = np.stack([np.cos(rang), np.sin(rang)], axis=1).astype(f32)
    lg = np.log1p(-np.exp2(-5.0 - np.arange(RH)))
    d = m[None, :] - m[:, None]
    decay = np.stack([np.where(d >= 0, np.exp(np.maximum(d, 0) * lg[h]), np.exp(np.maximum(-d, 0) * lg[RH - 1 - h]))
                      for h in range(RH)]) / 16.0
    decay = decay.astype(f32).reshape(RH, 2, P, S).transpose(2, 0, 1, 3)

    arrays = {
        "stream": stream,
        "x": get("x")[0].reshape(TT, P, D).transpose(1, 0, 2),
        "pT": get("p")[0, 0].T.reshape(2, P, S).transpose(1, 0, 2),
        "cols": table, "rows": rows,
        "sg_wT": get("sg_w")[0].transpose(2, 0, 1),
        "masks": masks, "ident": np.eye(P, dtype=f32), "dft": dft, "rot": rot, "decay": decay,
    }
    nc = bacc.Bacc("TRN2", target_bir_lowering=False, num_devices=1)
    args = []
    for name, a in arrays.items():
        arrays[name] = a = np.ascontiguousarray(a)
        args.append(nc.dram_tensor(name, a.shape, mybir.dt.from_np(a.dtype), kind="ExternalInput").ap())
    args.append(nc.dram_tensor("outT", (KT, P, S), F32, kind="ExternalOutput").ap())
    program(nc, *args)
    r = run_bass_kernel_spmd(nc, [arrays], core_ids=[0])
    return np.ascontiguousarray(r.results[0]["outT"].reshape(D, S).T).reshape(1, S, D)
```

```python
from contextlib import ExitStack

import concourse.bass as bass
from concourse import mybir

F32 = mybir.dt.float32
F32R = mybir.dt.float32r
U8 = mybir.dt.uint8
ALU = mybir.AluOpType
ACT = mybir.ActivationFunctionType
AX = mybir.AxisListType

P = 128
S = 256
TT = S // P
D = 1024
KT = D // P
FF = 2816
FT = FF // P
HEADS = 8
HH = HEADS // 2
RH = 4
RV = 512
EPS = 1e-6
TINY = 1.1754943508222875e-38

RAW = 3
WS = 4
GROUPS = FT // 2

STAGES = [("zu", 2), ("zv", 2), ("qa", 2), ("fa", 2), ("ba", 2), ("zi", 4), ("zg", 4),
          ("qb", 2), ("fb", 2), ("bb", 2), ("ga", 4), ("gb", 4), ("wb", 2), ("wa", 4),
          ("wout", 4), ("ffn0", 2 * GROUPS), ("down0", GROUPS), ("ple", 1), ("pleg", 4),
          ("fo", 4), ("ffn1", 2 * GROUPS), ("down1", GROUPS), ("rva", 4), ("rq", 4), ("rk", 4), ("rvb", 4),
          ("rg", 8), ("ro", 8), ("ffn2", 2 * GROUPS), ("down2", GROUPS)]
W0 = {}
NW = 0
for _name, _n in STAGES:
    W0[_name] = NW
    NW += _n

PEELED = 3

NADA = 56


def ffn_adas(name):
    return [W0[name] + 2 * j - 1 for j in range(PEELED, GROUPS)]


ADA_TICKS = list(range(5, 10)) + [19, 21, 23, 33, 34, 35, 36]
ADA_TICKS += ffn_adas("ffn0") + [W0["down0"] + j for j in (0, 2, 3, 4)]
ADA_TICKS += ffn_adas("ffn1") + [W0["down1"] + j for j in (0, 2, 3, 4)]
ADA_TICKS += [W0["rva"] + 3, W0["rq"] + 1, W0["rq"] + 3, W0["rk"] + 1, W0["rk"] + 3]
ADA_TICKS += [W0["rvb"] + j for j in range(4)] + [W0["rg"] + 7, W0["ro"], W0["ro"] + 1]
ADA_TICKS += ffn_adas("ffn2")
assert len(ADA_TICKS) == NADA
ADA_AT = {w: a for a, w in enumerate(ADA_TICKS)}
ADA_STATIC = {w: a for w, a in ADA_AT.items() if not any(w in ffn_adas(f) for f in ("ffn0", "ffn1", "ffn2"))}


def stream_order():
    order = [("w", w) for w in range(WS)]
    for w in range(NW):
        if w + WS < NW:
            order.append(("w", w + WS))
        if w in ADA_AT:
            order.append(("a", ADA_AT[w]))
    return order


ORDER = stream_order()
AT_RAW = {c: n for n, c in enumerate(ORDER)}
NRAW = len(ORDER)

COLS = {}
NCOL = 0
for _name, _n in [("mix_pre", 8), ("ffn_pre", 8), ("mix_g", 16), ("ffn_g", 16), ("fin_g", 8),
                  ("c", 8), ("gamma", 16), ("sg_b", 8), ("b_ada", 112)]:
    COLS[_name] = NCOL
    NCOL += _n


def plan_psum():
    use, u = {}, 0
    for name, n in [("zu", 1), ("zv", 1), ("qa", 1), ("fa", 1), ("ba", 1), ("zi", 2), ("zg", 2),
                    ("qb", 1), ("fb", 1), ("bb", 1), ("ga", 2), ("gb", 2), ("wb", 2), ("wa", 2),
                    ("wout", 2), ("ffn0", GROUPS), ("down0", 2), ("ple", 2), ("pleg", 2),
                    ("fo", 2), ("ffn1", GROUPS), ("down1", 2), ("rva", 2), ("rq", 2), ("rk", 2), ("rvb", 2),
                    ("rg", 4), ("ro", 2), ("ffn2", GROUPS), ("down2", 2)]:
        use[name] = u
        u += n
    jobs, release, split, counts, splits, k = {}, [], {}, {}, 0, 0
    table = [("norm0", 4, "norm"), ("sgu", 2, "sgu_read"), ("pa", 16, "p_copied"),
             ("offa", 2, "off_copied"), ("pva", 2, "pv_read"), ("tb", 2, "split"), ("pb", 16, "p_copied"),
             ("offb", 2, "off_copied"), ("pvb", 2, "pv_read"), ("ta", 4, "split"),
             ("tm", 4, "split"), ("norm1", 4, "norm"),
             ("h0", GROUPS, "split"), ("rows0", 2, "row_copied"), ("tx", 4, "split"),
             ("norm2", 2, "norm"), ("dft1", 4, "split"), ("norm2b", 2, "norm"), ("dft1b", 4, "split"), ("dft2", 4, "split"),
             ("rows1", 2, "row_copied"), ("norm3", 4, "norm"), ("h1", GROUPS, "split"),
             ("rows2", 2, "row_copied"), ("norm4", 4, "norm"), ("sc", 4, "sc_read"),
             ("av", 8, "av_read"), ("ty", 8, "split"), ("norm5", 4, "norm"),
             ("h2", GROUPS, "split"), ("rows3", 2, "row_copied"), ("norm6", 4, "fin_read")]
    for name, n, kind in table:
        jobs[name] = k
        for _ in range(n):
            if kind in ("norm", "split"):
                split[k] = splits
                splits += 1
            sem = {"norm": "norm_read", "split": "lo_done"}.get(kind, kind)
            if kind == "split":
                release.append((sem, splits))
            else:
                counts[sem] = counts.get(sem, 0) + 1
                release.append((sem, counts[sem]))
            k += 1
    return use, jobs, release, split


USE, JOB, RELEASE, SPLIT = plan_psum()


def tile_job(name, t):
    return JOB["norm2b"] if name == "norm2" and t else JOB[name] + 2 * t


RQ = {}
NRQ = 0
for _name, _n in [("norm0", 2), ("ln", 2), ("pva", 2), ("pvb", 2), ("mix", 4), ("ffn", 2),
                  ("norm2", 2), ("norm3", 2), ("norm4", 2), ("av", 8), ("norm5", 2), ("norm6", 2)]:
    RQ[_name] = NRQ
    NRQ += _n
SS = {q: n + 1 for n, q in enumerate(RQ[name] + t for name, k in [
    ("norm0", 2), ("mix", 4), ("ffn", 2), ("norm2", 2), ("norm3", 2), ("norm4", 2), ("norm5", 2), ("norm6", 2)]
    for t in range(k))}


def program(nc, stream, x, pT, cols, rows, sg_wT, masks, ident, dft, rot, decay, outT):
    with ExitStack() as ctx:
        base = (nc.sbuf_base + 255) // 256 * 256

        def sb(name, kb, shape, dt=F32):
            return nc.alloc_sbuf_tensor_at(name, shape, dt, offset=int(base + kb * 1024))

        raw = sb("raw", 0, [P, RAW, 2048])
        w_hi = sb("w_hi", 24, [P, WS, 2048], F32R)
        w_lo = sb("w_lo", 56, [P, WS, 2048], F32R)
        ht = [sb("ht_hi", 96, [P, KT, S], F32R), sb("ht_lo", 104, [P, KT, S], F32R)]
        gt = [sb("gt_hi", 112, [P, FT, S], F32R), sb("gt_lo", 134, [P, FT, S], F32R)]
        xres = sb("xres", 156, [P, TT, D])
        xn = sb("xn", 164, [P, TT, D])
        idn = sb("idn", 172, [P, P])
        ones = sb("ones", 172.5, [P, P])
        col = sb("col", 173, [P, NCOL])
        mod = sb("mod", 173.875, [P, 112])
        moda = sb("moda", 174.375, [P, 5, 8])
        ca = sb("ca", 174.625, [P, 8])
        lbt = sb("lbt", 174.75, [P, 5, 16])
        expo = sb("expo", 175.125, [P, 4])
        st = sb("st", 175.25, [P, NRQ, 3, 4])
        bn = sb("bn", 177, [P, 2, 6])
        mv = sb("mv", 177.125, [P, 2, 2])
        acc = sb("acc", 177.25, [P, 2, 2, 256])
        hb = sb("hb", 181.25, [P, 2, 512])
        ga = sb("ga", 156, [P, TT, D])
        gb = sb("gb", 193.25, [P, TT, D])
        vv = sb("vv", 164, [P, TT, D])
        zg = sb("zg", 185.25, [P, TT, D])
        hgrow = sb("hgrow", 201.25, [P, 2, 512])
        msk = sb("msk", 205.25, [P, 8, P], U8)
        sgw = sb("sgw", 185.25, [P, HEADS, P])
        vg = sb("vg", 189.25, [P, TT, 512])
        lnrow = sb("lnrow", 193.25, [P, 2, 512])
        qf = sb("qf", 112, [P, HH, S])
        qb = sb("qb", 116, [P, HH, S])
        kf = sb("kf", 120, [P, HH, S])
        kb = sb("kb", 124, [P, HH, S])
        tf = sb("tf", 128, [P, HH, S])
        tb = sb("tb", 132, [P, HH, S])
        sq = sb("sq", 136, [P, HH, S])
        sk = sb("sk", 140, [P, HH, S])
        at = sb("at", 144, [P, 2, HH, S])
        u = sb("u", 152, [P, TT, 512])
        bt = [sb("bt_hi", 181.25, [P, TT, 512], F32R), sb("bt_lo", 152, [P, TT, 512], F32R)]
        mskf = sb("mskf", 88, [P, 8, P])
        osq = sb("osq", 88, [P, TT, 512])
        on = sb("on", 92, [P, TT, 512])
        prow = sb("prow", 185.25, [P, 2, D])
        praw = sb("praw", 193.25, [P, 2, S])
        pt = [sb("pt_hi", 195.25, [P, 2, S], F32R), sb("pt_lo", 197.25, [P, 2, S], F32R)]
        dg = sb("dg", 88, [P, KT, P])
        prod = sb("prod", 92, [P, 2, TT, 256])
        csr = sb("csr", 112, [P, 2, 768])
        cs = [sb("cs_hi", 185.25, [P, 2, 768], F32R), sb("cs_lo", 191.25, [P, 2, 768], F32R)]
        grow = [sb("grow0", 201.25, [P, D]), sb("grow1", 197.25, [P, D])]
        tt = [sb("tt_hi", 112, [P, TT, 4, 512], F32R), sb("tt_lo", 134, [P, TT, 4, 512], F32R)]
        qr = sb("qr", 112, [P, RH, 2, S])
        kr = sb("kr", 120, [P, RH, 2, S])
        vr = sb("vr", 128, [P, TT, RH * RV])
        ar = sb("ar", 144, [P, RH, 2, S])
        yr = [sb("yr0", 164, [P, RH * RV]), sb("yr1", 88, [P, RH * RV])]
        gg = sb("gg", 185.25, [P, TT, RH * RV])
        dt = sb("dt", 88, [P, RH, 2, S])
        rt = sb("rt", 205.25, [P, 2, S])
        rab = sb("rab", 164, [P, 2, 4, S])
        gsig = sb("gsig", 118, [P, TT, D])
        outb = sb("outb", 185.25, [P, 4, 512])

        pair = [ctx.enter_context(nc.psum_tensor(f"pair{i}", [P, 2, 512], F32)) for i in range(2)]
        tp = [ctx.enter_context(nc.psum_tensor(f"tp{i}", [P, 512], F32)) for i in range(2)]
        adap = ctx.enter_context(nc.psum_tensor("adap", [P, 512], F32))

        sems = {}

        def sem(name):
            if name not in sems:
                sems[name] = ctx.enter_context(nc.semaphore(name))
            return sems[name]

        landed = [sem(f"landed{i}") for i in range(RAW)]
        raw_done = sem("raw_done")
        hi_done = sem("hi_done")
        w_used = sem("w_used")
        half_ready = sem("half_ready")
        evac = [sem("evac0"), sem("evac1")]
        tp_done = sem("tp_done")
        t_hi = sem("t_hi")
        lo_done = sem("lo_done")
        norm_read = sem("norm_read")
        ada_step = sem("ada_step")
        ada_used = sem("ada_used")
        ss_done = sem("ss_done")
        ms_done = sem("ms_done")
        rstd_done = sem("rstd_done")
        xn_done = sem("xn_done")
        x_ready = sem("x_ready")
        x_in = [sem("x_in0"), sem("x_in1")]
        small_in = sem("small_in")
        sgu_in = sem("sgu_in")
        hg_in = sem("hg_in")
        x_again = [sem("x_again0"), sem("x_again1")]
        prow_in = sem("prow_in")
        p_in = sem("p_in")
        dft_in = sem("dft_in")
        rot_in = sem("rot_in")
        decay_in = sem("decay_in")
        out_done = sem("out_done")
        consts = sem("consts")
        step = sem("step")
        a_step = sem("a_step")
        lb_e = sem("lb_e")
        ca_done = sem("ca_done")
        ln_done = sem("ln_done")
        hg_sk0 = sem("hg_sk0")
        hg_staged = sem("hg_staged")
        hg_qupd = sem("hg_qupd")
        hg_kupd = sem("hg_kupd")
        hg_tot = sem("hg_tot")
        pv_sq = sem("pv_sq")
        a_out = sem("a_out")
        b_out = sem("b_out")
        merged = sem("merged")
        silu_done = sem("silu_done")
        pt_hi = sem("pt_hi")
        pt_done = sem("pt_done")
        sig_done = sem("sig_done")
        cs_hi = sem("cs_hi")
        cs_done = sem("cs_done")
        dg_done = sem("dg_done")
        rot_done = sem("rot_done")
        y_done = sem("y_done")

        def colv(name, i, n=1):
            return col[:, COLS[name] + i:COLS[name] + i + n]

        def at_least(eng, s, value, per=0, i=None):
            if i is None or per == 0:
                if value > 0:
                    eng.wait_ge(s, value)
            else:
                assert value > 0
                eng.wait_ge(s, i * per + value)

        def wait_evac(eng, use, passes=None):
            at_least(eng, evac[use % 2], use // 2 + 1, 1, passes)

        block = ctx.enter_context(nc.Block())

        @block.sync
        def _(sp):
            for t in range(TT):
                sp.dma_start(xres[:, t, :], x[:, t, :]).then_inc(x_in[t], 16)
            sp.dma_start(raw[:, 0, :], stream[0]).then_inc(landed[0], 16)
            sp.dma_start(idn[:], ident).then_inc(small_in, 16)
            sp.dma_start(col[:], cols).then_inc(small_in, 16)
            for n in range(1, RAW):
                sp.dma_start(raw[:, n, :], stream[n]).then_inc(landed[n], 16)
            turns = NRAW // RAW
            with sp.Fori(1, turns) as i:
                for n in range(RAW):
                    sp.wait_ge(raw_done, i * RAW + (n + 1 - RAW))
                    sp.dma_start(raw[:, n, :], stream[i * RAW + n]).then_inc(landed[n], 16)
            for n in range(turns * RAW, NRAW):
                sp.wait_ge(raw_done, n + 1 - RAW)
                sp.dma_start(raw[:, n % RAW, :], stream[n]).then_inc(landed[n % RAW], 16)
            for j in range(4):
                t, half = j // 2, j % 2
                sp.wait_ge(sem("fin_read"), j + 1)
                dst = outT[4 * half:4 * half + 4, :, t * P:(t + 1) * P].rearrange("k p s -> p k s")
                sp.dma_start(dst, outb[:, j, :].rearrange("p (k s) -> p k s", k=4)).then_inc(out_done, 16)
            sp.wait_ge(out_done, 64)

        @block.gpsimd
        def _(pool):
            g = nc.gpsimd
            g.memset(ones[:], 1.0)
            g.memset(expo[:], -0.5).then_inc(consts, 1)
            pool.dma_start(sgw[:], sg_wT).then_inc(sgu_in, 16)
            pool.dma_start(lnrow[:, 0, :], rows[0:1, 0:512].to_broadcast([P, 512])).then_inc(sgu_in, 16)
            pool.dma_start(lnrow[:, 1, :], rows[0:1, 512:1024].to_broadcast([P, 512])).then_inc(sgu_in, 16)
            pool.dma_start(hgrow[:].rearrange("p a b -> p (a b)"), rows[1:2, :].to_broadcast([P, D])).then_inc(hg_in, 16)
            pool.dma_start(mskf[:], masks).then_inc(hg_in, 16)
            pool.wait_ge(consts, 1)

            def rsqrt(q, n=1, w=1):
                for r in range(q, q + n):
                    pool.wait_ge(ms_done, r + 1)
                    g.tensor_tensor(st[:, r, 2, 0:w], st[:, r, 1, 0:w], expo[:, 0:w], ALU.pow).then_inc(rstd_done, 1)

            def key_updates(half):
                for lv in range(1, 8):
                    h = 1 << (lv - 1)
                    v = [a[:].rearrange("p a (b two h) -> p (a b) two h", two=2, h=h) for a in (kf, kb, tf, tb)]
                    nb = HH * S // (2 * h)
                    pool.wait_ge(hg_staged, 8 * half + lv + 1)
                    if lv == 1:
                        pool.wait_ge(hg_qupd, 8 * half + 1)
                    else:
                        pool.wait_ge(hg_tot, 6 * half + lv - 1)
                    g.tensor_tensor(v[0][:, :, 0, :], v[0][:, :, 0, :], v[2][:, :, 1, 0:1].to_broadcast([P, nb, h]), ALU.mult)
                    g.tensor_tensor(v[1][:, :, 1, :], v[1][:, :, 1, :], v[3][:, :, 0, 0:1].to_broadcast([P, nb, h]), ALU.mult).then_inc(hg_kupd, 1)

            rsqrt(RQ["norm0"], 2)
            rsqrt(RQ["ln"], 2)
            key_updates(0)
            rsqrt(RQ["pva"], 2, 4)
            key_updates(1)
            rsqrt(RQ["pvb"], 2, 4)
            pool.wait_ge(tp_done, JOB["ta"] + 4)
            pool.dma_start(prow[:].rearrange("p a b -> p (a b)"),
                           rows[2:4, :].rearrange("(o a) b -> o (a b)", o=1).to_broadcast([P, 2 * D])).then_inc(prow_in, 16)
            for t in range(TT):
                pool.wait_ge(tp_done, JOB["tm"] + 2 * t + 2)
                pool.dma_start(xres[:, t, :], x[:, t, :]).then_inc(x_again[t], 16)
            pool.wait_ge(merged, 2)
            pool.dma_start(praw[:], pT).then_inc(p_in, 16)
            rsqrt(RQ["mix"], 4)
            rsqrt(RQ["ffn"], 2)
            pool.wait_ge(w_used, W0["down0"] + GROUPS)
            pool.dma_start(csr[:], dft).then_inc(dft_in, 16)
            rsqrt(RQ["norm2"], 2)
            rsqrt(RQ["norm3"], 2)
            pool.wait_ge(tp_done, JOB["rows2"] + 2)
            pool.dma_start(dt[:], decay).then_inc(decay_in, 16)
            pool.dma_start(rt[:], rot).then_inc(rot_in, 16)
            rsqrt(RQ["norm4"], 2)
            rsqrt(RQ["av"], 8)
            rsqrt(RQ["norm5"], 2)
            rsqrt(RQ["norm6"], 2)

        @block.tensor
        def _(pe):
            def passes(a, b):
                return [(a[1], b[0]), (a[0], b[0]), (a[0], b[1])]

            wsp = (w_hi, w_lo)

            def wait_chunk(w, i=None):
                at_least(pe, raw_done, AT_RAW["w", w] + 1, 6, i)

            def claim_pair(use, i=None):
                if use >= 2:
                    wait_evac(pe, use - 2, i)

            def claim(k):
                if k >= 2:
                    name, value = RELEASE[k - 2]
                    pe.wait_ge(sem(name), value)

            def wide_part(w, use, c, t):
                for k in range(4):
                    for n, (a, b) in enumerate(passes(ht, wsp)):
                        mm = pe.matmul(pair[use % 2][:, t, :], a[:, 4 * c + k, t * P:(t + 1) * P],
                                       b[:, w % WS, k * 512:(k + 1) * 512],
                                       start=(c == 0 and k == 0 and n == 0), stop=(c == 1 and k == 3 and n == 2))
                if t == TT - 1:
                    mm.then_inc(w_used, 1)

            def wide_chunk(w, use, c, i=None):
                wait_chunk(w, i)
                if c == 0:
                    claim_pair(use, i)
                for t in range(TT):
                    wide_part(w, use, c, t)

            def wide(w, use, i=None):
                for c in range(2):
                    wide_chunk(w + c, use, c, i)

            def feat(w, use, c):
                wait_chunk(w)
                if c == 0:
                    claim_pair(use)
                wv = [a[:, w % WS, :].rearrange("p (k n) -> p k n", k=KT) for a in wsp]
                for m in range(2):
                    for k in range(KT):
                        for n, (a, b) in enumerate(passes(wv, ht)):
                            mm = pe.matmul(pair[use % 2][:, c, m * S:(m + 1) * S], a[:, k, m * P:(m + 1) * P],
                                           b[:, k, :], start=(k == 0 and n == 0), stop=(k == KT - 1 and n == 2))
                mm.then_inc(w_used, 1)

            def turned_head(w, use, norm, split):
                wait_split(split, 2)
                for c in range(3):
                    wait_chunk(w + c)
                    if c % 2 == 0:
                        claim_pair(use + c // 2)
                    wide_part(w + c, use + c // 2, c % 2, 0)
                    if c == 1:
                        norm()
                wait_split(split, 4)
                for c in range(3):
                    wide_part(w + c, use + c // 2, c % 2, 1)

            def outer(w, n, use, src, k0=0, before={}, after={}):
                m = max(0, n - 4)
                order = [(c, t) for c in range(m) for t in range(TT)] + [(c, t) for t in range(TT) for c in range(m, n)]
                for c, t in order:
                    if (c, t) in before:
                        before[c, t]()
                    if t == 0:
                        wait_chunk(w + c)
                    if c == 0:
                        claim_pair(use + t)
                    for half in range(2):
                        for k in range(2):
                            for m, (a, b) in enumerate([(1, 0), (0, 0), (0, 1)]):
                                mm = pe.matmul(pair[(use + t) % 2][:, half, :], src(a, k0 + 2 * c + k, t),
                                               wsp[b][:, (w + c) % WS, k * D + half * 512:k * D + half * 512 + 512],
                                               start=(c == 0 and k == 0 and m == 0),
                                               stop=(c == n - 1 and k == 1 and m == 2))
                    if t == TT - 1:
                        mm.then_inc(w_used, 1)
                        ada_after(w + c)
                    elif c == n - 1:
                        mm.then_inc(half_ready, 1)
                    if (c, t) in after:
                        after[c, t]()

            def tiles(a):
                return lambda part, k, t: a[part][:, k, t * P:(t + 1) * P]

            def turn(k, srcs, bank_free=True):
                if bank_free:
                    claim(k)
                for n, a in enumerate(srcs):
                    mm = pe.transpose(tp[k % 2][:, n * P:(n + 1) * P], a, idn[:])
                mm.then_inc(tp_done, 1)

            def ada(a, i=None):
                at_least(pe, raw_done, AT_RAW["a", a] + 1, 6, i)
                for half in range(2):
                    n = 2 * a + half
                    dst = adap[:, n:n + 1] if i is None else adap[:, bass.ds(i * 4 + n, 1)]
                    for b in range(2):
                        mm = pe.matmul(dst, acc[:, a % 2, b, half * P:(half + 1) * P], ones[:, 0:1],
                                       start=(b == 0), stop=(b == 1))
                mm.then_inc(ada_used, 1)

            def ada_after(w):
                if w - 2 in ADA_STATIC:
                    ada(ADA_STATIC[w - 2])

            def turn_tile(name, src, t, ready, n):
                def go():
                    pe.wait_ge(ready, n)
                    for half in range(2):
                        turn(tile_job(name, t) + half,
                             [src[:, t, (4 * half + k) * P:(4 * half + k + 1) * P] for k in range(4)])
                return go

            def wait_split(name, n):
                pe.wait_ge(lo_done, SPLIT[JOB[name]] + n)

            def gate_rows(name, n_done):
                pe.wait_ge(dg_done, n_done)
                for half in range(2):
                    k = JOB[name] + half
                    claim(k)
                    pe.matmul(tp[k % 2][:], ones[:], dg[:, 4 * half:4 * half + 4, :].rearrange("p a b -> p (a b)"),
                              start=True, stop=True).then_inc(tp_done, 1)

            def ffn(name, jobs, norm, split):
                w, use, k, a = W0[name], USE[name], JOB[jobs], ADA_AT[ffn_adas(name)[0]]

                def hidden(j, k, i=None):
                    wait_evac(pe, use + j, i)
                    at_least(pe, lo_done, SPLIT[k] - 1, 2, i)
                    turn(k, [prod[:, j % 2, t, m * P:(m + 1) * P] for m in range(2) for t in range(TT)], False)

                turned_head(w, use, norm, split)
                wide_chunk(w + 3, use + 1, 1)
                hidden(0, k)
                wide(w + 4, use + 2)
                hidden(1, k + 1)
                with pe.Fori(0, (GROUPS - PEELED) // 2) as i:
                    for v in range(2):
                        j = PEELED + v
                        wide(w + 2 * j, use + j, i)
                        hidden(j - 1, k + j - 1, i)
                        ada(a + v, i)
                wait_split(jobs, GROUPS - 1)
                return lambda: hidden(GROUPS - 1, k + GROUPS - 1)

            def levels(half, name):
                job = JOB["pa" if half == 0 else "pb"]
                for lv in range(8):
                    wide_chunk(W0[name] + lv, USE[name] + lv // 2, lv % 2)
                    ada_after(W0[name] + lv)
                    pe.wait_ge(hg_staged, 8 * half + lv + 1)
                    if lv == 0:
                        pe.wait_ge(hg_sk0, half + 1)
                    for s in range(2):
                        k = job + 2 * lv + s
                        claim(k)
                        for hd in range(HH):
                            mm = pe.matmul(tp[k % 2][:, hd * P:(hd + 1) * P], sk[:, hd, s * P:(s + 1) * P],
                                           sq[:, hd, s * P:(s + 1) * P], start=True, stop=True)
                        mm.then_inc(tp_done, 1)

            def across(half):
                pe.wait_ge(hg_qupd, 8 * half + 8)
                pe.wait_ge(hg_kupd, 7 * half + 7)
                job = JOB["offa" if half == 0 else "offb"]
                for s in range(2):
                    k = job + s
                    claim(k)
                    ks, qs = (kf, qf) if s == 0 else (kb, qb)
                    for hd in range(HH):
                        mm = pe.matmul(tp[k % 2][:, hd * P:(hd + 1) * P], ks[:, hd, s * P:(s + 1) * P],
                                       qs[:, hd, (1 - s) * P:(2 - s) * P], start=True, stop=True)
                    mm.then_inc(tp_done, 1)

            def values(half):
                pe.wait_ge(sem("p_copied"), 16 * half + 16)
                pe.wait_ge(sem("off_copied"), 2 * half + 2)
                for t in range(TT):
                    k = JOB["pva" if half == 0 else "pvb"] + t
                    claim(k)
                    for hd in range(HH):
                        for s in range(2):
                            mm = pe.matmul(tp[k % 2][:, hd * P:(hd + 1) * P], at[:, s, hd, t * P:(t + 1) * P],
                                           vv[:, s, (HH * half + hd) * P:(HH * half + hd + 1) * P],
                                           start=(s == 0), stop=(s == 1))
                    mm.then_inc(tp_done, 1)

            pe.wait_ge(small_in, 32)
            pe.wait_ge(consts, 1)
            turn_tile("norm0", xn, 0, xn_done, 1)()
            turned_head(W0["zu"], USE["zu"], turn_tile("norm0", xn, 1, xn_done, 2), "norm0")
            wide_chunk(W0["zv"] + 1, USE["zv"], 1)
            for name in ("qa", "fa", "ba"):
                for c in range(2):
                    feat(W0[name] + c, USE[name], c)
                    ada_after(W0[name] + c)
                    if name == "ba" and c == 0:
                        pe.wait_ge(ln_done, 2)
                        pe.wait_ge(sgu_in, 48)
                        for t in range(TT):
                            k = JOB["sgu"] + t
                            claim(k)
                            for gr in range(8):
                                mm = pe.matmul(tp[k % 2][:, gr * 64:(gr + 1) * 64], sgw[:, gr, :],
                                               vg[:, t, gr * 64:(gr + 1) * 64], start=True, stop=True)
                            mm.then_inc(tp_done, 1)
            levels(0, "zi")
            for n, name in enumerate(("qb", "fb", "bb")):
                for c in range(2):
                    feat(W0[name] + c, USE[name], c)
                    ada_after(W0[name] + c)
                    if n == 0 and c == 0:
                        across(0)
                if n == 0:
                    wait_evac(pe, USE["zi"] + 1)
                    values(0)
            pe.wait_ge(b_out, 2)
            for t in range(TT):
                turn(JOB["tb"] + t, [u[:, t, k * P:(k + 1) * P] for k in range(4)])
            levels(1, "ga")
            wait_split("tb", 2)
            outer(W0["wb"], 2, USE["wb"], lambda part, k, t: bt[part][:, t, k * P:(k + 1) * P],
                  after={(1, 0): lambda: across(1), (0, 1): lambda: values(1)})
            turn_tile("ta", zg, 0, a_out, 3)()
            outer(W0["wa"], 4, USE["wa"], tiles(gt),
                  before={(0, 0): lambda: wait_split("ta", 2), (0, 1): lambda: wait_split("ta", 4)},
                  after={(1, 0): turn_tile("ta", zg, 1, a_out, 4),
                         (1, 1): turn_tile("tm", ga, 0, merged, 1)})
            outer(W0["wout"], 4, USE["wout"], tiles(ht),
                  before={(0, 0): lambda: wait_split("tm", 2), (0, 1): lambda: wait_split("tm", 4)},
                  after={(1, 0): turn_tile("tm", ga, 1, merged, 2),
                         (2, 1): turn_tile("norm1", xn, 0, xn_done, 3)})
            last = ffn("ffn0", "h0", turn_tile("norm1", xn, 1, xn_done, 4), "norm1")
            outer(W0["down0"], GROUPS, USE["down0"], tiles(gt),
                  before={(GROUPS - 1, 0): lambda: wait_split("h0", GROUPS)},
                  after={(0, 1): last, (8, 0): lambda: gate_rows("rows0", 1)})
            pe.wait_ge(pt_done, 1)
            outer(W0["ple"], 1, USE["ple"], tiles(pt),
                  after={(0, 0): turn_tile("tx", xres, 0, x_ready, 3)})
            outer(W0["pleg"], 4, USE["pleg"], tiles(ht),
                  before={(0, 0): lambda: wait_split("tx", 2), (0, 1): lambda: wait_split("tx", 4)},
                  after={(1, 0): turn_tile("tx", xres, 1, x_ready, 4),
                         (1, 1): turn_tile("norm2", xn, 0, xn_done, 5)})
            wait_split("norm2", 2)
            pe.wait_ge(cs_done, 1)
            for t in range(TT):
                for gr in range(4):
                    k = JOB["dft1b" if t else "dft1"] + gr
                    claim(k)
                    for d in range(2):
                        for n, (a, b) in enumerate(passes(ht, cs)):
                            mm = pe.matmul(tp[k % 2][:], a[:, 2 * gr + d, t * P:(t + 1) * P], b[:, d, 0:512],
                                           start=(d == 0 and n == 0), stop=(d == 1 and n == 2))
                    mm.then_inc(tp_done, 1)
                if t == 0:
                    turn_tile("norm2", xn, 1, xn_done, 6)()
                    wait_split("norm2b", 2)
            for gr in range(4):
                wait_split("dft1b", gr + 1)
                k = JOB["dft2"] + gr
                claim(k)
                for m in range(2):
                    for n, (t, part) in enumerate([(0, 0), (0, 1), (1, 0), (1, 1)]):
                        for o, (a, b) in enumerate(passes(tt, cs)):
                            mm = pe.matmul(tp[k % 2][:, m * S:(m + 1) * S],
                                           a[:, t, gr, part * S + m * P:part * S + (m + 1) * P],
                                           b[:, t, 2 * part * S:(2 * part + 1) * S],
                                           start=(n == 0 and o == 0), stop=(n == 3 and o == 2))
                mm.then_inc(tp_done, 1)
            outer(W0["fo"], 4, USE["fo"], tiles(ht),
                  before={(c, 0): lambda c=c: wait_split("dft2", c + 1) for c in range(4)},
                  after={(2, 0): lambda: gate_rows("rows1", 2), (1, 1): turn_tile("norm3", xn, 0, xn_done, 7)})
            last = ffn("ffn1", "h1", turn_tile("norm3", xn, 1, xn_done, 8), "norm3")
            outer(W0["down1"], GROUPS, USE["down1"], tiles(gt),
                  before={(GROUPS - 1, 0): lambda: wait_split("h1", GROUPS)},
                  after={(0, 1): last, (8, 0): lambda: gate_rows("rows2", 3),
                         (GROUPS - 3, 1): turn_tile("norm4", xn, 0, xn_done, 9)})
            turned_head(W0["rva"], USE["rva"], turn_tile("norm4", xn, 1, xn_done, 10), "norm4")
            wide_chunk(W0["rva"] + 3, USE["rva"] + 1, 1)
            for name in ("rq", "rk"):
                for c in range(4):
                    feat(W0[name] + c, USE[name] + c // 2, c % 2)
                    ada_after(W0[name] + c)
            for c in range(4):
                wide_chunk(W0["rvb"] + c, USE["rvb"] + c // 2, c % 2)
                ada_after(W0["rvb"] + c)
                if c == 1:
                    pe.wait_ge(rot_done, 4)
                if c:
                    for hd in ((), (0,), (1, 2), (3,))[c]:
                        k = JOB["sc"] + hd
                        claim(k)
                        for s in range(2):
                            for d in range(2):
                                mm = pe.matmul(tp[k % 2][:, s * S:(s + 1) * S], kr[:, hd, d, s * P:(s + 1) * P],
                                               qr[:, hd, d, :], start=(d == 0), stop=(d == 1))
                        mm.then_inc(tp_done, 1)

            def turn_head(hd):
                pe.wait_ge(y_done, hd + 1)
                for t in range(TT):
                    turn(JOB["ty"] + 2 * hd + t, [gg[:, t, (4 * hd + k) * P:(4 * hd + k + 1) * P] for k in range(4)])

            for c in range(8):
                wide_chunk(W0["rg"] + c, USE["rg"] + c // 2, c % 2)
                ada_after(W0["rg"] + c)
                if c == 0:
                    wait_evac(pe, USE["rvb"])
                    wait_evac(pe, USE["rvb"] + 1)
                    pe.wait_ge(sem("sc_read"), RH)
                if c < RH:
                    for t in range(TT):
                        k = JOB["av"] + 2 * c + t
                        claim(k)
                        for s in range(2):
                            mm = pe.matmul(tp[k % 2][:], ar[:, c, s, t * P:(t + 1) * P], vr[:, s, c * RV:(c + 1) * RV],
                                           start=(s == 0), stop=(s == 1))
                        mm.then_inc(tp_done, 1)
                elif c > RH:
                    turn_head(c - RH - 1)
            outer(W0["ro"], 8, USE["ro"], tiles(gt),
                  before={(0, 0): lambda: wait_split("ty", 2), (2, 0): lambda: wait_split("ty", 4),
                          (4, 0): lambda: wait_split("ty", 6), (6, 0): lambda: wait_split("ty", 8)},
                  after={(0, 1): lambda: turn_head(RH - 1), (5, 1): turn_tile("norm5", xn, 0, xn_done, 11)})
            last = ffn("ffn2", "h2", turn_tile("norm5", xn, 1, xn_done, 12), "norm5")
            outer(W0["down2"], GROUPS, USE["down2"], tiles(gt),
                  before={(GROUPS - 1, 0): lambda: wait_split("h2", GROUPS)},
                  after={(0, 1): last, (4, 1): lambda: gate_rows("rows3", 4),
                         (GROUPS - 2, 1): turn_tile("norm6", xn, 0, xn_done, 13)})
            turn_tile("norm6", xn, 1, xn_done, 14)()

        @block.scalar
        def _(act):
            sc = nc.scalar

            def split_hi(w, i=None):
                if w >= NW:
                    return
                n = AT_RAW["w", w]
                at_least(act, landed[n % RAW], 16 * (n // RAW + 1), 32, i)
                if w >= WS:
                    at_least(act, w_used, w - WS + 1, 4, i)
                sc.activation(w_hi[:, w % WS, :], raw[:, n % RAW, :], ACT.Copy).then_inc(hi_done, 1)

            def tick(w, i=None):
                split_hi(w + WS, i)

            def pair_ready(w, i=None):
                at_least(act, w_used, w + 1, 4, i)

            def evacuate(dst, use, func, scale=1.0, last=True):
                ins = sc.activation(dst, pair[use % 2][:], func, scale=scale)
                if last:
                    ins.then_inc(evac[use % 2], 1)

            def hi(k, dst, src=None, i=None):
                if src is None:
                    at_least(act, tp_done, k + 1, 2, i)
                    src = tp[k % 2][:]
                sc.activation(dst, src, ACT.Copy).then_inc(t_hi, 1)

            def norm_squares(q, t, n_x):
                act.wait_ge(x_ready, n_x) if n_x else act.wait_ge(x_in[t], 16)
                sc.activation(xn[:, t, :], xres[:, t, :], ACT.Square, accum_out=st[:, q, 0, 0:1]).then_inc(ss_done, 1)

            def norm_his(name, t):
                for half in range(2):
                    k = tile_job(name, t) + half
                    n = RELEASE[k][1]
                    act.wait_ge(norm_read, n)
                    hi(k, ht[0][:, 4 * half:4 * half + 4, t * P:(t + 1) * P],
                       hb[:, k % 2, :].rearrange("p (k s) -> p k s", k=4))

            def post_squares(q, t, w, use, halves):
                if t == 0:
                    act.wait_ge(half_ready, halves)
                else:
                    pair_ready(w)
                sc.activation(xn[:, t, :].rearrange("p (a b) -> p a b", a=2), pair[(use + t) % 2][:], ACT.Square,
                              accum_out=st[:, q, 0, 0:1]).then_inc(ss_done, 1)

            def turned(k, dst, q, t):
                hi(k, dst[0][:, 4 * q:4 * q + 4, t * P:(t + 1) * P], _four(tp[k % 2][:], k))

            def turned_tile(name, dst, t):
                for q in range(2):
                    turned(JOB[name] + 2 * t + q, dst, q, t)

            def _four(a, k):
                act.wait_ge(tp_done, k + 1)
                return a.rearrange("p (k s) -> p k s", k=4)

            def stage_level(half, lv):
                if lv == 0:
                    if half:
                        act.wait_ge(tp_done, JOB["pa"] + 16)
                    act.wait_ge(evac[USE["qa" if half == 0 else "qb"] % 2], USE["qa" if half == 0 else "qb"] // 2 + 1)
                    sc.activation(sq[:], qf[:], ACT.Copy).then_inc(hg_staged, 1)
                    return
                h = 1 << (lv - 1)
                v = [a[:].rearrange("p a (b two h) -> p (a b) two h", two=2, h=h) for a in (qf, qb, kf, kb, sq, sk)]
                act.wait_ge(hg_qupd, 8 * half + lv)
                at_least(act, hg_kupd, 7 * half + lv - 1)
                act.wait_ge(tp_done, JOB["pa" if half == 0 else "pb"] + 2 * lv)
                sc.activation(v[4][:, :, 1, :], v[0][:, :, 1, :], ACT.Copy)
                sc.activation(v[4][:, :, 0, :], v[1][:, :, 0, :], ACT.Copy)
                sc.activation(v[5][:, :, 0, :], v[2][:, :, 0, :], ACT.Copy)
                sc.activation(v[5][:, :, 1, :], v[3][:, :, 1, :], ACT.Copy).then_inc(hg_staged, 1)

            def across(half):
                for s in range(2):
                    k = JOB["offa" if half == 0 else "offb"] + s
                    act.wait_ge(tp_done, k + 1)
                    if half:
                        act.wait_ge(tp_done, JOB["pva"] + 2)
                    sc.activation(at[:, s, :, (1 - s) * P:(2 - s) * P], tp[k % 2][:].rearrange("p (a b) -> p a b", a=HH),
                                  ACT.Copy).then_inc(sem("off_copied"), 1)

            def value_squares(half):
                for t in range(TT):
                    k = JOB["pva" if half == 0 else "pvb"] + t
                    act.wait_ge(tp_done, k + 1)
                    if half:
                        act.wait_ge(a_out, 2)
                    sc.activation(osq[:, t, :], tp[k % 2][:], ACT.Square).then_inc(pv_sq, 1)

            def ffn(name, jobs):
                w, use, k = W0[name], USE[name], JOB[jobs]

                def group(j, w, use, i=None):
                    at_least(act, w_used, w + 2, 4, i)
                    if j >= 2:
                        at_least(act, tp_done, k + j - 1, 2, i)
                    for t in range(TT):
                        sc.activation(prod[:, j % 2, t, :], pair[use % 2][:, t, 0:256], ACT.Silu).then_inc(silu_done, 1)

                def hidden_hi(j, k, i=None):
                    at_least(act, tp_done, k + 1, 2, i)
                    dst = gt[0][:, 2 * j:2 * j + 2, :] if i is None else gt[0][:, bass.ds(i * 4 + 2 * j, 2), :]
                    sc.activation(dst, tp[k % 2][:].rearrange("p (a b) -> p a b", a=2), ACT.Copy).then_inc(t_hi, 1)

                for j in range(PEELED):
                    group(j, w + 2 * j, use + j)
                    if j:
                        hidden_hi(j - 1, k + j - 1)
                    tick(w + 2 * j)
                    tick(w + 2 * j + 1)
                with act.Fori(0, (GROUPS - PEELED) // 2) as i:
                    for j in range(PEELED, PEELED + 2):
                        group(j, w + 2 * j, use + j, i)
                        hidden_hi(j - 1, k + j - 1, i)
                        tick(w + 2 * j, i)
                        tick(w + 2 * j + 1, i)
                hidden_hi(GROUPS - 1, k + GROUPS - 1)

            def gate_rows(name, row):
                for half in range(2):
                    k = JOB[name] + half
                    act.wait_ge(tp_done, k + 1)
                    sc.activation(row[:, half * 512:(half + 1) * 512], tp[k % 2][:], ACT.Copy).then_inc(sem("row_copied"), 1)

            norm_squares(RQ["norm0"], 0, 0)
            norm_squares(RQ["norm0"] + 1, 1, 0)
            split_hi(0)
            norm_his("norm0", 0)
            split_hi(1)
            split_hi(2)
            norm_his("norm0", 1)
            split_hi(3)
            act.wait_ge(lb_e, 1)
            sc.activation(lbt[:, 1, :], lbt[:, 0, :], ACT.Exp).then_inc(lb_e, 1)
            sc.activation(ca[:], colv("c", 0, 8), ACT.Silu).then_inc(ca_done, 1)
            tick(0)
            pair_ready(1)
            evacuate(u[:], USE["zu"], ACT.Gelu)
            tick(1)
            tick(2)
            pair_ready(3)
            evacuate(vg[:], USE["zv"], ACT.Gelu)
            tick(3)

            def head_gates(half):
                q, f, b = ("qa", "fa", "ba") if half == 0 else ("qb", "fb", "bb")
                tick(W0[q])
                if half:
                    act.wait_ge(tp_done, JOB["offa"] + 2)
                    across(0)
                pair_ready(W0[q] + 1)
                as4 = "p a (b s) -> p (a b) s"
                sc.activation(qf[:], pair[USE[q] % 2][:].rearrange(as4, b=2), ACT.Silu).then_inc(evac[USE[q] % 2], 1)
                tick(W0[q] + 1)
                if half:
                    value_squares(0)
                stage_level(half, 0)
                tick(W0[f])
                pair_ready(W0[f] + 1)
                sc.activation(tf[:], pair[USE[f] % 2][:].rearrange(as4, b=2), ACT.Sigmoid)
                sc.activation(kf[:], pair[USE[f] % 2][:].rearrange(as4, b=2), ACT.Sigmoid, scale=-1.0).then_inc(evac[USE[f] % 2], 1)
                tick(W0[f] + 1)
                tick(W0[b])
                pair_ready(W0[b] + 1)
                sc.activation(tb[:], pair[USE[b] % 2][:].rearrange(as4, b=2), ACT.Sigmoid)
                sc.activation(kb[:], pair[USE[b] % 2][:].rearrange(as4, b=2), ACT.Sigmoid, scale=-1.0).then_inc(evac[USE[b] % 2], 1)
                tick(W0[b] + 1)

            def boundary(w, q, name, n_x):
                norm_squares(q, 0, n_x)
                tick(w - 3)
                norm_his(name, 0)
                tick(w - 2)
                tick(w - 1)
                norm_squares(q + 1, 1, n_x + 1)
                norm_his(name, 1)
                tick(w)

            def gated_chunks(half, name0, plan):
                for lv in range(8):
                    w = W0[name0] + lv
                    if lv % 2 == 1:
                        pair_ready(w)
                        dst, func = plan[lv // 2]
                        use = USE[name0] + lv // 2
                        evacuate(dst, use, func)
                    tick(w)
                    if lv < 7:
                        stage_level(half, lv + 1)

            head_gates(0)
            gated_chunks(0, "zi", [(vv[:, :, 0:512], ACT.Copy), (vv[:, :, 512:1024], ACT.Copy),
                                   (zg[:, :, 0:512], ACT.Silu), (zg[:, :, 512:1024], ACT.Silu)])
            head_gates(1)
            for t in range(TT):
                hi(JOB["tb"] + t, bt[0][:, t, :])
            gated_chunks(1, "ga", [(ga[:, :, 0:512], ACT.Sigmoid), (ga[:, :, 512:1024], ACT.Sigmoid),
                                   (gb[:, :, 0:512], ACT.Sigmoid), (gb[:, :, 512:1024], ACT.Sigmoid)])
            across(1)
            tick(W0["wb"])
            value_squares(1)
            turned_tile("ta", gt, 0)
            tick(W0["wb"] + 1)
            turned_tile("ta", gt, 1)
            tick(W0["wa"])
            turned_tile("tm", ht, 0)
            tick(W0["wa"] + 1)
            tick(W0["wa"] + 2)
            turned_tile("tm", ht, 1)
            tick(W0["wa"] + 3)
            w = W0["wout"]
            for t in range(TT):
                post_squares(RQ["mix"] + 2 * t, t, w + 3, USE["wout"], 3)
                norm_squares(RQ["mix"] + 2 * t + 1, t, 1 + t)
                if t == 0:
                    tick(w)
                norm_his("norm1", t)
                if t == 0:
                    tick(w + 1)
                    tick(w + 2)
            tick(w + 3)
            ffn("ffn0", "h0")
            w = W0["down0"]
            for c in range(GROUPS - 4):
                tick(w + c)
                if c == 0:
                    act.wait_ge(p_in, 16)
                    sc.activation(pt[0][:], praw[:], ACT.Copy).then_inc(pt_hi, 1)
            gate_rows("rows0", grow[0])
            post_squares(RQ["ffn"], 0, w + GROUPS - 1, USE["down0"], 4)
            tick(w + GROUPS - 4)
            tick(w + GROUPS - 3)
            tick(w + GROUPS - 2)
            post_squares(RQ["ffn"] + 1, 1, w + GROUPS - 1, USE["down0"], 4)
            tick(w + GROUPS - 1)
            for t in range(TT):
                if t == 0:
                    act.wait_ge(half_ready, 5)
                else:
                    pair_ready(W0["ple"])
                act.wait_ge(x_ready, 3 + t)
                sc.activation(xn[:, t, :].rearrange("p (a b) -> p a b", a=2), pair[(USE["ple"] + t) % 2][:],
                              ACT.Copy).then_inc(evac[(USE["ple"] + t) % 2], 1)
                if t:
                    tick(W0["ple"])
                turned_tile("tx", ht, t)
            act.wait_ge(dft_in, 16)
            act.wait_ge(w_used, W0["ple"] + 1)
            act.wait_ge(x_ready, 4)
            sc.activation(cs[0][:], csr[:], ACT.Copy).then_inc(cs_hi, 1)
            w = W0["pleg"] + 3
            for t in range(TT):
                if t == 0:
                    act.wait_ge(half_ready, 6)
                else:
                    pair_ready(w)
                sc.activation(gsig[:, t, :].rearrange("p (a b) -> p a b", a=2), pair[(USE["pleg"] + t) % 2][:],
                              ACT.Sigmoid).then_inc(evac[(USE["pleg"] + t) % 2], 1)
                norm_squares(RQ["norm2"] + t, t, 5 + t)
                if t == 0:
                    tick(w - 3)
                norm_his("norm2", t)
                if t == 0:
                    tick(w - 2)
                    tick(w - 1)
                else:
                    tick(w)
                for gr in range(4):
                    hi(JOB["dft1b" if t else "dft1"] + gr, tt[0][:, t, gr, :])
            for gr in range(4):
                k = JOB["dft2"] + gr
                act.wait_ge(tp_done, k + 1)
                hi(k, ht[0][:, 2 * gr:2 * gr + 2, :], tp[k % 2][:].rearrange("p (a b) -> p a b", a=2))
            gate_rows("rows1", grow[1])
            boundary(W0["fo"] + 3, RQ["norm3"], "norm3", 7)
            ffn("ffn1", "h1")
            for w in range(W0["down1"], W0["down1"] + GROUPS - 4):
                tick(w)
            gate_rows("rows2", grow[0])
            boundary(W0["down1"] + GROUPS - 1, RQ["norm4"], "norm4", 9)

            def values(name, gr):
                c = gr % 2
                tick(W0[name] + 2 * c)
                pair_ready(W0[name] + 2 * c + 1)
                evacuate(vr[:, :, gr * RV:(gr + 1) * RV], USE[name] + c, ACT.Copy)
                tick(W0[name] + 2 * c + 1)

            values("rva", 0)
            values("rva", 1)
            for w in range(W0["rq"], W0["rvb"]):
                tick(w)
            values("rvb", 2)
            values("rvb", 3)

            def head_his(hd):
                for t in range(TT):
                    turned(JOB["ty"] + 2 * hd + t, gt, hd, t)

            for gr in range(4):
                tick(W0["rg"] + 2 * gr)
                if gr == 3:
                    head_his(0)
                pair_ready(W0["rg"] + 2 * gr + 1)
                evacuate(gg[:, :, gr * RV:(gr + 1) * RV], USE["rg"] + gr, ACT.Silu)
                tick(W0["rg"] + 2 * gr + 1)
            head_his(1)
            head_his(2)
            tick(W0["ro"])
            head_his(3)
            for w in range(W0["ro"] + 1, W0["ro"] + 4):
                tick(w)
            boundary(W0["ro"] + 7, RQ["norm5"], "norm5", 11)
            ffn("ffn2", "h2")
            for w in range(W0["down2"], W0["down2"] + GROUPS - 1):
                if w == W0["down2"] + 3:
                    gate_rows("rows3", grow[1])
                tick(w)
            for t in range(TT):
                norm_squares(RQ["norm6"] + t, t, 13 + t)

        @block.vector
        def _(dve):
            v = nc.vector
            steps = [0]

            def link(ins):
                steps[0] += 1
                ins.then_inc(step, 1)
                dve.wait_ge(step, steps[0])

            def as_f32(a):
                return a.bitcast(F32)

            whi32 = as_f32(w_hi[:])
            ht32, gt32, tt32 = as_f32(ht[0][:]), as_f32(gt[0][:]), as_f32(tt[0][:])

            def split_lo(w, i=None):
                if w >= NW:
                    return
                n = AT_RAW["w", w]
                at_least(dve, hi_done, w + 1, 4, i)
                v.tensor_tensor(w_lo[:, w % WS, :], raw[:, n % RAW, :], whi32[:, w % WS, :],
                                ALU.subtract).then_inc(raw_done, 1)

            def ada(a, i=None):
                n = AT_RAW["a", a]
                at_least(dve, landed[n % RAW], 16 * (n // RAW + 1), 32, i)
                if a >= 2:
                    at_least(dve, ada_used, a - 1, 2, i)
                for k in range(KT):
                    src, dst = raw[:, n % RAW, k * 256:(k + 1) * 256], acc[:, a % 2, k % 2, :]
                    if k < 2:
                        ins = v.tensor_scalar(dst, src, ca[:, k:k + 1], None, ALU.mult)
                    else:
                        at_least(dve, ada_step, 7 * a + k - 1, 14, i)
                        ins = v.scalar_tensor_tensor(out=dst, in0=src, scalar=ca[:, k:k + 1], in1=dst,
                                                     op0=ALU.mult, op1=ALU.add)
                    ins.then_inc(raw_done if k == KT - 1 else ada_step, 1)

            def tick(w, i=None):
                split_lo(w + WS, i)
                if w in ADA_STATIC:
                    ada(ADA_STATIC[w])

            def ready(use, t, w, halves):
                if t == 0:
                    dve.wait_ge(half_ready, halves)
                else:
                    dve.wait_ge(w_used, w + 1)

            def mean_square(q):
                dve.wait_ge(ss_done, SS[q])
                v.tensor_scalar(st[:, q, 1, 0:1], st[:, q, 0, 0:1], 1.0 / D, EPS, ALU.mult, ALU.add).then_inc(ms_done, 1)
                dve.wait_ge(rstd_done, q + 1)

            def two(a):
                return a.rearrange("p (a b) -> p a b", a=2)

            def norm(q, t, before=None):
                if before is not None:
                    tick(before)
                mean_square(q)
                v.tensor_scalar(xn[:, t, :], xres[:, t, :], st[:, q, 2, 0:1], None, ALU.mult).then_inc(xn_done, 1)

            def scaled(name, t, scale, shift, dst):
                for half in range(2):
                    k = tile_job(name, t) + half
                    dve.wait_ge(tp_done, k + 1)
                    if k in SPLIT:
                        at_least(dve, lo_done, SPLIT[k] - 1)
                    for m in range(4):
                        f = 4 * half + m
                        ins = v.tensor_scalar(dst(k, half)[:, m * P:(m + 1) * P], tp[k % 2][:, m * P:(m + 1) * P],
                                              scale[:, f:f + 1], None if shift is None else shift[:, f:f + 1],
                                              ALU.mult, *(() if shift is None else (ALU.add,)))
                    ins.then_inc(sem(RELEASE[k][0]), 1)

            def norm_jobs(name, t, scale, shift=None):
                scaled(name, t, scale, shift, lambda k, half: hb[:, k % 2, :])
                for half in range(2):
                    k = tile_job(name, t) + half
                    dve.wait_ge(norm_read, RELEASE[k][1])
                    dve.wait_ge(t_hi, SPLIT[k] + 1)
                    where = (slice(None), slice(4 * half, 4 * half + 4), slice(t * P, (t + 1) * P))
                    v.tensor_tensor(ht[1][where], hb[:, k % 2, :].rearrange("p (k s) -> p k s", k=4), ht32[where],
                                    ALU.subtract).then_inc(lo_done, 1)

            def lo(k, dst, hi32, src, i=None):
                at_least(dve, t_hi, SPLIT[k] + 1, 2, i)
                v.tensor_tensor(dst, src, hi32, ALU.subtract).then_inc(lo_done, 1)

            def turned(k, dst, hi32, q, t):
                where = (slice(None), slice(4 * q, 4 * q + 4), slice(t * P, (t + 1) * P))
                lo(k, dst[1][where], hi32[where], tp[k % 2][:].rearrange("p (k s) -> p k s", k=4))

            def turned_tile(name, dst, hi32, t):
                for q in range(2):
                    turned(JOB[name] + 2 * t + q, dst, hi32, q, t)

            def post(q, t, use, row):
                mean_square(q)
                p = (use + t) % 2
                v.scalar_tensor_tensor(out=two(xn[:, t, :]), in0=pair[p][:], scalar=st[:, q, 2, 0:1], in1=two(row),
                                       op0=ALU.mult, op1=ALU.mult).then_inc(evac[p], 1)
                wait_evac(dve, use + t)
                v.tensor_tensor(xres[:, t, :], xres[:, t, :], xn[:, t, :], ALU.add).then_inc(x_ready, 1)

            def gated_post(t, use, w, halves, row, rows):
                ready(use, t, w, halves)
                dve.wait_ge(sem("row_copied"), rows)
                p = (use + t) % 2
                v.tensor_tensor(two(xn[:, t, :]), pair[p][:], two(row), ALU.mult).then_inc(evac[p], 1)
                wait_evac(dve, use + t)
                v.tensor_tensor(xres[:, t, :], xres[:, t, :], xn[:, t, :], ALU.add).then_inc(x_ready, 1)

            def mod_columns(a, b, used):
                dve.wait_ge(ada_used, used)
                link(v.tensor_tensor(mod[:, a:b], adap[:, a:b], colv("b_ada", a, b - a), ALU.add))

            def mod_scale(n, at_col, gain):
                link(v.scalar_tensor_tensor(out=moda[:, n, :], in0=mod[:, at_col:at_col + 8], scalar=1.0, in1=gain,
                                            op0=ALU.add, op1=ALU.mult))

            def gate_diagonals(at_col, read=None):
                if read is not None:
                    dve.wait_ge(tp_done, read)
                for m in range(KT):
                    ins = v.tensor_scalar(dg[:, m, :], idn[:], mod[:, at_col + m:at_col + m + 1], None, ALU.mult)
                ins.then_inc(dg_done, 1)

            def ffn(name, jobs):
                w, use, k, n0 = W0[name], USE[name], JOB[jobs], GROUPS * int(name[-1])

                def group(j, use, i=None):
                    for t in range(TT):
                        at_least(dve, silu_done, 2 * (n0 + j) + t + 1, 4, i)
                        ins = v.tensor_tensor(prod[:, j % 2, t, :], prod[:, j % 2, t, :], pair[use % 2][:, t, 256:512], ALU.mult)
                    ins.then_inc(evac[use % 2], 1)

                def hidden_lo(j, k, i=None):
                    where = slice(2 * j, 2 * j + 2) if i is None else bass.ds(i * 4 + 2 * j, 2)
                    lo(k, gt[1][:, where, :], gt32[:, where, :], tp[k % 2][:].rearrange("p (a b) -> p a b", a=2), i)

                for j in range(PEELED):
                    group(j, use + j)
                    if j:
                        hidden_lo(j - 1, k + j - 1)
                    tick(w + 2 * j)
                    tick(w + 2 * j + 1)
                with dve.Fori(0, (GROUPS - PEELED) // 2) as i:
                    for n in range(2):
                        j = PEELED + n
                        ada(ADA_AT[w + 2 * j - 1], i)
                        group(j, use + j, i)
                        hidden_lo(j - 1, k + j - 1, i)
                        tick(w + 2 * j, i)
                        tick(w + 2 * j + 1, i)
                hidden_lo(GROUPS - 1, k + GROUPS - 1)

            def head_gates(half):
                q, f, b = ("qa", "fa", "ba") if half == 0 else ("qb", "fb", "bb")
                for name, d, fx, kx in ((f, 0, tf, kf), (b, 1, tb, kb)):
                    tick(W0[name]) if name == f else None
                    wait_evac(dve, USE[name])
                    for hd in range(HH):
                        n = 8 * d + HH * half + hd
                        v.tensor_scalar(kx[:, hd, :], kx[:, hd, :], lbt[:, 0, n:n + 1], None, ALU.mult)
                        ins = v.tensor_scalar(fx[:, hd, :], fx[:, hd, :], lbt[:, 0, n:n + 1], lbt[:, 4, n:n + 1],
                                              ALU.mult, ALU.add)
                    link(ins)
                    link(v.tensor_scalar(fx[:], fx[:], TINY, None, ALU.max))
                    if name == f:
                        tick(W0[f] + 1)
                        tick(W0[b])
                if half:
                    dve.wait_ge(tp_done, JOB["pa"] + 16)
                v.tensor_tensor(sk[:], kf[:], kb[:], ALU.add).then_inc(hg_sk0, 1)
                dve.wait_ge(hg_staged, 8 * half + 1)
                link(v.tensor_tensor(qb[:], qf[:], tb[:], ALU.mult))
                v.tensor_tensor(qf[:], qf[:], tf[:], ALU.mult).then_inc(hg_qupd, 1)
                tick(W0[b] + 1)

            def query_updates(half, lv):
                h = 1 << (lv - 1)
                nb = HH * S // (2 * h)
                qa, qc, fa, fc = [a[:].rearrange("p a (b two h) -> p (a b) two h", two=2, h=h) for a in (qf, qb, tf, tb)]
                dve.wait_ge(hg_qupd, 8 * half + lv)
                dve.wait_ge(hg_staged, 8 * half + lv + 1)
                if lv > 1:
                    dve.wait_ge(hg_tot, 6 * half + lv - 1)
                v.tensor_tensor(qa[:, :, 1, :], qa[:, :, 1, :], fa[:, :, 0, 0:1].to_broadcast([P, nb, h]), ALU.mult)
                v.tensor_tensor(qc[:, :, 0, :], qc[:, :, 0, :], fc[:, :, 1, 0:1].to_broadcast([P, nb, h]),
                                ALU.mult).then_inc(hg_qupd, 1)
                if lv < 7:
                    dve.wait_ge(hg_kupd, 7 * half + lv)
                    dve.wait_ge(hg_qupd, 8 * half + lv + 1)
                    v.tensor_tensor(fa[:, :, 0, 0:1], fa[:, :, 0, 0:1], fa[:, :, 1, 0:1], ALU.mult)
                    v.tensor_tensor(fc[:, :, 0, 0:1], fc[:, :, 0, 0:1], fc[:, :, 1, 0:1], ALU.mult).then_inc(hg_tot, 1)

            def take_scores(half, lv):
                for s in range(2):
                    k = JOB["pa" if half == 0 else "pb"] + 2 * lv + s
                    dve.wait_ge(tp_done, k + 1)
                    n = RELEASE[k][1]
                    if n > 2:
                        dve.wait_ge(sem("p_copied"), n - 2)
                    v.copy_predicated(at[:, s, :, s * P:(s + 1) * P], msk[:, lv:lv + 1, :].to_broadcast([P, HH, P]),
                                      tp[k % 2][:].rearrange("p (a b) -> p a b", a=HH)).then_inc(sem("p_copied"), 1)

            def head_outputs(half, t):
                k, q = JOB["pva" if half == 0 else "pvb"] + t, RQ["pva" if half == 0 else "pvb"] + t
                dve.wait_ge(pv_sq, 2 * half + t + 1)
                link(v.tensor_reduce(st[:, q, 0, :], osq[:, t, :].rearrange("p (a b) -> p a b", a=HH), AX.X, ALU.add))
                v.tensor_scalar(st[:, q, 1, :], st[:, q, 0, :], 1.0 / P, EPS, ALU.mult, ALU.add).then_inc(ms_done, 1)
                dve.wait_ge(rstd_done, q + 1)
                at_least(dve, a_out, 2 * half + t)
                v.tensor_tensor(on[:, t, :].rearrange("p (a b) -> p a b", a=HH),
                                tp[k % 2][:].rearrange("p (a b) -> p a b", a=HH),
                                st[:, q, 2, :].unsqueeze(2).to_broadcast([P, HH, P]), ALU.mult).then_inc(sem("pv_read"), 1)
                dve.wait_ge(sem("pv_read"), 2 * half + t + 1)
                link(v.tensor_tensor(on[:, t, :], on[:, t, :], hgrow[:, half, :], ALU.mult))
                z = zg[:, t, half * 512:(half + 1) * 512]
                v.tensor_tensor(z, z, on[:, t, :], ALU.mult).then_inc(a_out, 1)

            for t in range(TT):
                norm(RQ["norm0"] + t, t)
            dve.wait_ge(small_in, 32)
            norm_jobs("norm0", 0, colv("mix_pre", 0, 8))
            split_lo(0)
            split_lo(1)
            norm_jobs("norm0", 1, colv("mix_pre", 0, 8))
            split_lo(2)
            split_lo(3)
            gamma = colv("gamma", 0, 16)
            v.tensor_tensor(lbt[:, 0, :], gamma, gamma, ALU.subtract).then_inc(lb_e, 1)
            dve.wait_ge(lb_e, 2)
            link(v.reciprocal(lbt[:, 2, :], lbt[:, 1, :]))
            link(v.tensor_tensor(lbt[:, 3, :], lbt[:, 1, :], lbt[:, 2, :], ALU.mult))
            link(v.tensor_tensor(lbt[:, 4, :], lbt[:, 3, :], lbt[:, 3, :], ALU.subtract))
            link(v.tensor_scalar(lbt[:, 0, :], lbt[:, 4, :], -1.0, 1.0, ALU.mult, ALU.add))
            dve.wait_ge(ca_done, 1)
            for w in range(3):
                tick(w)
            wait_evac(dve, USE["zv"])
            dve.wait_ge(sgu_in, 48)
            for t in range(TT):
                link(v.bn_stats(bn[:, t, :], vg[:, t, :]))
                link(v.bn_aggr(mv[:, t, :], bn[:, t, :]))
                q = RQ["ln"] + t
                v.tensor_scalar(st[:, q, 1, 0:1], mv[:, t, 1:2], EPS, None, ALU.add).then_inc(ms_done, 1)
                dve.wait_ge(rstd_done, q + 1)
                link(v.tensor_scalar(vg[:, t, :], vg[:, t, :], mv[:, t, 0:1], st[:, q, 2, 0:1], ALU.subtract, ALU.mult))
                link(v.tensor_tensor(vg[:, t, :], vg[:, t, :], lnrow[:, 0, :], ALU.mult))
                v.tensor_tensor(vg[:, t, :], vg[:, t, :], lnrow[:, 1, :], ALU.add).then_inc(ln_done, 1)
            for w in range(3, 6):
                tick(w)

            def gate_positions():
                for t in range(TT):
                    k = JOB["sgu"] + t
                    dve.wait_ge(tp_done, k + 1)
                    v.tensor_tensor(vg[:, t, :].rearrange("p (a b) -> p a b", a=8), tp[k % 2][:].rearrange("p (a b) -> p a b", a=8),
                                    colv("sg_b", 0, 8).unsqueeze(2).to_broadcast([P, 8, 64]), ALU.add).then_inc(sem("sgu_read"), 1)
                    dve.wait_ge(sem("sgu_read"), t + 1)
                    v.tensor_tensor(u[:, t, :], u[:, t, :], vg[:, t, :], ALU.mult).then_inc(b_out, 1)

            head_gates(0)
            gate_positions()
            dve.wait_ge(hg_in, 32)
            link(v.tensor_copy(msk[:], mskf[:]))
            for lv in range(8):
                tick(W0["zi"] + lv)
                take_scores(0, lv)
                if lv < 7:
                    query_updates(0, lv + 1)
            tick(W0["qb"])
            tick(W0["qb"] + 1)
            for t in range(TT):
                head_outputs(0, t)
            head_gates(1)
            for t in range(TT):
                k = JOB["tb"] + t
                lo(k, bt[1][:, t, :], as_f32(bt[0][:, t, :]), tp[k % 2][:])
            for lv in range(8):
                tick(W0["ga"] + lv)
                take_scores(1, lv)
                if lv < 7:
                    query_updates(1, lv + 1)

            def gated_b(t):
                ready(USE["wb"], t, W0["wb"] + 1, 1)
                wait_evac(dve, USE["gb"] + 1)
                v.tensor_tensor(two(gb[:, t, :]), two(gb[:, t, :]), pair[(USE["wb"] + t) % 2][:],
                                ALU.mult).then_inc(evac[(USE["wb"] + t) % 2], 1)

            def merge(t):
                ready(USE["wa"], t, W0["wa"] + 3, 2)
                p = (USE["wa"] + t) % 2
                v.tensor_tensor(two(ga[:, t, :]), two(ga[:, t, :]), pair[p][:], ALU.mult).then_inc(evac[p], 1)
                wait_evac(dve, USE["wa"] + t)
                v.tensor_tensor(ga[:, t, :], ga[:, t, :], gb[:, t, :], ALU.add).then_inc(merged, 1)

            gated_b(0)
            head_outputs(1, 0)
            tick(W0["wb"])
            head_outputs(1, 1)
            gated_b(1)
            turned_tile("ta", gt, gt32, 0)
            tick(W0["wb"] + 1)
            turned_tile("ta", gt, gt32, 1)
            merge(0)
            tick(W0["wa"])
            turned_tile("tm", ht, ht32, 0)
            tick(W0["wa"] + 1)
            merge(1)
            tick(W0["wa"] + 2)
            turned_tile("tm", ht, ht32, 1)
            tick(W0["wa"] + 3)
            dve.wait_ge(prow_in, 16)
            w = W0["wout"]
            for t in range(TT):
                dve.wait_ge(x_again[t], 16)
                post(RQ["mix"] + 2 * t, t, USE["wout"], prow[:, 0, :])
                norm(RQ["mix"] + 2 * t + 1, t, w + 2 if t else None)
                norm_jobs("norm1", t, colv("ffn_pre", 0, 8))
                if t == 0:
                    tick(w)
                    tick(w + 1)
            tick(w + 3)
            ffn("ffn0", "h0")
            w = W0["down0"]
            for c in range(GROUPS - 4):
                tick(w + c)
                if c == 0:
                    dve.wait_ge(pt_hi, 1)
                    v.tensor_tensor(pt[1][:], praw[:], as_f32(pt[0][:]), ALU.subtract).then_inc(pt_done, 1)
            mod_columns(0, 48, 24)
            mod_scale(0, 8, colv("mix_g", 0, 8))
            mod_scale(1, 32, colv("ffn_g", 0, 8))
            gate_diagonals(16)
            post(RQ["ffn"], 0, USE["down0"], prow[:, 1, :])
            tick(w + GROUPS - 4)
            tick(w + GROUPS - 3)
            post(RQ["ffn"] + 1, 1, USE["down0"], prow[:, 1, :])
            tick(w + GROUPS - 2)
            tick(w + GROUPS - 1)
            turned_tile("tx", ht, ht32, 0)
            tick(W0["ple"])
            turned_tile("tx", ht, ht32, 1)
            dve.wait_ge(cs_hi, 1)
            v.tensor_tensor(cs[1][:], csr[:], as_f32(cs[0][:]), ALU.subtract).then_inc(cs_done, 1)
            w = W0["pleg"] + 3
            for t in range(TT):
                wait_evac(dve, USE["pleg"] + t)
                link(v.tensor_tensor(xn[:, t, :], xn[:, t, :], gsig[:, t, :], ALU.mult))
                v.tensor_tensor(xres[:, t, :], xres[:, t, :], xn[:, t, :], ALU.add).then_inc(x_ready, 1)
                norm(RQ["norm2"] + t, t, w - 1 if t else None)
                norm_jobs("norm2", t, moda[:, 0, :], mod[:, 0:8])
                if t == 0:
                    tick(w - 3)
                    tick(w - 2)
                for gr in range(4):
                    k = JOB["dft1b" if t else "dft1"] + gr
                    lo(k, tt[1][:, t, gr, :], tt32[:, t, gr, :], tp[k % 2][:])
            tick(w)
            for gr in range(4):
                k = JOB["dft2"] + gr
                lo(k, ht[1][:, 2 * gr:2 * gr + 2, :], ht32[:, 2 * gr:2 * gr + 2, :], tp[k % 2][:].rearrange("p (a b) -> p a b", a=2))
            gate_diagonals(40, JOB["rows0"] + 2)

            def boundary(w, use, halves, row, rows, q, name, scale, shift):
                gated_post(0, use, w, halves, row, rows)
                norm(q, 0)
                norm_jobs(name, 0, scale, shift)
                tick(w - 3)
                tick(w - 2)
                gated_post(1, use, w, halves, row, rows)
                norm(q + 1, 1, w - 1)
                norm_jobs(name, 1, scale, shift)
                tick(w)

            boundary(W0["fo"] + 3, USE["fo"], 7, grow[0][:], 2, RQ["norm3"], "norm3", moda[:, 1, :], mod[:, 24:32])
            ffn("ffn1", "h1")
            for w in range(W0["down1"], W0["down1"] + GROUPS - 4):
                tick(w)
            mod_columns(48, 72, 36)
            mod_scale(2, 56, colv("mix_g", 8, 8))
            gate_diagonals(64, JOB["rows1"] + 2)
            boundary(W0["down1"] + GROUPS - 1, USE["down1"], 8, grow[1][:], 4, RQ["norm4"], "norm4", moda[:, 2, :], mod[:, 48:56])
            for c in range(4):
                tick(W0["rva"] + c)
            dve.wait_ge(rot_in, 16)
            for n, name in enumerate(("rq", "rk")):
                dst = qr if n == 0 else kr
                for m in range(2):
                    tick(W0[name] + 2 * m)
                    use = USE[name] + m
                    dve.wait_ge(w_used, W0[name] + 2 * m + 2)
                    src = pair[use % 2][:].rearrange("p a (x s) -> p (a x) s", x=2)
                    if n or m:
                        dve.wait_ge(rot_done, 2 * n + m)
                    v.tensor_tensor(rab[:, 0, :, :], src, rt[:, 0:1, :].to_broadcast([P, 4, S]), ALU.mult)
                    v.tensor_tensor(rab[:, 1, :, :], src, rt[:, 1:2, :].to_broadcast([P, 4, S]), ALU.mult).then_inc(evac[use % 2], 1)
                    wait_evac(dve, use)
                    c, d = [rab[:, y, :, :].rearrange("p (a x) s -> p a x s", x=2) for y in range(2)]
                    v.tensor_tensor(dst[:, 2 * m:2 * m + 2, 0, :], c[:, :, 0, :], d[:, :, 1, :], ALU.subtract)
                    v.tensor_tensor(dst[:, 2 * m:2 * m + 2, 1, :], d[:, :, 0, :], c[:, :, 1, :], ALU.add).then_inc(rot_done, 1)
                    tick(W0[name] + 2 * m + 1)
            dve.wait_ge(decay_in, 16)
            for c in range(4):
                tick(W0["rvb"] + c)
                for hd in ((), (0,), (1, 2), (3,))[c]:
                    k = JOB["sc"] + hd
                    dve.wait_ge(tp_done, k + 1)
                    v.tensor_tensor(ar[:, hd, :, :], tp[k % 2][:].rearrange("p (a b) -> p a b", a=2), dt[:, hd, :, :],
                                    ALU.mult).then_inc(sem("sc_read"), 1)

            def gated_head(hd):
                dve.wait_ge(sem("av_read"), 2 * hd + 2)
                wait_evac(dve, USE["rg"] + hd)
                for t in range(TT):
                    z = gg[:, t, hd * RV:(hd + 1) * RV]
                    ins = v.tensor_tensor(z, z, yr[t][:, hd * RV:(hd + 1) * RV], ALU.mult)
                ins.then_inc(y_done, 1)

            def head_los(hd):
                for t in range(TT):
                    turned(JOB["ty"] + 2 * hd + t, gt, gt32, hd, t)

            dve.wait_ge(sem("sc_read"), RH)
            for c in range(8):
                tick(W0["rg"] + c)
                if c < RH:
                    for t in range(TT):
                        k, q = JOB["av"] + 2 * c + t, RQ["av"] + 2 * c + t
                        dve.wait_ge(tp_done, k + 1)
                        link(v.bn_stats(bn[:, t, :], tp[k % 2][:]))
                        link(v.bn_aggr(mv[:, t, :], bn[:, t, :]))
                        v.tensor_scalar(st[:, q, 1, 0:1], mv[:, t, 1:2], EPS, None, ALU.add).then_inc(ms_done, 1)
                        dve.wait_ge(rstd_done, q + 1)
                        v.tensor_scalar(yr[t][:, c * RV:(c + 1) * RV], tp[k % 2][:], mv[:, t, 0:1], st[:, q, 2, 0:1],
                                        ALU.subtract, ALU.mult).then_inc(sem("av_read"), 1)
                if c in (3, 4, 6):
                    gated_head((3, 4, 6).index(c))
                if c > 5:
                    head_los(c - 6)
            gated_head(3)
            head_los(2)
            tick(W0["ro"])
            head_los(3)
            for w in range(W0["ro"] + 1, W0["ro"] + 4):
                tick(w)
            mod_columns(72, 96, 48)
            mod_scale(3, 80, colv("ffn_g", 8, 8))
            boundary(W0["ro"] + 7, USE["ro"], 9, grow[0][:], 6, RQ["norm5"], "norm5", moda[:, 3, :], mod[:, 72:80])
            ffn("ffn2", "h2")
            tick(W0["down2"])
            mod_columns(96, 112, NADA)
            mod_scale(4, 104, colv("fin_g", 0, 8))
            gate_diagonals(88)
            for w in range(W0["down2"] + 1, W0["down2"] + GROUPS - 1):
                tick(w)
            for t in range(TT):
                gated_post(t, USE["down2"], W0["down2"] + GROUPS - 1, 10, grow[1][:], 8)
                norm(RQ["norm6"] + t, t)
                scaled("norm6", t, moda[:, 4, :], mod[:, 96:104], lambda k, half: outb[:, k - JOB["norm6"], :])


def kernel(**inputs):
    import numpy as np
    import concourse.bacc as bacc
    from concourse.bass_utils import run_bass_kernel_spmd

    def get(name):
        return np.ascontiguousarray(inputs[name])

    def deep(w, n):
        k, cols = w.shape
        kt = 2048 // n
        a = w.reshape(k // (kt * P), kt, P, cols // n, n)
        return a.transpose(3, 0, 2, 1, 4).reshape(-1, P, 2048)

    def gate_up(wg, wu):
        a = np.stack([wg.reshape(D, GROUPS, 256), wu.reshape(D, GROUPS, 256)], axis=2)
        return deep(a.reshape(D, GROUPS * 512), 512)

    def outer(w):
        return w.reshape(-1, 2, P, D).transpose(0, 2, 1, 3).reshape(-1, P, 2048)

    w_in = get("w_in")[0]
    z = {}
    off = 0
    for name, n in (("q", 1024), ("f", 1024), ("b", 1024), ("zi", 1024), ("zg", 1024), ("zu", 512), ("zv", 512),
                    ("ga", 1024), ("gb", 1024)):
        z[name] = w_in[:, off:off + n]
        off += n
    ri, fi, fo = get("w_ret_in_2")[0], get("w_ffn_in_2"), get("w_ffn_out_2")
    parts = {
        "zu": deep(z["zu"], 512), "zv": deep(z["zv"], 512),
        "zi": deep(z["zi"], 512), "zg": deep(z["zg"], 512), "ga": deep(z["ga"], 512), "gb": deep(z["gb"], 512),
        "wa": outer(get("w_a")[0]), "wb": outer(get("w_b")[0]), "wout": outer(get("w_out")[0]),
        "ffn0": gate_up(get("w_gate")[0], get("w_up")[0]), "down0": outer(get("w_down")[0]),
        "ple": outer(get("w_ple")[0]), "pleg": outer(get("w_ple_gate")[0]), "fo": outer(get("w_fourier_out_2")[0]),
        "ffn1": gate_up(fi[0][:, :FF], fi[0][:, FF:]), "down1": outer(fo[0]),
        "rq": deep(ri[:, 0:1024], 256), "rk": deep(ri[:, 1024:2048], 256),
        "rva": deep(ri[:, 2048:3072], 512), "rvb": deep(ri[:, 3072:4096], 512), "rg": deep(ri[:, 4096:6144], 512), "ro": outer(get("w_ret_out_2")[0]),
        "ffn2": gate_up(fi[1][:, :FF], fi[1][:, FF:]), "down2": outer(fo[1]),
    }
    for half, h in enumerate("ab"):
        for name in "qfb":
            parts[name + h] = deep(z[name][:, 512 * half:512 * half + 512], 256)
    weights = [c for name, n in STAGES for c in parts[name]]
    wada = get("w_ada_2")
    adas = [c for w in (wada[0], wada[1], get("w_ada_final_2")) for c in deep(w, 256)]
    stream = np.stack([(weights if kind == "w" else adas)[n] for kind, n in ORDER])

    def columns(a):
        return a.reshape(-1, P).T

    table = np.concatenate([columns(get(n).reshape(-1)) for n in (
        "norm_mix_pre", "norm_ffn_pre", "norm_mix_g_2", "norm_ffn_g_2", "final_norm_g_2", "c_2", "lb_gamma_fwd",
        "lb_gamma_bwd", "sg_b", "b_ada_2", "b_ada_final_2")], axis=1)
    rows = np.stack([np.concatenate([get("sg_ln_g")[0], get("sg_ln_b")[0]]), get("hg_norm")[0],
                     get("norm_mix_post")[0], get("norm_ffn_post")[0]])

    f32 = np.float32
    n = np.arange(P)
    masks = [n[:, None] == n[None, :]]
    for lv in range(7):
        h = 1 << lv
        masks.append((n[:, None] // (2 * h) == n[None, :] // (2 * h)) & (n[:, None] // h != n[None, :] // h))
    masks = np.stack(masks, axis=1).astype(np.float32)
    m = np.arange(S)
    ang = 2.0 * np.pi * ((m[:, None] * m[None, :]) % S) / S
    dft = np.concatenate([np.cos(ang), np.sin(ang), -np.sin(ang)], axis=1) / 16.0
    dft = dft.astype(f32).reshape(2, P, 768).transpose(1, 0, 2)
    freq = (f32(10000.0) ** (-np.arange(P, dtype=f32) / f32(P))).astype(f32)
    rang = (freq[:, None] * m[None, :].astype(f32)).astype(f32).astype(np.float64)
    rot = np.stack([np.cos(rang), np.sin(rang)], axis=1).astype(f32)
    lg = np.log1p(-np.exp2(-5.0 - np.arange(RH)))
    d = m[None, :] - m[:, None]
    decay = np.stack([np.where(d >= 0, np.exp(np.maximum(d, 0) * lg[h]), np.exp(np.maximum(-d, 0) * lg[RH - 1 - h]))
                      for h in range(RH)]) / 16.0
    decay = decay.astype(f32).reshape(RH, 2, P, S).transpose(2, 0, 1, 3)

    arrays = {
        "stream": stream,
        "x": get("x")[0].reshape(TT, P, D).transpose(1, 0, 2),
        "pT": get("p")[0, 0].T.reshape(2, P, S).transpose(1, 0, 2),
        "cols": table, "rows": rows,
        "sg_wT": get("sg_w")[0].transpose(2, 0, 1),
        "masks": masks, "ident": np.eye(P, dtype=f32), "dft": dft, "rot": rot, "decay": decay,
    }
    nc = bacc.Bacc("TRN2", target_bir_lowering=False, num_devices=1)
    args = []
    for name, a in arrays.items():
        arrays[name] = a = np.ascontiguousarray(a)
        args.append(nc.dram_tensor(name, a.shape, mybir.dt.from_np(a.dtype), kind="ExternalInput").ap())
    args.append(nc.dram_tensor("outT", (KT, P, S), F32, kind="ExternalOutput").ap())
    program(nc, *args)
    r = run_bass_kernel_spmd(nc, [arrays], core_ids=[0])
    return np.ascontiguousarray(r.results[0]["outT"].reshape(D, S).T).reshape(1, S, D)
```

```python
from contextlib import ExitStack

import concourse.bass as bass
from concourse import mybir

F32 = mybir.dt.float32
F32R = mybir.dt.float32r
U8 = mybir.dt.uint8
ALU = mybir.AluOpType
ACT = mybir.ActivationFunctionType
AX = mybir.AxisListType

P = 128
S = 256
TT = S // P
D = 1024
KT = D // P
FF = 2816
FT = FF // P
HEADS = 8
HH = HEADS // 2
RH = 4
RV = 512
EPS = 1e-6
TINY = 1.1754943508222875e-38

WARM = 18
RAW = 3
WS = 4
GROUPS = FT // 2

STAGES = [("zu", 2), ("zv", 2), ("qa", 2), ("fa", 2), ("ba", 2), ("zi", 4), ("zg", 4),
          ("qb", 2), ("fb", 2), ("bb", 2), ("ga", 4), ("gb", 4), ("wb", 2), ("wa", 4),
          ("wout", 4), ("ffn0", 2 * GROUPS), ("down0", GROUPS), ("ple", 1), ("pleg", 4),
          ("fo", 4), ("ffn1", 2 * GROUPS), ("down1", GROUPS), ("rva", 4), ("rq", 4), ("rk", 4), ("rvb", 4),
          ("rg", 8), ("ro", 8), ("ffn2", 2 * GROUPS), ("down2", GROUPS)]
W0 = {}
NW = 0
for _name, _n in STAGES:
    W0[_name] = NW
    NW += _n

WIDE = 2
PEELED = 3

NADA = 56


def ffn_adas(name):
    return [W0[name] + 2 * j - 1 for j in range(WIDE, GROUPS)]


ADA_TICKS = [0, 1, 2, 5, 17, 18, 20, 31, 33]
ADA_TICKS += ffn_adas("ffn0") + [W0["down0"] + j for j in (1, 3, 5)]
ADA_TICKS += ffn_adas("ffn1") + [W0["down1"] + j for j in (1, 3)]
ADA_TICKS += [W0["rva"] + 1, W0["rva"] + 3, W0["rq"] + 1, W0["rq"] + 3, W0["rk"], W0["rvb"], W0["rvb"] + 2]
ADA_TICKS += [W0["rg"] + 5, W0["rg"] + 7] + [W0["ro"] + j for j in range(3)]
ADA_TICKS += ffn_adas("ffn2") + [W0["down2"] + j for j in (2, 4, 6)]
assert len(ADA_TICKS) == NADA
ADA_AT = {w: a for a, w in enumerate(ADA_TICKS)}
ADA_STATIC = {w: a for w, a in ADA_AT.items() if not any(w in ffn_adas(f) for f in ("ffn0", "ffn1", "ffn2"))}


NORMED = {"norm1": W0["wout"] + 3, "norm3": W0["fo"] + 3, "norm4": W0["down1"] + GROUPS - 1, "norm5": W0["ro"] + 7}
POOL_LO = [w + 1 + j for name, w in NORMED.items() for j in range(1 if name == "norm1" else 2)]


def stream_order():
    order = [("w", w) for w in range(WS)]
    for w in range(NW):
        if w + WS < NW:
            order.append(("w", w + WS))
        if w in ADA_AT:
            order.append(("a", ADA_AT[w]))
    return order


ORDER = stream_order()
AT_RAW = {c: n for n, c in enumerate(ORDER)}
NRAW = len(ORDER)

COLS = {}
NCOL = 0
for _name, _n in [("mix_pre", 8), ("ffn_pre", 8), ("mix_g", 16), ("ffn_g", 16), ("fin_g", 8),
                  ("c", 8), ("gamma", 16), ("sg_b", 8), ("b_ada", 112)]:
    COLS[_name] = NCOL
    NCOL += _n


def plan_psum():
    use, u = {}, 0
    for name, n in [("zu", 1), ("zv", 1), ("qa", 1), ("fa", 1), ("ba", 1), ("zi", 2), ("zg", 2),
                    ("qb", 1), ("fb", 1), ("bb", 1), ("ga", 2), ("gb", 2), ("wb", 2), ("wa", 2),
                    ("wout", 2), ("ffn0", GROUPS), ("down0", 2), ("ple", 2), ("pleg", 2),
                    ("fo", 2), ("ffn1", GROUPS), ("down1", 2), ("rva", 2), ("rq", 2), ("rk", 2), ("rvb", 2),
                    ("rg", 4), ("ro", 2), ("ffn2", GROUPS), ("down2", 2)]:
        use[name] = u
        u += n
    jobs, release, split, counts, splits, k = {}, [], {}, {}, 0, 0
    table = [("norm0", 4, "norm"), ("sgu", 2, "sgu_read"), ("pa", 16, "p_copied"),
             ("offa", 2, "off_copied"), ("pva", 2, "pv_read"), ("tb", 2, "split"), ("pb", 16, "p_copied"),
             ("offb", 2, "off_copied"), ("pvb", 2, "pv_read"), ("ta", 4, "split"),
             ("tm", 4, "split"), ("norm1", 4, "norm"),
             ("h0", WIDE, "split"), ("tx", 4, "split"),
             ("norm2", 2, "norm"), ("dft1", 4, "split"),
             ("rows0", 2, "row_copied"), ("norm2b", 2, "norm"), ("dft1b", 4, "split"), ("dft2", 4, "split"),
             ("norm3", 4, "norm"), ("h1", WIDE, "split"), ("rows1", 2, "row_copied"),
             ("norm4", 4, "norm"), ("sc", 4, "sc_read"), ("rows2", 2, "row_copied"),
             ("av", 8, "av_read"), ("ty", 8, "split"), ("norm5", 4, "norm"),
             ("h2", WIDE, "split"), ("rows3", 2, "row_copied"), ("norm6", 4, "fin_read")]
    for name, n, kind in table:
        jobs[name] = k
        for _ in range(n):
            if kind in ("norm", "split"):
                split[k] = splits
                splits += 1
            sem = {"norm": "norm_read", "split": "lo_done"}.get(kind, kind)
            if kind == "split":
                release.append((sem, splits))
            else:
                counts[sem] = counts.get(sem, 0) + 1
                release.append((sem, counts[sem]))
            k += 1
    return use, jobs, release, split


USE, JOB, RELEASE, SPLIT = plan_psum()


def tile_job(name, t):
    return JOB["norm2b"] if name == "norm2" and t else JOB[name] + 2 * t


RQ = {}
NRQ = 0
for _name, _n in [("norm0", 2), ("ln", 2), ("pva", 2), ("pvb", 2), ("mix", 4), ("ffn", 2),
                  ("norm2", 2), ("norm3", 2), ("norm4", 2), ("av", 8), ("norm5", 2), ("norm6", 2)]:
    RQ[_name] = NRQ
    NRQ += _n
SS = {q: n + 1 for n, q in enumerate(RQ[name] + t for name, k in [
    ("norm0", 2), ("mix", 4), ("ffn", 2), ("norm2", 2), ("norm3", 2), ("norm4", 2), ("norm5", 2), ("norm6", 2)]
    for t in range(k))}


def program(nc, stream, x, pT, cols, rows, sg_wT, masks, ident, dft, rot, decay, outT):
    with ExitStack() as ctx:
        base = (nc.sbuf_base + 255) // 256 * 256

        def sb(name, kb, shape, dt=F32):
            return nc.alloc_sbuf_tensor_at(name, shape, dt, offset=int(base + kb * 1024))

        raw = sb("raw", 0, [P, RAW, 2048])
        w_hi = sb("w_hi", 24, [P, WS, 2048], F32R)
        w_lo = sb("w_lo", 56, [P, WS, 2048], F32R)
        ht = [sb("ht_hi", 96, [P, KT, S], F32R), sb("ht_lo", 104, [P, KT, S], F32R)]
        gt = [sb("gt_hi", 112, [P, FT, S], F32R), sb("gt_lo", 134, [P, FT, S], F32R)]
        xres = sb("xres", 156, [P, TT, D])
        xn = sb("xn", 164, [P, TT, D])
        idn = sb("idn", 172, [P, P])
        ones = sb("ones", 172.5, [P, P])
        col = sb("col", 173, [P, NCOL])
        mod = sb("mod", 173.875, [P, 112])
        moda = sb("moda", 174.375, [P, 5, 8])
        ca = sb("ca", 174.625, [P, 8])
        lbt = sb("lbt", 174.75, [P, 5, 16])
        expo = sb("expo", 175.125, [P, 4])
        st = sb("st", 175.25, [P, NRQ, 3, 4])
        bn = sb("bn", 177, [P, 2, 6])
        mv = sb("mv", 177.125, [P, 2, 2])
        acc = sb("acc", 177.25, [P, 2, 2, 256])
        hb = sb("hb", 181.25, [P, 2, 512])
        ga = sb("ga", 156, [P, TT, D])
        gb = sb("gb", 193.25, [P, TT, D])
        vv = sb("vv", 164, [P, TT, D])
        zg = sb("zg", 185.25, [P, TT, D])
        hgrow = sb("hgrow", 201.25, [P, 2, 512])
        msk = sb("msk", 205.25, [P, 8, P], U8)
        sgw = sb("sgw", 185.25, [P, HEADS, P])
        vg = sb("vg", 189.25, [P, TT, 512])
        lnrow = sb("lnrow", 193.25, [P, 2, 512])
        qf = sb("qf", 112, [P, HH, S])
        qb = sb("qb", 116, [P, HH, S])
        kf = sb("kf", 120, [P, HH, S])
        kb = sb("kb", 124, [P, HH, S])
        tf = sb("tf", 128, [P, HH, S])
        tb = sb("tb", 132, [P, HH, S])
        sq = sb("sq", 136, [P, HH, S])
        sk = sb("sk", 140, [P, HH, S])
        at = sb("at", 144, [P, 2, HH, S])
        u = sb("u", 152, [P, TT, 512])
        bt = [sb("bt_hi", 181.25, [P, TT, 512], F32R), sb("bt_lo", 152, [P, TT, 512], F32R)]
        mskf = sb("mskf", 88, [P, 8, P])
        osq = sb("osq", 88, [P, TT, 512])
        on = sb("on", 92, [P, TT, 512])
        prow = sb("prow", 185.25, [P, 2, D])
        praw = sb("praw", 193.25, [P, 2, S])
        pt = [sb("pt_hi", 195.25, [P, 2, S], F32R), sb("pt_lo", 197.25, [P, 2, S], F32R)]
        dg = sb("dg", 88, [P, KT, P])
        dgb = sb("dgb", 185.25, [P, KT, P])
        prod = sb("prod", 92, [P, 2, TT, 256])
        csr = sb("csr", 112, [P, 2, 768])
        cs = [sb("cs_hi", 185.25, [P, 2, 768], F32R), sb("cs_lo", 191.25, [P, 2, 768], F32R)]
        grow = [sb("grow0", 201.25, [P, D]), sb("grow1", 197.25, [P, D])]
        tt = [sb("tt_hi", 112, [P, TT, 4, 512], F32R), sb("tt_lo", 134, [P, TT, 4, 512], F32R)]
        qr = sb("qr", 112, [P, RH, 2, S])
        kr = sb("kr", 120, [P, RH, 2, S])
        vr = sb("vr", 128, [P, TT, RH * RV])
        ar = sb("ar", 144, [P, RH, 2, S])
        yr = [sb("yr0", 164, [P, RH * RV]), sb("yr1", 88, [P, RH * RV])]
        gg = sb("gg", 185.25, [P, TT, RH * RV])
        dt = sb("dt", 88, [P, RH, 2, S])
        rt = sb("rt", 205.25, [P, 2, S])
        rab = sb("rab", 164, [P, 2, 4, S])
        gsig = sb("gsig", 118, [P, TT, D])
        outb = sb("outb", 185.25, [P, 4, 512])

        pair = [ctx.enter_context(nc.psum_tensor(f"pair{i}", [P, 2, 512], F32)) for i in range(2)]
        tp = [ctx.enter_context(nc.psum_tensor(f"tp{i}", [P, 512], F32)) for i in range(2)]
        adap = ctx.enter_context(nc.psum_tensor("adap", [P, 512], F32))

        sems = {}

        def sem(name):
            if name not in sems:
                sems[name] = ctx.enter_context(nc.semaphore(name))
            return sems[name]

        landed = [sem(f"landed{i}") for i in range(RAW)]
        raw_done = sem("raw_done")
        hi_done = sem("hi_done")
        w_used = sem("w_used")
        half_ready = sem("half_ready")
        evac = [sem("evac0"), sem("evac1")]
        tp_done = sem("tp_done")
        t_hi = sem("t_hi")
        lo_done = sem("lo_done")
        norm_read = sem("norm_read")
        ada_step = sem("ada_step")
        ada_used = sem("ada_used")
        ss_done = sem("ss_done")
        ms_done = sem("ms_done")
        rstd_done = sem("rstd_done")
        xn_done = sem("xn_done")
        x_ready = sem("x_ready")
        x_in = [sem("x_in0"), sem("x_in1")]
        small_in = sem("small_in")
        sgu_in = sem("sgu_in")
        hg_in = sem("hg_in")
        x_again = [sem("x_again0"), sem("x_again1")]
        prow_in = sem("prow_in")
        p_in = sem("p_in")
        dft_in = sem("dft_in")
        rot_in = sem("rot_in")
        decay_in = sem("decay_in")
        out_done = sem("out_done")
        consts = sem("consts")
        hid_hi = sem("hid_hi")
        hid_done = sem("hid_done")
        zg_done = sem("zg_done")
        step = sem("step")
        a_step = sem("a_step")
        lb_e = sem("lb_e")
        ca_done = sem("ca_done")
        ln_done = sem("ln_done")
        hg_sk0 = sem("hg_sk0")
        hg_staged = sem("hg_staged")
        hg_qupd = sem("hg_qupd")
        hg_kupd = sem("hg_kupd")
        hg_tot = sem("hg_tot")
        pv_sq = sem("pv_sq")
        a_out = sem("a_out")
        b_out = sem("b_out")
        merged = sem("merged")
        silu_done = sem("silu_done")
        pt_hi = sem("pt_hi")
        pt_done = sem("pt_done")
        sig_done = sem("sig_done")
        cs_hi = sem("cs_hi")
        cs_done = sem("cs_done")
        dg_done = sem("dg_done")
        rot_done = sem("rot_done")
        y_done = sem("y_done")

        def colv(name, i, n=1):
            return col[:, COLS[name] + i:COLS[name] + i + n]

        def at_least(eng, s, value, per=0, i=None):
            if i is None or per == 0:
                if value > 0:
                    eng.wait_ge(s, value)
            else:
                assert value > 0
                eng.wait_ge(s, i * per + value)

        def wait_evac(eng, use, passes=None):
            at_least(eng, evac[use % 2], use // 2 + 1, 1, passes)

        block = ctx.enter_context(nc.Block())

        @block.sync
        def _(sp):
            sp.dma_start(xres[:, 0, :], x[:, 0, :]).then_inc(x_in[0], 16)
            sp.dma_start(idn[:], ident).then_inc(small_in, 16)
            sp.dma_start(col[:], cols).then_inc(small_in, 16)
            sp.dma_start(raw[:, 0, :], stream[0]).then_inc(landed[0], 16)
            sp.dma_start(xres[:, 1, :], x[:, 1, :]).then_inc(x_in[1], 16)
            for n in range(1, RAW):
                sp.dma_start(raw[:, n, :], stream[n]).then_inc(landed[n], 16)
            turns = NRAW // RAW
            with sp.Fori(1, turns) as i:
                for n in range(RAW):
                    sp.wait_ge(raw_done, i * RAW + (n + 1 - RAW))
                    sp.dma_start(raw[:, n, :], stream[i * RAW + n]).then_inc(landed[n], 16)
            for n in range(turns * RAW, NRAW):
                sp.wait_ge(raw_done, n + 1 - RAW)
                sp.dma_start(raw[:, n % RAW, :], stream[n]).then_inc(landed[n % RAW], 16)
            for j in range(4):
                t, half = j // 2, j % 2
                sp.wait_ge(sem("fin_read"), j + 1)
                dst = outT[4 * half:4 * half + 4, :, t * P:(t + 1) * P].rearrange("k p s -> p k s")
                sp.dma_start(dst, outb[:, j, :].rearrange("p (k s) -> p k s", k=4)).then_inc(out_done, 16)
            sp.wait_ge(out_done, 64)

        @block.gpsimd
        def _(pool):
            g = nc.gpsimd
            g.memset(ones[:], 1.0)
            g.memset(expo[:], -0.5).then_inc(consts, 1)
            pool.wait_ge(consts, 1)

            def rsqrt(q, n=1, w=1):
                for r in range(q, q + n):
                    pool.wait_ge(ms_done, r + 1)
                    g.tensor_tensor(st[:, r, 2, 0:w], st[:, r, 1, 0:w], expo[:, 0:w], ALU.pow).then_inc(rstd_done, 1)

            def key_updates(half):
                for lv in range(1, 8):
                    h = 1 << (lv - 1)
                    v = [a[:].rearrange("p a (b two h) -> p (a b) two h", two=2, h=h) for a in (kf, kb, tf, tb)]
                    nb = HH * S // (2 * h)
                    pool.wait_ge(hg_staged, 8 * half + lv + 1)
                    if lv == 1:
                        pool.wait_ge(hg_qupd, 8 * half + 1)
                    else:
                        pool.wait_ge(hg_tot, 6 * half + lv - 1)
                    g.tensor_tensor(v[0][:, :, 0, :], v[0][:, :, 0, :], v[2][:, :, 1, 0:1].to_broadcast([P, nb, h]), ALU.mult)
                    g.tensor_tensor(v[1][:, :, 1, :], v[1][:, :, 1, :], v[3][:, :, 0, 0:1].to_broadcast([P, nb, h]), ALU.mult).then_inc(hg_kupd, 1)

            def split_los(w):
                for c in [c for c in (w + 1, w + 2) if c in POOL_LO]:
                    n = AT_RAW["w", c]
                    pool.wait_ge(hi_done, c + 1)
                    pool.wait_ge(raw_done, n)
                    g.tensor_tensor(w_lo[:, c % WS, :], raw[:, n % RAW, :], w_hi[:, c % WS, :].bitcast(F32),
                                    ALU.subtract).then_inc(raw_done, 1)

            def norm_rsqrts(name):
                rsqrt(RQ[name])
                split_los(NORMED[name])
                rsqrt(RQ[name] + 1)

            rsqrt(RQ["norm0"], 2)
            pool.wait_ge(hi_done, 2)
            pool.dma_start(sgw[:], sg_wT).then_inc(sgu_in, 16)
            pool.dma_start(lnrow[:, 0, :], rows[0:1, 0:512].to_broadcast([P, 512])).then_inc(sgu_in, 16)
            pool.dma_start(lnrow[:, 1, :], rows[0:1, 512:1024].to_broadcast([P, 512])).then_inc(sgu_in, 16)
            pool.dma_start(hgrow[:].rearrange("p a b -> p (a b)"), rows[1:2, :].to_broadcast([P, D])).then_inc(hg_in, 16)
            pool.dma_start(mskf[:], masks).then_inc(hg_in, 16)
            rsqrt(RQ["ln"], 2)
            key_updates(0)
            for half in range(2):
                wait_evac(pool, USE["zg"] + half)
                if half == 0:
                    pool.wait_ge(hg_in, 32)
                z = zg[:, :, half * 512:(half + 1) * 512]
                g.tensor_tensor(z, z, hgrow[:, half:half + 1, :].to_broadcast([P, TT, 512]), ALU.mult).then_inc(zg_done, 1)
            rsqrt(RQ["pva"], 2, 4)
            key_updates(1)
            rsqrt(RQ["pvb"], 2, 4)
            pool.wait_ge(tp_done, JOB["ta"] + 4)
            pool.dma_start(prow[:].rearrange("p a b -> p (a b)"),
                           rows[2:4, :].rearrange("(o a) b -> o (a b)", o=1).to_broadcast([P, 2 * D])).then_inc(prow_in, 16)
            for t in range(TT):
                pool.wait_ge(tp_done, JOB["tm"] + 2 * t + 2)
                pool.dma_start(xres[:, t, :], x[:, t, :]).then_inc(x_again[t], 16)
            pool.wait_ge(merged, 2)
            pool.dma_start(praw[:], pT).then_inc(p_in, 16)
            rsqrt(RQ["mix"], 2)
            split_los(NORMED["norm1"])
            rsqrt(RQ["mix"] + 2, 2)
            rsqrt(RQ["ffn"], 2)
            pool.wait_ge(w_used, W0["down0"] + GROUPS)
            pool.dma_start(csr[:], dft).then_inc(dft_in, 16)
            rsqrt(RQ["norm2"], 2)
            norm_rsqrts("norm3")
            pool.wait_ge(tp_done, JOB["rows1"] + 2)
            pool.dma_start(dt[:], decay).then_inc(decay_in, 16)
            pool.dma_start(rt[:], rot).then_inc(rot_in, 16)
            norm_rsqrts("norm4")
            rsqrt(RQ["av"], 8)
            norm_rsqrts("norm5")
            rsqrt(RQ["norm6"], 2)

        @block.tensor
        def _(pe):
            def passes(a, b):
                return [(a[1], b[0]), (a[0], b[0]), (a[0], b[1])]

            wsp = (w_hi, w_lo)

            def wait_chunk(w, i=None):
                at_least(pe, raw_done, AT_RAW["w", w] + 1, 6, i)

            def claim_pair(use, i=None):
                if use >= 2:
                    wait_evac(pe, use - 2, i)

            def claim(k):
                if k >= 2:
                    name, value = RELEASE[k - 2]
                    pe.wait_ge(sem(name), value)

            def wide_part(w, use, c, t):
                for k in range(4):
                    for n, (a, b) in enumerate(passes(ht, wsp)):
                        mm = pe.matmul(pair[use % 2][:, t, :], a[:, 4 * c + k, t * P:(t + 1) * P],
                                       b[:, w % WS, k * 512:(k + 1) * 512],
                                       start=(c == 0 and k == 0 and n == 0), stop=(c == 1 and k == 3 and n == 2))
                if t == TT - 1:
                    mm.then_inc(w_used, 1)

            def wide_chunk(w, use, c, i=None):
                wait_chunk(w, i)
                if c == 0:
                    claim_pair(use, i)
                for t in range(TT):
                    wide_part(w, use, c, t)

            def wide(w, use, i=None):
                for c in range(2):
                    wide_chunk(w + c, use, c, i)

            def feat(w, use, c, i=None):
                wait_chunk(w, i)
                if c == 0:
                    claim_pair(use, i)
                wv = [a[:, w % WS, :].rearrange("p (k n) -> p k n", k=KT) for a in wsp]
                for m in range(2):
                    for k in range(KT):
                        for n, (a, b) in enumerate(passes(wv, ht)):
                            mm = pe.matmul(pair[use % 2][:, c, m * S:(m + 1) * S], a[:, k, m * P:(m + 1) * P],
                                           b[:, k, :], start=(k == 0 and n == 0), stop=(k == KT - 1 and n == 2))
                mm.then_inc(w_used, 1)

            def turned_head(w, use, norm, split):
                wait_split(split, 2)
                for c in range(4):
                    wait_chunk(w + c)
                    if c % 2 == 0:
                        claim_pair(use + c // 2)
                    wide_part(w + c, use + c // 2, c % 2, 0)
                    if c == 2:
                        norm()
                wait_split(split, 4)
                for c in range(4):
                    wide_part(w + c, use + c // 2, c % 2, 1)

            def outer(w, n, use, src, k0=0, before={}, after={}):
                m = max(0, n - 4)
                order = [(c, t) for c in range(m) for t in range(TT)] + [(c, t) for t in range(TT) for c in range(m, n)]
                for c, t in order:
                    if (c, t) in before:
                        before[c, t]()
                    if t == 0:
                        wait_chunk(w + c)
                    if c == 0:
                        claim_pair(use + t)
                    for half in range(2):
                        for k in range(2):
                            for m, (a, b) in enumerate([(1, 0), (0, 0), (0, 1)]):
                                mm = pe.matmul(pair[(use + t) % 2][:, half, :], src(a, k0 + 2 * c + k, t),
                                               wsp[b][:, (w + c) % WS, k * D + half * 512:k * D + half * 512 + 512],
                                               start=(c == 0 and k == 0 and m == 0),
                                               stop=(c == n - 1 and k == 1 and m == 2))
                    if t == TT - 1:
                        mm.then_inc(w_used, 1)
                        ada_after(w + c)
                    elif c == n - 1:
                        mm.then_inc(half_ready, 1)
                    if (c, t) in after:
                        after[c, t]()

            def tiles(a):
                return lambda part, k, t: a[part][:, k, t * P:(t + 1) * P]

            def turn(k, srcs):
                claim(k)
                for n, a in enumerate(srcs):
                    mm = pe.transpose(tp[k % 2][:, n * P:(n + 1) * P], a, idn[:])
                mm.then_inc(tp_done, 1)

            def ada(a, i=None):
                at_least(pe, raw_done, AT_RAW["a", a] + 1, 6, i)
                for half in range(2):
                    n = 2 * a + half
                    dst = adap[:, n:n + 1] if i is None else adap[:, bass.ds(i * 4 + n, 1)]
                    mm = pe.matmul(dst, acc[:, a % 2, 0, half * P:(half + 1) * P], ones[:, 0:1], start=True, stop=True)
                mm.then_inc(ada_used, 1)

            def ada_after(w):
                if w - 3 in ADA_STATIC:
                    ada(ADA_STATIC[w - 3])

            def turn_tile(name, src, t, ready, n):
                def go():
                    pe.wait_ge(ready, n)
                    for half in range(2):
                        turn(tile_job(name, t) + half,
                             [src[:, t, (4 * half + k) * P:(4 * half + k + 1) * P] for k in range(4)])
                return go

            def wait_split(name, n):
                pe.wait_ge(lo_done, SPLIT[JOB[name]] + n)

            def gate_rows(name, n_done, dg=dg):
                pe.wait_ge(dg_done, n_done)
                for half in range(2):
                    k = JOB[name] + half
                    claim(k)
                    pe.matmul(tp[k % 2][:], ones[:], dg[:, 4 * half:4 * half + 4, :].rearrange("p a b -> p (a b)"),
                              start=True, stop=True).then_inc(tp_done, 1)

            def ffn(name, jobs, norm, split):
                w, use, k, a = W0[name], USE[name], JOB[jobs], ADA_AT[ffn_adas(name)[0]]

                def hidden(j):
                    wait_evac(pe, use + j)
                    turn(k + j, [prod[:, j % 2, t, m * P:(m + 1) * P] for m in range(2) for t in range(TT)])

                turned_head(w, use, norm, split)
                hidden(0)
                for c in range(2):
                    feat(w + 4 + c, use + 2, c)
                hidden(1)
                with pe.Fori(0, (GROUPS - PEELED) // 2) as i:
                    for v in range(2):
                        j = PEELED + v
                        feat(w + 2 * j, use + j, 0, i)
                        ada(a + v, i)
                        feat(w + 2 * j + 1, use + j, 1, i)

            def down(name, jobs, after):
                a = ADA_AT[ffn_adas(name.replace("down", "ffn"))[-1]]
                n = GROUPS - WIDE
                wait_split(jobs, WIDE)
                pe.wait_ge(hid_done, n * int(name[-1]) + n - 1)
                outer(W0[name], GROUPS, USE[name], tiles(gt),
                      before={(GROUPS - 1, 0): lambda: pe.wait_ge(hid_done, n * int(name[-1]) + n)},
                      after={(0, 1): lambda: ada(a), **after})

            def levels(half, name):
                job = JOB["pa" if half == 0 else "pb"]
                for lv in range(8):
                    wide_chunk(W0[name] + lv, USE[name] + lv // 2, lv % 2)
                    ada_after(W0[name] + lv)
                    pe.wait_ge(hg_staged, 8 * half + lv + 1)
                    if lv == 0:
                        pe.wait_ge(hg_sk0, half + 1)
                    for s in range(2):
                        k = job + 2 * lv + s
                        claim(k)
                        for hd in range(HH):
                            mm = pe.matmul(tp[k % 2][:, hd * P:(hd + 1) * P], sk[:, hd, s * P:(s + 1) * P],
                                           sq[:, hd, s * P:(s + 1) * P], start=True, stop=True)
                        mm.then_inc(tp_done, 1)

            def across(half):
                pe.wait_ge(hg_qupd, 8 * half + 8)
                pe.wait_ge(hg_kupd, 7 * half + 7)
                job = JOB["offa" if half == 0 else "offb"]
                for s in range(2):
                    k = job + s
                    claim(k)
                    ks, qs = (kf, qf) if s == 0 else (kb, qb)
                    for hd in range(HH):
                        mm = pe.matmul(tp[k % 2][:, hd * P:(hd + 1) * P], ks[:, hd, s * P:(s + 1) * P],
                                       qs[:, hd, (1 - s) * P:(2 - s) * P], start=True, stop=True)
                    mm.then_inc(tp_done, 1)

            def values(half):
                pe.wait_ge(sem("p_copied"), 16 * half + 16)
                pe.wait_ge(sem("off_copied"), 2 * half + 2)
                for t in range(TT):
                    k = JOB["pva" if half == 0 else "pvb"] + t
                    claim(k)
                    for hd in range(HH):
                        for s in range(2):
                            mm = pe.matmul(tp[k % 2][:, hd * P:(hd + 1) * P], at[:, s, hd, t * P:(t + 1) * P],
                                           vv[:, s, (HH * half + hd) * P:(HH * half + hd + 1) * P],
                                           start=(s == 0), stop=(s == 1))
                    mm.then_inc(tp_done, 1)

            pe.wait_ge(consts, 1)
            for n in range(WARM):
                pe.matmul(adap[:, 384:512], ones[:], ones[:], start=(n == 0), stop=(n == WARM - 1))
            pe.wait_ge(small_in, 32)
            turn_tile("norm0", xn, 0, xn_done, 1)()
            turned_head(W0["zu"], USE["zu"], turn_tile("norm0", xn, 1, xn_done, 2), "norm0")
            ada_after(W0["zv"] + 1)
            for name in ("qa", "fa", "ba"):
                for c in range(2):
                    feat(W0[name] + c, USE[name], c)
                    ada_after(W0[name] + c)
                    if name == "ba" and c == 0:
                        pe.wait_ge(ln_done, 2)
                        pe.wait_ge(sgu_in, 48)
                        for t in range(TT):
                            k = JOB["sgu"] + t
                            claim(k)
                            for gr in range(8):
                                mm = pe.matmul(tp[k % 2][:, gr * 64:(gr + 1) * 64], sgw[:, gr, :],
                                               vg[:, t, gr * 64:(gr + 1) * 64], start=True, stop=True)
                            mm.then_inc(tp_done, 1)
            levels(0, "zi")
            for n, name in enumerate(("qb", "fb", "bb")):
                for c in range(2):
                    feat(W0[name] + c, USE[name], c)
                    ada_after(W0[name] + c)
                    if n == 0 and c == 0:
                        across(0)
                    if n == 1 and c == 1:
                        pe.wait_ge(b_out, 2)
                        for t in range(TT):
                            turn(JOB["tb"] + t, [u[:, t, k * P:(k + 1) * P] for k in range(4)])
                if n == 0:
                    wait_evac(pe, USE["zi"] + 1)
                    values(0)
            levels(1, "ga")
            wait_split("tb", 2)
            outer(W0["wb"], 2, USE["wb"], lambda part, k, t: bt[part][:, t, k * P:(k + 1) * P],
                  after={(1, 0): lambda: across(1), (0, 1): lambda: values(1)})
            turn_tile("ta", zg, 0, a_out, 3)()
            outer(W0["wa"], 4, USE["wa"], tiles(gt),
                  before={(0, 0): lambda: wait_split("ta", 2), (0, 1): lambda: wait_split("ta", 4)},
                  after={(1, 0): turn_tile("ta", zg, 1, a_out, 4),
                         (0, 1): turn_tile("tm", ga, 0, merged, 1)})
            outer(W0["wout"], 4, USE["wout"], tiles(ht),
                  before={(0, 0): lambda: wait_split("tm", 2), (0, 1): lambda: wait_split("tm", 4)},
                  after={(1, 0): turn_tile("tm", ga, 1, merged, 2),
                         (2, 1): turn_tile("norm1", xn, 0, xn_done, 3)})
            ffn("ffn0", "h0", turn_tile("norm1", xn, 1, xn_done, 4), "norm1")
            down("down0", "h0", after={})
            pe.wait_ge(pt_done, 1)
            outer(W0["ple"], 1, USE["ple"], tiles(pt),
                  after={(0, 0): turn_tile("tx", xres, 0, x_ready, 3)})
            outer(W0["pleg"], 4, USE["pleg"], tiles(ht),
                  before={(0, 0): lambda: wait_split("tx", 2), (0, 1): lambda: wait_split("tx", 4)},
                  after={(1, 0): turn_tile("tx", xres, 1, x_ready, 4),
                         (1, 1): turn_tile("norm2", xn, 0, xn_done, 5)})
            wait_split("norm2", 2)
            pe.wait_ge(cs_done, 1)
            for t in range(TT):
                for gr in range(4):
                    k = JOB["dft1b" if t else "dft1"] + gr
                    claim(k)
                    for d in range(2):
                        for n, (a, b) in enumerate(passes(ht, cs)):
                            mm = pe.matmul(tp[k % 2][:], a[:, 2 * gr + d, t * P:(t + 1) * P], b[:, d, 0:512],
                                           start=(d == 0 and n == 0), stop=(d == 1 and n == 2))
                    mm.then_inc(tp_done, 1)
                if t == 0:
                    gate_rows("rows0", 1)
                    turn_tile("norm2", xn, 1, xn_done, 6)()
                    wait_split("norm2b", 2)
            for gr in range(4):
                wait_split("dft1b", gr + 1)
                k = JOB["dft2"] + gr
                claim(k)
                for m in range(2):
                    for n, (t, part) in enumerate([(0, 0), (0, 1), (1, 0), (1, 1)]):
                        for o, (a, b) in enumerate(passes(tt, cs)):
                            mm = pe.matmul(tp[k % 2][:, m * S:(m + 1) * S],
                                           a[:, t, gr, part * S + m * P:part * S + (m + 1) * P],
                                           b[:, t, 2 * part * S:(2 * part + 1) * S],
                                           start=(n == 0 and o == 0), stop=(n == 3 and o == 2))
                mm.then_inc(tp_done, 1)
            outer(W0["fo"], 4, USE["fo"], tiles(ht),
                  before={(c, 0): lambda c=c: wait_split("dft2", c + 1) for c in range(4)},
                  after={(1, 1): turn_tile("norm3", xn, 0, xn_done, 7)})
            ffn("ffn1", "h1", turn_tile("norm3", xn, 1, xn_done, 8), "norm3")
            down("down1", "h1", after={(4, 1): lambda: gate_rows("rows1", 2),
                                       (GROUPS - 3, 1): turn_tile("norm4", xn, 0, xn_done, 9)})
            turned_head(W0["rva"], USE["rva"], turn_tile("norm4", xn, 1, xn_done, 10), "norm4")
            for name in ("rq", "rk"):
                for c in range(4):
                    feat(W0[name] + c, USE[name] + c // 2, c % 2)
                    ada_after(W0[name] + c)
            for c in range(4):
                wide_chunk(W0["rvb"] + c, USE["rvb"] + c // 2, c % 2)
                ada_after(W0["rvb"] + c)
                if c == 1:
                    pe.wait_ge(rot_done, 4)
                if c:
                    for hd in ((), (0,), (1, 2), (3,))[c]:
                        k = JOB["sc"] + hd
                        claim(k)
                        for s in range(2):
                            for d in range(2):
                                mm = pe.matmul(tp[k % 2][:, s * S:(s + 1) * S], kr[:, hd, d, s * P:(s + 1) * P],
                                               qr[:, hd, d, :], start=(d == 0), stop=(d == 1))
                        mm.then_inc(tp_done, 1)
            gate_rows("rows2", 3, dgb)

            def turn_head(hd):
                pe.wait_ge(y_done, hd + 1)
                for t in range(TT):
                    turn(JOB["ty"] + 2 * hd + t, [gg[:, t, (4 * hd + k) * P:(4 * hd + k + 1) * P] for k in range(4)])

            for c in range(8):
                wide_chunk(W0["rg"] + c, USE["rg"] + c // 2, c % 2)
                ada_after(W0["rg"] + c)
                if c == 0:
                    wait_evac(pe, USE["rvb"])
                    wait_evac(pe, USE["rvb"] + 1)
                    pe.wait_ge(sem("sc_read"), RH)
                if c < RH:
                    for t in range(TT):
                        k = JOB["av"] + 2 * c + t
                        claim(k)
                        for s in range(2):
                            mm = pe.matmul(tp[k % 2][:], ar[:, c, s, t * P:(t + 1) * P], vr[:, s, c * RV:(c + 1) * RV],
                                           start=(s == 0), stop=(s == 1))
                        mm.then_inc(tp_done, 1)
                elif c > RH:
                    turn_head(c - RH - 1)
            outer(W0["ro"], 8, USE["ro"], tiles(gt),
                  before={(0, 0): lambda: wait_split("ty", 2), (2, 0): lambda: wait_split("ty", 4),
                          (4, 0): lambda: wait_split("ty", 6), (6, 0): lambda: wait_split("ty", 8)},
                  after={(0, 1): lambda: turn_head(RH - 1), (5, 1): turn_tile("norm5", xn, 0, xn_done, 11)})
            ffn("ffn2", "h2", turn_tile("norm5", xn, 1, xn_done, 12), "norm5")
            down("down2", "h2", after={(4, 1): lambda: gate_rows("rows3", 4),
                                       (GROUPS - 2, 1): turn_tile("norm6", xn, 0, xn_done, 13)})
            turn_tile("norm6", xn, 1, xn_done, 14)()

        @block.scalar
        def _(act):
            sc = nc.scalar

            def split_hi(w, i=None):
                if w >= NW:
                    return
                n = AT_RAW["w", w]
                at_least(act, landed[n % RAW], 16 * (n // RAW + 1), 32, i)
                if w >= WS:
                    at_least(act, w_used, w - WS + 1, 4, i)
                sc.activation(w_hi[:, w % WS, :], raw[:, n % RAW, :], ACT.Copy).then_inc(hi_done, 1)

            def tick(w, i=None):
                split_hi(w + WS, i)

            def pair_ready(w, i=None):
                at_least(act, w_used, w + 1, 4, i)

            def evacuate(dst, use, func, scale=1.0, last=True):
                ins = sc.activation(dst, pair[use % 2][:], func, scale=scale)
                if last:
                    ins.then_inc(evac[use % 2], 1)

            def hi(k, dst, src=None, i=None):
                if src is None:
                    at_least(act, tp_done, k + 1, 2, i)
                    src = tp[k % 2][:]
                sc.activation(dst, src, ACT.Copy).then_inc(t_hi, 1)

            def norm_squares(q, t, n_x):
                act.wait_ge(x_ready, n_x) if n_x else act.wait_ge(x_in[t], 16)
                sc.activation(xn[:, t, :], xres[:, t, :], ACT.Square, accum_out=st[:, q, 0, 0:1]).then_inc(ss_done, 1)

            def norm_his(name, t):
                for half in range(2):
                    k = tile_job(name, t) + half
                    n = RELEASE[k][1]
                    act.wait_ge(norm_read, n)
                    hi(k, ht[0][:, 4 * half:4 * half + 4, t * P:(t + 1) * P],
                       hb[:, k % 2, :].rearrange("p (k s) -> p k s", k=4))

            def post_squares(q, t, w, use, halves):
                if t == 0:
                    act.wait_ge(half_ready, halves)
                else:
                    pair_ready(w)
                sc.activation(xn[:, t, :].rearrange("p (a b) -> p a b", a=2), pair[(use + t) % 2][:], ACT.Square,
                              accum_out=st[:, q, 0, 0:1]).then_inc(ss_done, 1)

            def turned(k, dst, q, t):
                hi(k, dst[0][:, 4 * q:4 * q + 4, t * P:(t + 1) * P], _four(tp[k % 2][:], k))

            def turned_tile(name, dst, t):
                for q in range(2):
                    turned(JOB[name] + 2 * t + q, dst, q, t)

            def _four(a, k):
                act.wait_ge(tp_done, k + 1)
                return a.rearrange("p (k s) -> p k s", k=4)

            def stage_level(half, lv):
                if lv == 0:
                    if half:
                        act.wait_ge(tp_done, JOB["pa"] + 16)
                    act.wait_ge(evac[USE["qa" if half == 0 else "qb"] % 2], USE["qa" if half == 0 else "qb"] // 2 + 1)
                    sc.activation(sq[:], qf[:], ACT.Copy).then_inc(hg_staged, 1)
                    return
                h = 1 << (lv - 1)
                v = [a[:].rearrange("p a (b two h) -> p (a b) two h", two=2, h=h) for a in (qf, qb, kf, kb, sq, sk)]
                act.wait_ge(hg_qupd, 8 * half + lv)
                at_least(act, hg_kupd, 7 * half + lv - 1)
                act.wait_ge(tp_done, JOB["pa" if half == 0 else "pb"] + 2 * lv)
                sc.activation(v[4][:, :, 1, :], v[0][:, :, 1, :], ACT.Copy)
                sc.activation(v[4][:, :, 0, :], v[1][:, :, 0, :], ACT.Copy)
                sc.activation(v[5][:, :, 0, :], v[2][:, :, 0, :], ACT.Copy)
                sc.activation(v[5][:, :, 1, :], v[3][:, :, 1, :], ACT.Copy).then_inc(hg_staged, 1)

            def across(half):
                for s in range(2):
                    k = JOB["offa" if half == 0 else "offb"] + s
                    act.wait_ge(tp_done, k + 1)
                    if half:
                        act.wait_ge(tp_done, JOB["pva"] + 2)
                    sc.activation(at[:, s, :, (1 - s) * P:(2 - s) * P], tp[k % 2][:].rearrange("p (a b) -> p a b", a=HH),
                                  ACT.Copy).then_inc(sem("off_copied"), 1)

            def value_squares(half):
                for t in range(TT):
                    k = JOB["pva" if half == 0 else "pvb"] + t
                    act.wait_ge(tp_done, k + 1)
                    if half:
                        act.wait_ge(a_out, 2)
                    sc.activation(osq[:, t, :], tp[k % 2][:], ACT.Square).then_inc(pv_sq, 1)

            def ffn(name, jobs):
                w, use, k, n0 = W0[name], USE[name], JOB[jobs], (GROUPS - WIDE) * int(name[-1])

                def gate(j, i=None):
                    pair_ready(w + 2 * j + 1, i)
                    if j == WIDE:
                        act.wait_ge(tp_done, k + 1)
                    elif j > WIDE:
                        at_least(act, hid_done, n0 + j - WIDE, 2, i)
                    sc.activation(prod[:, j % 2, :, :], pair[(use + j) % 2][:, :, 0:256], ACT.Silu).then_inc(silu_done, 1)

                def hidden_hi(j, i=None):
                    wait_evac(act, use + j, i)
                    dst = gt[0][:, 2 * j:2 * j + 2, :] if i is None else gt[0][:, bass.ds(i * 4 + 2 * j, 2), :]
                    sc.activation(dst, prod[:, j % 2, :, :], ACT.Copy).then_inc(hid_hi, 1)

                for j in range(WIDE):
                    gate(j)
                    if j:
                        hi(k, gt[0][:, 0:2, :], _two(tp[k % 2][:], k))
                    tick(w + 2 * j)
                    tick(w + 2 * j + 1)
                for j in range(WIDE, PEELED):
                    gate(j)
                    hidden_hi(j)
                    hi(k + 1, gt[0][:, 2:4, :], _two(tp[(k + 1) % 2][:], k + 1))
                    tick(w + 2 * j)
                    tick(w + 2 * j + 1)
                with act.Fori(0, (GROUPS - PEELED) // 2) as i:
                    for j in range(PEELED, PEELED + 2):
                        gate(j, i)
                        hidden_hi(j, i)
                        tick(w + 2 * j, i)
                        tick(w + 2 * j + 1, i)

            def _two(a, k):
                act.wait_ge(tp_done, k + 1)
                return a.rearrange("p (a b) -> p a b", a=2)

            def gate_rows(name, row):
                for half in range(2):
                    k = JOB[name] + half
                    act.wait_ge(tp_done, k + 1)
                    sc.activation(row[:, half * 512:(half + 1) * 512], tp[k % 2][:], ACT.Copy).then_inc(sem("row_copied"), 1)

            norm_squares(RQ["norm0"], 0, 0)
            split_hi(0)
            norm_his("norm0", 0)
            split_hi(1)
            norm_squares(RQ["norm0"] + 1, 1, 0)
            for w in range(2, WS):
                split_hi(w)
            sc.activation(ca[:], colv("c", 0, 8), ACT.Silu).then_inc(ca_done, 1)
            norm_his("norm0", 1)
            act.wait_ge(lb_e, 1)
            sc.activation(lbt[:, 1, :], lbt[:, 0, :], ACT.Exp).then_inc(lb_e, 1)
            tick(0)
            pair_ready(1)
            evacuate(u[:], USE["zu"], ACT.Gelu)
            tick(1)
            tick(2)
            pair_ready(3)
            evacuate(vg[:], USE["zv"], ACT.Gelu)
            tick(3)

            def head_gates(half):
                q, f, b = ("qa", "fa", "ba") if half == 0 else ("qb", "fb", "bb")
                tick(W0[q])
                if half:
                    act.wait_ge(tp_done, JOB["offa"] + 2)
                    across(0)
                pair_ready(W0[q] + 1)
                as4 = "p a (b s) -> p (a b) s"
                sc.activation(qf[:], pair[USE[q] % 2][:].rearrange(as4, b=2), ACT.Silu).then_inc(evac[USE[q] % 2], 1)
                tick(W0[q] + 1)
                if half:
                    value_squares(0)
                stage_level(half, 0)
                tick(W0[f])
                pair_ready(W0[f] + 1)
                sc.activation(tf[:], pair[USE[f] % 2][:].rearrange(as4, b=2), ACT.Sigmoid)
                sc.activation(kf[:], pair[USE[f] % 2][:].rearrange(as4, b=2), ACT.Sigmoid, scale=-1.0).then_inc(evac[USE[f] % 2], 1)
                tick(W0[f] + 1)
                tick(W0[b])
                if half:
                    for t in range(TT):
                        hi(JOB["tb"] + t, bt[0][:, t, :])
                pair_ready(W0[b] + 1)
                sc.activation(tb[:], pair[USE[b] % 2][:].rearrange(as4, b=2), ACT.Sigmoid)
                sc.activation(kb[:], pair[USE[b] % 2][:].rearrange(as4, b=2), ACT.Sigmoid, scale=-1.0).then_inc(evac[USE[b] % 2], 1)
                tick(W0[b] + 1)

            def boundary(w, q, name, n_x):
                norm_squares(q, 0, n_x)
                tick(w - 3)
                tick(w - 2)
                norm_his(name, 0)
                tick(w - 1)
                norm_squares(q + 1, 1, n_x + 1)
                tick(w)
                norm_his(name, 1)

            def gated_chunks(half, name0, plan):
                for lv in range(8):
                    w = W0[name0] + lv
                    if lv % 2 == 1:
                        pair_ready(w)
                        dst, func = plan[lv // 2]
                        use = USE[name0] + lv // 2
                        evacuate(dst, use, func)
                    tick(w)
                    if lv < 7:
                        stage_level(half, lv + 1)

            head_gates(0)
            gated_chunks(0, "zi", [(vv[:, :, 0:512], ACT.Copy), (vv[:, :, 512:1024], ACT.Copy),
                                   (zg[:, :, 0:512], ACT.Silu), (zg[:, :, 512:1024], ACT.Silu)])
            head_gates(1)
            gated_chunks(1, "ga", [(ga[:, :, 0:512], ACT.Sigmoid), (ga[:, :, 512:1024], ACT.Sigmoid),
                                   (gb[:, :, 0:512], ACT.Sigmoid), (gb[:, :, 512:1024], ACT.Sigmoid)])
            across(1)
            tick(W0["wb"])
            value_squares(1)
            turned_tile("ta", gt, 0)
            tick(W0["wb"] + 1)
            turned_tile("ta", gt, 1)
            tick(W0["wa"])
            turned_tile("tm", ht, 0)
            tick(W0["wa"] + 1)
            tick(W0["wa"] + 2)
            tick(W0["wa"] + 3)
            turned_tile("tm", ht, 1)
            w = W0["wout"]
            for t in range(TT):
                post_squares(RQ["mix"] + 2 * t, t, w + 3, USE["wout"], 3)
                if t == 0:
                    tick(w)
                norm_squares(RQ["mix"] + 2 * t + 1, t, 1 + t)
                tick(w + 3 if t else w + 1)
                norm_his("norm1", t)
                if t == 0:
                    tick(w + 2)
            ffn("ffn0", "h0")
            w = W0["down0"]
            for c in range(GROUPS - 4):
                tick(w + c)
                if c == 0:
                    act.wait_ge(p_in, 16)
                    sc.activation(pt[0][:], praw[:], ACT.Copy).then_inc(pt_hi, 1)
            post_squares(RQ["ffn"], 0, w + GROUPS - 1, USE["down0"], 4)
            tick(w + GROUPS - 4)
            tick(w + GROUPS - 3)
            tick(w + GROUPS - 2)
            post_squares(RQ["ffn"] + 1, 1, w + GROUPS - 1, USE["down0"], 4)
            tick(w + GROUPS - 1)
            for t in range(TT):
                if t == 0:
                    act.wait_ge(half_ready, 5)
                else:
                    pair_ready(W0["ple"])
                act.wait_ge(x_ready, 3 + t)
                sc.activation(xn[:, t, :].rearrange("p (a b) -> p a b", a=2), pair[(USE["ple"] + t) % 2][:],
                              ACT.Copy).then_inc(evac[(USE["ple"] + t) % 2], 1)
                if t:
                    tick(W0["ple"])
                turned_tile("tx", ht, t)
            act.wait_ge(dft_in, 16)
            act.wait_ge(w_used, W0["ple"] + 1)
            act.wait_ge(x_ready, 4)
            sc.activation(cs[0][:], csr[:], ACT.Copy).then_inc(cs_hi, 1)
            w = W0["pleg"] + 3

            def dft_his(name, t, groups):
                for gr in groups:
                    hi(JOB[name] + gr, tt[0][:, t, gr, :])

            for t in range(TT):
                if t == 0:
                    act.wait_ge(half_ready, 6)
                else:
                    pair_ready(w)
                sc.activation(gsig[:, t, :].rearrange("p (a b) -> p a b", a=2), pair[(USE["pleg"] + t) % 2][:],
                              ACT.Sigmoid).then_inc(evac[(USE["pleg"] + t) % 2], 1)
                if t:
                    dft_his("dft1", 0, (0, 1))
                norm_squares(RQ["norm2"] + t, t, 5 + t)
                if t:
                    dft_his("dft1", 0, (2, 3))
                    gate_rows("rows0", grow[0])
                norm_his("norm2", t)
                if t == 0:
                    tick(w - 3)
            dft_his("dft1b", 1, range(4))
            for gr in range(4):
                k = JOB["dft2"] + gr
                hi(k, ht[0][:, 2 * gr:2 * gr + 2, :], _two(tp[k % 2][:], k))
                if gr != 2:
                    tick(w - 2 + (gr + 1) // 2)
            boundary(W0["fo"] + 3, RQ["norm3"], "norm3", 7)
            ffn("ffn1", "h1")
            for w in range(W0["down1"], W0["down1"] + GROUPS - 4):
                if w == W0["down1"] + 4:
                    gate_rows("rows1", grow[1])
                tick(w)
            boundary(W0["down1"] + GROUPS - 1, RQ["norm4"], "norm4", 9)

            def values(name, gr):
                c = gr % 2
                tick(W0[name] + 2 * c)
                pair_ready(W0[name] + 2 * c + 1)
                evacuate(vr[:, :, gr * RV:(gr + 1) * RV], USE[name] + c, ACT.Copy)
                tick(W0[name] + 2 * c + 1)

            values("rva", 0)
            values("rva", 1)
            for w in range(W0["rq"], W0["rvb"]):
                tick(w)
            values("rvb", 2)
            values("rvb", 3)

            def head_his(hd):
                for t in range(TT):
                    turned(JOB["ty"] + 2 * hd + t, gt, hd, t)

            gate_rows("rows2", grow[0])
            for gr in range(4):
                if gr == 3:
                    head_his(1)
                tick(W0["rg"] + 2 * gr)
                pair_ready(W0["rg"] + 2 * gr + 1)
                evacuate(gg[:, :, gr * RV:(gr + 1) * RV], USE["rg"] + gr, ACT.Silu)
                if gr == 2:
                    head_his(0)
                if gr == 3:
                    head_his(2)
                tick(W0["rg"] + 2 * gr + 1)
            tick(W0["ro"])
            head_his(3)
            for w in range(W0["ro"] + 1, W0["ro"] + 4):
                tick(w)
            boundary(W0["ro"] + 7, RQ["norm5"], "norm5", 11)
            ffn("ffn2", "h2")
            for w in range(W0["down2"], W0["down2"] + GROUPS - 1):
                if w == W0["down2"] + 3:
                    gate_rows("rows3", grow[1])
                tick(w)
            for t in range(TT):
                norm_squares(RQ["norm6"] + t, t, 13 + t)

        @block.vector
        def _(dve):
            v = nc.vector
            steps = [0]

            def link(ins):
                steps[0] += 1
                ins.then_inc(step, 1)
                dve.wait_ge(step, steps[0])

            def as_f32(a):
                return a.bitcast(F32)

            whi32 = as_f32(w_hi[:])
            ht32, gt32, tt32 = as_f32(ht[0][:]), as_f32(gt[0][:]), as_f32(tt[0][:])

            def after_pool(n):
                if ORDER[n - 1] in [("w", w) for w in POOL_LO]:
                    dve.wait_ge(raw_done, n)

            def split_lo(w, i=None):
                if w >= NW:
                    return
                n = AT_RAW["w", w]
                if w in POOL_LO:
                    return
                after_pool(n)
                at_least(dve, hi_done, w + 1, 4, i)
                v.tensor_tensor(w_lo[:, w % WS, :], raw[:, n % RAW, :], whi32[:, w % WS, :],
                                ALU.subtract).then_inc(raw_done, 1)

            def ada(a, i=None):
                n = AT_RAW["a", a]
                after_pool(n)
                at_least(dve, landed[n % RAW], 16 * (n // RAW + 1), 32, i)
                if a >= 2:
                    at_least(dve, ada_used, a - 1, 2, i)
                for k in range(KT):
                    src, dst = raw[:, n % RAW, k * 256:(k + 1) * 256], acc[:, a % 2, k % 2, :]
                    if k < 2:
                        ins = v.tensor_scalar(dst, src, ca[:, k:k + 1], None, ALU.mult)
                    else:
                        at_least(dve, ada_step, 8 * a + k - 1, 16, i)
                        ins = v.scalar_tensor_tensor(out=dst, in0=src, scalar=ca[:, k:k + 1], in1=dst,
                                                     op0=ALU.mult, op1=ALU.add)
                    ins.then_inc(ada_step, 1)
                at_least(dve, ada_step, 8 * a + 8, 16, i)
                v.tensor_tensor(acc[:, a % 2, 0, :], acc[:, a % 2, 0, :], acc[:, a % 2, 1, :], ALU.add).then_inc(raw_done, 1)

            def tick(w, i=None):
                split_lo(w + WS, i)
                if w in ADA_STATIC:
                    ada(ADA_STATIC[w])

            def ready(use, t, w, halves):
                if t == 0:
                    dve.wait_ge(half_ready, halves)
                else:
                    dve.wait_ge(w_used, w + 1)

            def mean_square(q):
                dve.wait_ge(ss_done, SS[q])
                v.tensor_scalar(st[:, q, 1, 0:1], st[:, q, 0, 0:1], 1.0 / D, EPS, ALU.mult, ALU.add).then_inc(ms_done, 1)
                dve.wait_ge(rstd_done, q + 1)

            def two(a):
                return a.rearrange("p (a b) -> p a b", a=2)

            def norm(q, t, before=None):
                if before is not None:
                    tick(before)
                mean_square(q)
                v.tensor_scalar(xn[:, t, :], xres[:, t, :], st[:, q, 2, 0:1], None, ALU.mult).then_inc(xn_done, 1)

            def scaled(name, t, scale, shift, dst):
                for half in range(2):
                    k = tile_job(name, t) + half
                    dve.wait_ge(tp_done, k + 1)
                    if k in SPLIT:
                        at_least(dve, lo_done, SPLIT[k] - 1)
                    for m in range(4):
                        f = 4 * half + m
                        ins = v.tensor_scalar(dst(k, half)[:, m * P:(m + 1) * P], tp[k % 2][:, m * P:(m + 1) * P],
                                              scale[:, f:f + 1], None if shift is None else shift[:, f:f + 1],
                                              ALU.mult, *(() if shift is None else (ALU.add,)))
                    ins.then_inc(sem(RELEASE[k][0]), 1)

            def norm_jobs(name, t, scale, shift=None):
                scaled(name, t, scale, shift, lambda k, half: hb[:, k % 2, :])
                for half in range(2):
                    k = tile_job(name, t) + half
                    dve.wait_ge(norm_read, RELEASE[k][1])
                    dve.wait_ge(t_hi, SPLIT[k] + 1)
                    where = (slice(None), slice(4 * half, 4 * half + 4), slice(t * P, (t + 1) * P))
                    v.tensor_tensor(ht[1][where], hb[:, k % 2, :].rearrange("p (k s) -> p k s", k=4), ht32[where],
                                    ALU.subtract).then_inc(lo_done, 1)

            def lo(k, dst, hi32, src, i=None):
                at_least(dve, t_hi, SPLIT[k] + 1, 2, i)
                v.tensor_tensor(dst, src, hi32, ALU.subtract).then_inc(lo_done, 1)

            def turned(k, dst, hi32, q, t):
                where = (slice(None), slice(4 * q, 4 * q + 4), slice(t * P, (t + 1) * P))
                lo(k, dst[1][where], hi32[where], tp[k % 2][:].rearrange("p (k s) -> p k s", k=4))

            def turned_tile(name, dst, hi32, t):
                for q in range(2):
                    turned(JOB[name] + 2 * t + q, dst, hi32, q, t)

            def post(q, t, use, row):
                mean_square(q)
                p = (use + t) % 2
                v.scalar_tensor_tensor(out=two(xn[:, t, :]), in0=pair[p][:], scalar=st[:, q, 2, 0:1], in1=two(row),
                                       op0=ALU.mult, op1=ALU.mult).then_inc(evac[p], 1)
                wait_evac(dve, use + t)
                v.tensor_tensor(xres[:, t, :], xres[:, t, :], xn[:, t, :], ALU.add).then_inc(x_ready, 1)

            def gated_post(t, use, w, halves, row, rows):
                ready(use, t, w, halves)
                dve.wait_ge(sem("row_copied"), rows)
                p = (use + t) % 2
                v.tensor_tensor(two(xn[:, t, :]), pair[p][:], two(row), ALU.mult).then_inc(evac[p], 1)
                wait_evac(dve, use + t)
                v.tensor_tensor(xres[:, t, :], xres[:, t, :], xn[:, t, :], ALU.add).then_inc(x_ready, 1)

            def mod_columns(a, b, used):
                dve.wait_ge(ada_used, used)
                link(v.tensor_tensor(mod[:, a:b], adap[:, a:b], colv("b_ada", a, b - a), ALU.add))

            def mod_scale(n, at_col, gain):
                link(v.scalar_tensor_tensor(out=moda[:, n, :], in0=mod[:, at_col:at_col + 8], scalar=1.0, in1=gain,
                                            op0=ALU.add, op1=ALU.mult))

            def gate_diagonals(at_col, read=None, dg=dg):
                if read is not None:
                    dve.wait_ge(tp_done, read)
                for m in range(KT):
                    ins = v.tensor_scalar(dg[:, m, :], idn[:], mod[:, at_col + m:at_col + m + 1], None, ALU.mult)
                ins.then_inc(dg_done, 1)

            def ffn(name, jobs):
                w, use, k, n0 = W0[name], USE[name], JOB[jobs], int(name[-1])

                def gate(j, i=None):
                    at_least(dve, silu_done, GROUPS * n0 + j + 1, 2, i)
                    v.tensor_tensor(prod[:, j % 2, :, :], prod[:, j % 2, :, :], pair[(use + j) % 2][:, :, 256:512],
                                    ALU.mult).then_inc(evac[(use + j) % 2], 1)

                def hidden_lo(j, i=None):
                    where = slice(2 * j, 2 * j + 2) if i is None else bass.ds(i * 4 + 2 * j, 2)
                    at_least(dve, hid_hi, (GROUPS - WIDE) * n0 + j - WIDE + 1, 2, i)
                    v.tensor_tensor(gt[1][:, where, :], prod[:, j % 2, :, :], gt32[:, where, :],
                                    ALU.subtract).then_inc(hid_done, 1)

                def turned_lo(j):
                    lo(k + j, gt[1][:, 2 * j:2 * j + 2, :], gt32[:, 2 * j:2 * j + 2, :],
                       tp[(k + j) % 2][:].rearrange("p (a b) -> p a b", a=2))

                for j in range(WIDE):
                    gate(j)
                    if j:
                        turned_lo(0)
                    tick(w + 2 * j)
                    tick(w + 2 * j + 1)
                for j in range(WIDE, PEELED):
                    gate(j)
                    ada(ADA_AT[w + 2 * j - 1])
                    tick(w + 2 * j)
                    hidden_lo(j)
                    turned_lo(1)
                    tick(w + 2 * j + 1)
                with dve.Fori(0, (GROUPS - PEELED) // 2) as i:
                    for j in range(PEELED, PEELED + 2):
                        gate(j, i)
                        ada(ADA_AT[w + 2 * j - 1], i)
                        tick(w + 2 * j, i)
                        hidden_lo(j, i)
                        tick(w + 2 * j + 1, i)

            def head_gates(half, read_banks):
                q, f, b = ("qa", "fa", "ba") if half == 0 else ("qb", "fb", "bb")
                def keys(d, name, kx):
                    wait_evac(dve, USE[name])
                    for hd in range(HH):
                        n = 8 * d + HH * half + hd
                        ins = v.tensor_scalar(kx[:, hd, :], kx[:, hd, :], lbt[:, 0, n:n + 1], None, ALU.mult)
                    return ins

                def gates(d, fx):
                    for hd in range(HH):
                        n = 8 * d + HH * half + hd
                        ins = v.tensor_scalar(fx[:, hd, :], fx[:, hd, :], lbt[:, 0, n:n + 1], lbt[:, 4, n:n + 1],
                                              ALU.mult, ALU.add)
                    link(ins)
                    link(v.tensor_scalar(fx[:], fx[:], TINY, None, ALU.max))

                tick(W0[f])
                keys(0, f, kf)
                gates(0, tf)
                tick(W0[f] + 1)
                tick(W0[b])
                read_banks()
                link(keys(1, b, kb))
                if half:
                    dve.wait_ge(tp_done, JOB["pa"] + 16)
                v.tensor_tensor(sk[:], kf[:], kb[:], ALU.add).then_inc(hg_sk0, 1)
                gates(1, tb)
                dve.wait_ge(hg_staged, 8 * half + 1)
                link(v.tensor_tensor(qb[:], qf[:], tb[:], ALU.mult))
                v.tensor_tensor(qf[:], qf[:], tf[:], ALU.mult).then_inc(hg_qupd, 1)
                tick(W0[b] + 1)

            def query_updates(half, lv):
                h = 1 << (lv - 1)
                nb = HH * S // (2 * h)
                qa, qc, fa, fc = [a[:].rearrange("p a (b two h) -> p (a b) two h", two=2, h=h) for a in (qf, qb, tf, tb)]
                dve.wait_ge(hg_qupd, 8 * half + lv)
                dve.wait_ge(hg_staged, 8 * half + lv + 1)
                if lv > 1:
                    dve.wait_ge(hg_tot, 6 * half + lv - 1)
                v.tensor_tensor(qa[:, :, 1, :], qa[:, :, 1, :], fa[:, :, 0, 0:1].to_broadcast([P, nb, h]), ALU.mult)
                v.tensor_tensor(qc[:, :, 0, :], qc[:, :, 0, :], fc[:, :, 1, 0:1].to_broadcast([P, nb, h]),
                                ALU.mult).then_inc(hg_qupd, 1)
                if lv < 7:
                    dve.wait_ge(hg_kupd, 7 * half + lv)
                    dve.wait_ge(hg_qupd, 8 * half + lv + 1)
                    v.tensor_tensor(fa[:, :, 0, 0:1], fa[:, :, 0, 0:1], fa[:, :, 1, 0:1], ALU.mult)
                    v.tensor_tensor(fc[:, :, 0, 0:1], fc[:, :, 0, 0:1], fc[:, :, 1, 0:1], ALU.mult).then_inc(hg_tot, 1)

            def take_scores(half, lv):
                for s in range(2):
                    k = JOB["pa" if half == 0 else "pb"] + 2 * lv + s
                    dve.wait_ge(tp_done, k + 1)
                    n = RELEASE[k][1]
                    if n > 2:
                        dve.wait_ge(sem("p_copied"), n - 2)
                    v.copy_predicated(at[:, s, :, s * P:(s + 1) * P], msk[:, lv:lv + 1, :].to_broadcast([P, HH, P]),
                                      tp[k % 2][:].rearrange("p (a b) -> p a b", a=HH)).then_inc(sem("p_copied"), 1)

            def head_outputs(half):
                q = RQ["pva" if half == 0 else "pvb"]
                for t in range(TT):
                    dve.wait_ge(pv_sq, 2 * half + t + 1)
                    link(v.tensor_reduce(st[:, q + t, 0, :], osq[:, t, :].rearrange("p (a b) -> p a b", a=HH), AX.X, ALU.add))
                    v.tensor_scalar(st[:, q + t, 1, :], st[:, q + t, 0, :], 1.0 / P, EPS, ALU.mult, ALU.add).then_inc(ms_done, 1)
                for t in range(TT):
                    k = JOB["pva" if half == 0 else "pvb"] + t
                    dve.wait_ge(rstd_done, q + t + 1)
                    at_least(dve, a_out, 2 * half)
                    v.tensor_tensor(on[:, t, :].rearrange("p (a b) -> p a b", a=HH),
                                    tp[k % 2][:].rearrange("p (a b) -> p a b", a=HH),
                                    st[:, q + t, 2, :].unsqueeze(2).to_broadcast([P, HH, P]), ALU.mult).then_inc(sem("pv_read"), 1)
                dve.wait_ge(zg_done, half + 1)
                for t in range(TT):
                    dve.wait_ge(sem("pv_read"), 2 * half + t + 1)
                    z = zg[:, t, half * 512:(half + 1) * 512]
                    v.tensor_tensor(z, z, on[:, t, :], ALU.mult).then_inc(a_out, 1)

            norm(RQ["norm0"], 0)
            dve.wait_ge(small_in, 32)
            norm_jobs("norm0", 0, colv("mix_pre", 0, 8))
            split_lo(0)
            split_lo(1)
            norm(RQ["norm0"] + 1, 1)
            split_lo(2)
            split_lo(3)
            norm_jobs("norm0", 1, colv("mix_pre", 0, 8))
            gamma = colv("gamma", 0, 16)
            v.tensor_tensor(lbt[:, 0, :], gamma, gamma, ALU.subtract).then_inc(lb_e, 1)
            dve.wait_ge(lb_e, 2)
            link(v.reciprocal(lbt[:, 2, :], lbt[:, 1, :]))
            link(v.tensor_tensor(lbt[:, 3, :], lbt[:, 1, :], lbt[:, 2, :], ALU.mult))
            link(v.tensor_tensor(lbt[:, 4, :], lbt[:, 3, :], lbt[:, 3, :], ALU.subtract))
            link(v.tensor_scalar(lbt[:, 0, :], lbt[:, 4, :], -1.0, 1.0, ALU.mult, ALU.add))
            dve.wait_ge(hg_in, 32)
            link(v.tensor_copy(msk[:], mskf[:]))
            dve.wait_ge(ca_done, 1)
            for w in range(3):
                tick(w)
            wait_evac(dve, USE["zv"])
            dve.wait_ge(sgu_in, 48)
            for t in range(TT):
                link(v.bn_stats(bn[:, t, :], vg[:, t, :]))
                link(v.bn_aggr(mv[:, t, :], bn[:, t, :]))
                q = RQ["ln"] + t
                v.tensor_scalar(st[:, q, 1, 0:1], mv[:, t, 1:2], EPS, None, ALU.add).then_inc(ms_done, 1)
                dve.wait_ge(rstd_done, q + 1)
                link(v.tensor_scalar(vg[:, t, :], vg[:, t, :], mv[:, t, 0:1], st[:, q, 2, 0:1], ALU.subtract, ALU.mult))
                link(v.tensor_tensor(vg[:, t, :], vg[:, t, :], lnrow[:, 0, :], ALU.mult))
                v.tensor_tensor(vg[:, t, :], vg[:, t, :], lnrow[:, 1, :], ALU.add).then_inc(ln_done, 1)
                tick(3 + t)
            tick(5)

            def gate_positions():
                for t in range(TT):
                    k = JOB["sgu"] + t
                    dve.wait_ge(tp_done, k + 1)
                    v.tensor_tensor(vg[:, t, :].rearrange("p (a b) -> p a b", a=8), tp[k % 2][:].rearrange("p (a b) -> p a b", a=8),
                                    colv("sg_b", 0, 8).unsqueeze(2).to_broadcast([P, 8, 64]), ALU.add).then_inc(sem("sgu_read"), 1)

            def gate_u():
                for t in range(TT):
                    dve.wait_ge(sem("sgu_read"), t + 1)
                    v.tensor_tensor(u[:, t, :], u[:, t, :], vg[:, t, :], ALU.mult).then_inc(b_out, 1)

            head_gates(0, gate_positions)
            for lv in range(8):
                if lv in (0, 1, 7):
                    take_scores(0, lv)
                    if lv == 0:
                        gate_u()
                tick(W0["zi"] + lv)
                if lv not in (0, 1, 7):
                    take_scores(0, lv)
                if lv < 7:
                    query_updates(0, lv + 1)
            tick(W0["qb"])
            tick(W0["qb"] + 1)
            head_outputs(0)

            def turned_b():
                for t in range(TT):
                    k = JOB["tb"] + t
                    lo(k, bt[1][:, t, :], as_f32(bt[0][:, t, :]), tp[k % 2][:])

            head_gates(1, turned_b)
            for lv in range(8):
                if lv in (0, 7):
                    take_scores(1, lv)
                tick(W0["ga"] + lv)
                if lv not in (0, 7):
                    take_scores(1, lv)
                if lv < 7:
                    query_updates(1, lv + 1)

            def gated_b(t):
                ready(USE["wb"], t, W0["wb"] + 1, 1)
                wait_evac(dve, USE["gb"] + 1)
                v.tensor_tensor(two(gb[:, t, :]), two(gb[:, t, :]), pair[(USE["wb"] + t) % 2][:],
                                ALU.mult).then_inc(evac[(USE["wb"] + t) % 2], 1)

            def merge(t):
                ready(USE["wa"], t, W0["wa"] + 3, 2)
                p = (USE["wa"] + t) % 2
                v.tensor_tensor(two(ga[:, t, :]), two(ga[:, t, :]), pair[p][:], ALU.mult).then_inc(evac[p], 1)
                wait_evac(dve, USE["wa"] + t)
                v.tensor_tensor(ga[:, t, :], ga[:, t, :], gb[:, t, :], ALU.add).then_inc(merged, 1)

            gated_b(0)
            head_outputs(1)
            turned_tile("ta", gt, gt32, 0)
            tick(W0["wb"])
            gated_b(1)
            tick(W0["wb"] + 1)
            turned_tile("ta", gt, gt32, 1)
            merge(0)
            turned_tile("tm", ht, ht32, 0)
            tick(W0["wa"])
            tick(W0["wa"] + 1)
            tick(W0["wa"] + 2)
            merge(1)
            tick(W0["wa"] + 3)
            turned_tile("tm", ht, ht32, 1)
            dve.wait_ge(prow_in, 16)
            w = W0["wout"]
            for t in range(TT):
                dve.wait_ge(x_again[t], 16)
                post(RQ["mix"] + 2 * t, t, USE["wout"], prow[:, 0, :])
                norm(RQ["mix"] + 2 * t + 1, t, w + 2 if t else None)
                if t:
                    tick(w + 3)
                norm_jobs("norm1", t, colv("ffn_pre", 0, 8))
                if t == 0:
                    tick(w)
                    tick(w + 1)
            ffn("ffn0", "h0")
            w = W0["down0"]
            for c in range(GROUPS - 4):
                tick(w + c)
                if c == 0:
                    mod_columns(0, 24, 18)
                    mod_scale(0, 8, colv("mix_g", 0, 8))
                    gate_diagonals(16)
                    dve.wait_ge(pt_hi, 1)
                    v.tensor_tensor(pt[1][:], praw[:], as_f32(pt[0][:]), ALU.subtract).then_inc(pt_done, 1)
            post(RQ["ffn"], 0, USE["down0"], prow[:, 1, :])
            tick(w + GROUPS - 4)
            tick(w + GROUPS - 3)
            post(RQ["ffn"] + 1, 1, USE["down0"], prow[:, 1, :])
            turned_tile("tx", ht, ht32, 0)
            tick(w + GROUPS - 2)
            tick(w + GROUPS - 1)
            tick(W0["ple"])
            turned_tile("tx", ht, ht32, 1)
            dve.wait_ge(cs_hi, 1)
            v.tensor_tensor(cs[1][:], csr[:], as_f32(cs[0][:]), ALU.subtract).then_inc(cs_done, 1)
            w = W0["pleg"] + 3

            def dft_los(name, t, groups):
                for gr in groups:
                    k = JOB[name] + gr
                    lo(k, tt[1][:, t, gr, :], tt32[:, t, gr, :], tp[k % 2][:])

            for t in range(TT):
                wait_evac(dve, USE["pleg"] + t)
                link(v.tensor_tensor(xn[:, t, :], xn[:, t, :], gsig[:, t, :], ALU.mult))
                if t:
                    dft_los("dft1", 0, (0,))
                v.tensor_tensor(xres[:, t, :], xres[:, t, :], xn[:, t, :], ALU.add).then_inc(x_ready, 1)
                if t:
                    dft_los("dft1", 0, (1,))
                norm(RQ["norm2"] + t, t)
                if t:
                    dft_los("dft1", 0, (2, 3))
                norm_jobs("norm2", t, moda[:, 0, :], mod[:, 0:8])
                if t == 0:
                    tick(w - 3)
            dft_los("dft1b", 1, range(4))
            for gr in range(4):
                k = JOB["dft2"] + gr
                lo(k, ht[1][:, 2 * gr:2 * gr + 2, :], ht32[:, 2 * gr:2 * gr + 2, :], tp[k % 2][:].rearrange("p (a b) -> p a b", a=2))
                if gr != 2:
                    tick(w - 2 + (gr + 1) // 2)
            mod_columns(24, 40, 21)
            mod_scale(1, 32, colv("ffn_g", 0, 8))

            def boundary(w, use, halves, row, rows, q, name, scale, shift, columns=None):
                gated_post(0, use, w, halves, row, rows)
                norm(q, 0)
                if columns is not None:
                    columns()
                norm_jobs(name, 0, scale, shift)
                tick(w - 3)
                tick(w - 2)
                gated_post(1, use, w, halves, row, rows)
                norm(q + 1, 1, w - 1)
                tick(w)
                norm_jobs(name, 1, scale, shift)

            boundary(W0["fo"] + 3, USE["fo"], 7, grow[0][:], 2, RQ["norm3"], "norm3", moda[:, 1, :], mod[:, 24:32])
            ffn("ffn1", "h1")
            for w in range(W0["down1"], W0["down1"] + GROUPS - 4):
                tick(w)
                if w == W0["down1"]:
                    mod_columns(40, 48, 30)
                    gate_diagonals(40, JOB["rows0"] + 2)
            mod_columns(48, 64, 32)
            mod_scale(2, 56, colv("mix_g", 8, 8))
            boundary(W0["down1"] + GROUPS - 1, USE["down1"], 8, grow[1][:], 4, RQ["norm4"], "norm4", moda[:, 2, :], mod[:, 48:56])
            for c in range(4):
                tick(W0["rva"] + c)
            dve.wait_ge(rot_in, 16)
            for n, name in enumerate(("rq", "rk")):
                dst = qr if n == 0 else kr
                for m in range(2):
                    tick(W0[name] + 2 * m)
                    use = USE[name] + m
                    dve.wait_ge(w_used, W0[name] + 2 * m + 2)
                    src = pair[use % 2][:].rearrange("p a (x s) -> p (a x) s", x=2)
                    if n or m:
                        dve.wait_ge(rot_done, 2 * n + m)
                    v.tensor_tensor(rab[:, 0, :, :], src, rt[:, 0:1, :].to_broadcast([P, 4, S]), ALU.mult)
                    v.tensor_tensor(rab[:, 1, :, :], src, rt[:, 1:2, :].to_broadcast([P, 4, S]), ALU.mult).then_inc(evac[use % 2], 1)
                    wait_evac(dve, use)
                    c, d = [rab[:, y, :, :].rearrange("p (a x) s -> p a x s", x=2) for y in range(2)]
                    v.tensor_tensor(dst[:, 2 * m:2 * m + 2, 0, :], c[:, :, 0, :], d[:, :, 1, :], ALU.subtract)
                    v.tensor_tensor(dst[:, 2 * m:2 * m + 2, 1, :], d[:, :, 0, :], c[:, :, 1, :], ALU.add).then_inc(rot_done, 1)
                    tick(W0[name] + 2 * m + 1)
            mod_columns(64, 72, 37)
            gate_diagonals(64, None, dgb)
            dve.wait_ge(decay_in, 16)
            for c in range(4):
                for hd in ((), (0,), (1, 2), (3,))[c]:
                    k = JOB["sc"] + hd
                    dve.wait_ge(tp_done, k + 1)
                    v.tensor_tensor(ar[:, hd, :, :], tp[k % 2][:].rearrange("p (a b) -> p a b", a=2), dt[:, hd, :, :],
                                    ALU.mult).then_inc(sem("sc_read"), 1)
                tick(W0["rvb"] + c)

            def gated_head(hd):
                dve.wait_ge(sem("av_read"), 2 * hd + 2)
                wait_evac(dve, USE["rg"] + hd)
                for t in range(TT):
                    z = gg[:, t, hd * RV:(hd + 1) * RV]
                    ins = v.tensor_tensor(z, z, yr[t][:, hd * RV:(hd + 1) * RV], ALU.mult)
                ins.then_inc(y_done, 1)

            def head_los(hd):
                for t in range(TT):
                    turned(JOB["ty"] + 2 * hd + t, gt, gt32, hd, t)

            dve.wait_ge(sem("sc_read"), RH)
            for c in range(5):
                tick(W0["rg"] + c)
                if c < RH:
                    for t in range(TT):
                        k, q = JOB["av"] + 2 * c + t, RQ["av"] + 2 * c + t
                        dve.wait_ge(tp_done, k + 1)
                        link(v.bn_stats(bn[:, t, :], tp[k % 2][:]))
                        link(v.bn_aggr(mv[:, t, :], bn[:, t, :]))
                        v.tensor_scalar(st[:, q, 1, 0:1], mv[:, t, 1:2], EPS, None, ALU.add).then_inc(ms_done, 1)
                    for t in range(TT):
                        k, q = JOB["av"] + 2 * c + t, RQ["av"] + 2 * c + t
                        dve.wait_ge(rstd_done, q + 1)
                        v.tensor_scalar(yr[t][:, c * RV:(c + 1) * RV], tp[k % 2][:], mv[:, t, 0:1], st[:, q, 2, 0:1],
                                        ALU.subtract, ALU.mult).then_inc(sem("av_read"), 1)
            gated_head(0)
            gated_head(1)
            head_los(0)
            tick(W0["rg"] + 5)
            gated_head(2)
            head_los(1)
            tick(W0["rg"] + 6)
            gated_head(3)
            head_los(2)
            tick(W0["rg"] + 7)
            tick(W0["ro"])
            head_los(3)
            for w in range(W0["ro"] + 1, W0["ro"] + 4):
                tick(w)

            def last_columns():
                mod_columns(72, 88, 44)
                mod_scale(3, 80, colv("ffn_g", 8, 8))

            boundary(W0["ro"] + 7, USE["ro"], 9, grow[0][:], 6, RQ["norm5"], "norm5", moda[:, 3, :], mod[:, 72:80],
                     last_columns)
            ffn("ffn2", "h2")
            tick(W0["down2"])
            mod_columns(88, 96, 53)
            gate_diagonals(88)
            for w in range(W0["down2"] + 1, W0["down2"] + GROUPS - 1):
                tick(w)
            for t in range(TT):
                gated_post(t, USE["down2"], W0["down2"] + GROUPS - 1, 10, grow[1][:], 8)
                norm(RQ["norm6"] + t, t)
                if t == 0:
                    mod_columns(96, 112, NADA)
                    mod_scale(4, 104, colv("fin_g", 0, 8))
                scaled("norm6", t, moda[:, 4, :], mod[:, 96:104], lambda k, half: outb[:, k - JOB["norm6"], :])


def kernel(**inputs):
    import numpy as np
    import concourse.bacc as bacc
    from concourse.bass_utils import run_bass_kernel_spmd

    def get(name):
        return np.ascontiguousarray(inputs[name])

    def deep(w, n):
        k, cols = w.shape
        kt = 2048 // n
        a = w.reshape(k // (kt * P), kt, P, cols // n, n)
        return a.transpose(3, 0, 2, 1, 4).reshape(-1, P, 2048)

    def gate_up(wg, wu):
        m, out = 256 * WIDE, []
        for a, b, n in ((wg[:, :m], wu[:, :m], 256), (wg[:, m:], wu[:, m:], 128)):
            c = np.stack([a.reshape(D, -1, n), b.reshape(D, -1, n)], axis=2).reshape(D, -1)
            out.append(deep(c, 2 * n))
        return np.concatenate(out)

    def outer(w):
        return w.reshape(-1, 2, P, D).transpose(0, 2, 1, 3).reshape(-1, P, 2048)

    w_in = get("w_in")[0]
    z = {}
    off = 0
    for name, n in (("q", 1024), ("f", 1024), ("b", 1024), ("zi", 1024), ("zg", 1024), ("zu", 512), ("zv", 512),
                    ("ga", 1024), ("gb", 1024)):
        z[name] = w_in[:, off:off + n]
        off += n
    ri, fi, fo = get("w_ret_in_2")[0], get("w_ffn_in_2"), get("w_ffn_out_2")
    parts = {
        "zu": deep(z["zu"], 512), "zv": deep(z["zv"], 512),
        "zi": deep(z["zi"], 512), "zg": deep(z["zg"], 512), "ga": deep(z["ga"], 512), "gb": deep(z["gb"], 512),
        "wa": outer(get("w_a")[0]), "wb": outer(get("w_b")[0]), "wout": outer(get("w_out")[0]),
        "ffn0": gate_up(get("w_gate")[0], get("w_up")[0]), "down0": outer(get("w_down")[0]),
        "ple": outer(get("w_ple")[0]), "pleg": outer(get("w_ple_gate")[0]), "fo": outer(get("w_fourier_out_2")[0]),
        "ffn1": gate_up(fi[0][:, :FF], fi[0][:, FF:]), "down1": outer(fo[0]),
        "rq": deep(ri[:, 0:1024], 256), "rk": deep(ri[:, 1024:2048], 256),
        "rva": deep(ri[:, 2048:3072], 512), "rvb": deep(ri[:, 3072:4096], 512), "rg": deep(ri[:, 4096:6144], 512), "ro": outer(get("w_ret_out_2")[0]),
        "ffn2": gate_up(fi[1][:, :FF], fi[1][:, FF:]), "down2": outer(fo[1]),
    }
    for half, h in enumerate("ab"):
        for name in "qfb":
            parts[name + h] = deep(z[name][:, 512 * half:512 * half + 512], 256)
    weights = [c for name, n in STAGES for c in parts[name]]
    wada = get("w_ada_2")
    adas = [c for w in (wada[0], wada[1], get("w_ada_final_2")) for c in deep(w, 256)]
    stream = np.stack([(weights if kind == "w" else adas)[n] for kind, n in ORDER])

    def columns(a):
        return a.reshape(-1, P).T

    table = np.concatenate([columns(get(n).reshape(-1)) for n in (
        "norm_mix_pre", "norm_ffn_pre", "norm_mix_g_2", "norm_ffn_g_2", "final_norm_g_2", "c_2", "lb_gamma_fwd",
        "lb_gamma_bwd", "sg_b", "b_ada_2", "b_ada_final_2")], axis=1)
    rows = np.stack([np.concatenate([get("sg_ln_g")[0], get("sg_ln_b")[0]]), get("hg_norm")[0],
                     get("norm_mix_post")[0], get("norm_ffn_post")[0]])

    f32 = np.float32
    n = np.arange(P)
    masks = [n[:, None] == n[None, :]]
    for lv in range(7):
        h = 1 << lv
        masks.append((n[:, None] // (2 * h) == n[None, :] // (2 * h)) & (n[:, None] // h != n[None, :] // h))
    masks = np.stack(masks, axis=1).astype(np.float32)
    m = np.arange(S)
    ang = 2.0 * np.pi * ((m[:, None] * m[None, :]) % S) / S
    dft = np.concatenate([np.cos(ang), np.sin(ang), -np.sin(ang)], axis=1) / 16.0
    dft = dft.astype(f32).reshape(2, P, 768).transpose(1, 0, 2)
    freq = (f32(10000.0) ** (-np.arange(P, dtype=f32) / f32(P))).astype(f32)
    rang = (freq[:, None] * m[None, :].astype(f32)).astype(f32).astype(np.float64)
    rot = np.stack([np.cos(rang), np.sin(rang)], axis=1).astype(f32)
    lg = np.log1p(-np.exp2(-5.0 - np.arange(RH)))
    d = m[None, :] - m[:, None]
    decay = np.stack([np.where(d >= 0, np.exp(np.maximum(d, 0) * lg[h]), np.exp(np.maximum(-d, 0) * lg[RH - 1 - h]))
                      for h in range(RH)]) / 16.0
    decay = decay.astype(f32).reshape(RH, 2, P, S).transpose(2, 0, 1, 3)

    arrays = {
        "stream": stream,
        "x": get("x")[0].reshape(TT, P, D).transpose(1, 0, 2),
        "pT": get("p")[0, 0].T.reshape(2, P, S).transpose(1, 0, 2),
        "cols": table, "rows": rows,
        "sg_wT": get("sg_w")[0].transpose(2, 0, 1),
        "masks": masks, "ident": np.eye(P, dtype=f32), "dft": dft, "rot": rot, "decay": decay,
    }
    nc = bacc.Bacc("TRN2", target_bir_lowering=False, num_devices=1)
    args = []
    for name, a in arrays.items():
        arrays[name] = a = np.ascontiguousarray(a)
        args.append(nc.dram_tensor(name, a.shape, mybir.dt.from_np(a.dtype), kind="ExternalInput").ap())
    args.append(nc.dram_tensor("outT", (KT, P, S), F32, kind="ExternalOutput").ap())
    program(nc, *args)
    r = run_bass_kernel_spmd(nc, [arrays], core_ids=[0])
    return np.ascontiguousarray(r.results[0]["outT"].reshape(D, S).T).reshape(1, S, D)
```
